# Optimizing a Trainium2 kernel written in Bass

```python
import math
import jax
import jax.numpy as jnp
from jax import lax
import numpy as np

D_MODEL = 1024
BATCH = 1
SEQ = 256
DEPTH = 2

HEAD_DIM_ATTN = 64
N_HEADS_SB = 8
N_HEADS_DIL = 8
WIDTH_SB = N_HEADS_SB * HEAD_DIM_ATTN
WIDTH_DIL = N_HEADS_DIL * HEAD_DIM_ATTN
ATTN_WIDTH = WIDTH_SB + WIDTH_DIL
DIL_CONFIGS = ((128, 1), (512, 4), (2048, 16))
Q_BLOCK = 128
NUM_BUCKETS = 32
MAX_DISTANCE = 2048
N_HEADS_MLSTM = 8
HEAD_DIM_MLSTM = D_MODEL // N_HEADS_MLSTM
MLSTM_WIDTH = N_HEADS_MLSTM * HEAD_DIM_MLSTM
MLSTM_CHUNK = 128
CONV_WIDTH = 4
FORGET_BIAS_LO = 3.0
FORGET_BIAS_HI = 6.0
D_FF = 2816
N_EVEN = (DEPTH + 1) // 2
N_ODD = DEPTH // 2
EPS = 1e-6


def _rms_norm(x, g):
    xf = x.astype(jnp.float32)
    y = xf * lax.rsqrt(jnp.mean(xf * xf, axis=-1, keepdims=True) + EPS)
    return (y * g.astype(jnp.float32)).astype(x.dtype)

def _swiglu(x, w_gate, w_up, w_down):
    return (jax.nn.silu(x @ w_gate) * (x @ w_up)) @ w_down

def _t5_bucket(dist):
    max_exact = NUM_BUCKETS // 2
    d = jnp.maximum(dist, 1).astype(jnp.float32)
    log_b = max_exact + (jnp.log(d / max_exact) / math.log(MAX_DISTANCE / max_exact)
                         * (NUM_BUCKETS - max_exact)).astype(jnp.int32)
    log_b = jnp.minimum(log_b, NUM_BUCKETS - 1)
    return jnp.where(dist < max_exact, dist, log_b)

def _stick_breaking_attention(q, k, v):
    bsz, t, h, dh = q.shape
    nb = t // Q_BLOCK
    qb = q.reshape(bsz, nb, Q_BLOCK, h, dh).transpose(1, 0, 2, 3, 4)
    starts = jnp.arange(nb) * Q_BLOCK
    k_pos = jnp.arange(t)
    scale = 1.0 / math.sqrt(dh)

    def block(args):
        q_blk, start = args
        z = jnp.einsum('bqhd,bkhd->bhqk', q_blk, k) * scale
        causal = k_pos[None, :] < (start + jnp.arange(Q_BLOCK))[:, None]
        log_keep = jnp.where(causal, jax.nn.log_sigmoid(-z), 0.0)
        later = lax.cumsum(log_keep, axis=3, reverse=True) - log_keep
        log_w = jnp.where(causal, jax.nn.log_sigmoid(z) + later, -jnp.inf)
        return jnp.einsum('bhqk,bkhd->bqhd', jnp.exp(log_w), v)

    out = lax.map(block, (qb, starts))
    return out.transpose(1, 0, 2, 3, 4).reshape(bsz, t, h, dh)

def _dilated_branch(q, k, v, rel_bias, window, dil):
    bsz, t, h, dh = q.shape
    steps = window // dil
    seq_l = t // dil
    nb = -(-seq_l // Q_BLOCK)
    lp = nb * Q_BLOCK
    n = bsz * dil

    def to_res(a):
        return a.reshape(bsz, seq_l, dil, h, dh).transpose(0, 2, 1, 3, 4).reshape(n, seq_l, h, dh)

    qb = jnp.pad(to_res(q), ((0, 0), (0, lp - seq_l), (0, 0), (0, 0))).reshape(n, nb, Q_BLOCK, h, dh)

    def band(a):
        a = jnp.pad(to_res(a), ((0, 0), (Q_BLOCK, lp - seq_l), (0, 0), (0, 0)))
        a = a.reshape(n, nb + 1, Q_BLOCK, h, dh)
        return jnp.concatenate([a[:, :-1], a[:, 1:]], axis=2)

    kb, vb = band(k), band(v)
    qi = jnp.arange(Q_BLOCK)[:, None]
    ki = jnp.arange(2 * Q_BLOCK)[None, :]
    dist = qi + Q_BLOCK - ki
    bias = rel_bias[_t5_bucket(jnp.maximum(dist, 0) * dil)].transpose(2, 0, 1)
    key_pos = jnp.arange(nb)[:, None, None] * Q_BLOCK + ki[None] - Q_BLOCK
    valid = (dist >= 0) & (dist <= steps) & (key_pos >= 0)
    s = jnp.einsum('nbqhd,nbkhd->nbhqk', qb, kb) / math.sqrt(dh) + bias
    s = jnp.where(valid[None, :, None], s, -jnp.inf)
    m = jnp.max(s, axis=-1)
    p = jnp.exp(s - m[..., None])
    l = jnp.sum(p, axis=-1)
    num = jnp.einsum('nbhqk,nbkhd->nbqhd', p, vb)

    def back(a):
        a = a[:, :seq_l]
        rest = a.shape[2:]
        a = a.reshape((bsz, dil, seq_l) + rest)
        a = a.transpose((0, 2, 1) + tuple(range(3, a.ndim)))
        return a.reshape((bsz, t) + rest)

    num = back(num.reshape(n, lp, h, dh))
    m = back(m.transpose(0, 1, 3, 2).reshape(n, lp, h))
    l = back(l.transpose(0, 1, 3, 2).reshape(n, lp, h))
    return num, m, l

def _dilated_attention(q, k, v, rel_bias):
    outs = [_dilated_branch(q, k, v, rel_bias, w, d) for (w, d) in DIL_CONFIGS]
    m_all = jnp.stack([o[1] for o in outs])
    wts = jnp.exp(m_all - jnp.max(m_all, axis=0))
    num = sum(wts[i][..., None] * outs[i][0] for i in range(len(outs)))
    den = sum(wts[i] * outs[i][2] for i in range(len(outs)))
    return num / den[..., None]

def _attn_mixer(xn, w_in, w_out, rel_bias):
    bsz, t, _ = xn.shape
    proj = (xn @ w_in).astype(jnp.float32)
    idx = [WIDTH_SB, 2 * WIDTH_SB, 3 * WIDTH_SB, 3 * WIDTH_SB + WIDTH_DIL, 3 * WIDTH_SB + 2 * WIDTH_DIL]
    qa, ka, va, qd, kd, vd = jnp.split(proj, idx, axis=-1)
    sb = lambda a: a.reshape(bsz, t, N_HEADS_SB, HEAD_DIM_ATTN)
    dl = lambda a: a.reshape(bsz, t, N_HEADS_DIL, HEAD_DIM_ATTN)
    out_sb = _stick_breaking_attention(sb(qa), sb(ka), sb(va))
    out_dil = _dilated_attention(dl(qd), dl(kd), dl(vd), rel_bias.astype(jnp.float32))
    mixed = jnp.concatenate([out_sb.reshape(bsz, t, WIDTH_SB), out_dil.reshape(bsz, t, WIDTH_DIL)], axis=-1)
    return mixed.astype(xn.dtype) @ w_out

def _causal_depthwise_conv(x, w):
    return lax.conv_general_dilated(
        x, w[:, None, :], window_strides=(1,), padding=((CONV_WIDTH - 1, 0),),
        dimension_numbers=('NWC', 'WIO', 'NWC'), feature_group_count=x.shape[-1])

def _mlstm(q, k, v, i_pre, f_pre):
    bsz, t, h, dh = q.shape
    nc = t // MLSTM_CHUNK
    cl = MLSTM_CHUNK

    def chunks(a):
        a = a.reshape((bsz, nc, cl, h) + a.shape[3:])
        return a.transpose((0, 3, 1, 2) + tuple(range(4, a.ndim)))

    qc = chunks(q) / math.sqrt(dh)
    kc, vc = chunks(k), chunks(v)
    ic = chunks(i_pre)
    bc = jnp.cumsum(jax.nn.log_sigmoid(chunks(f_pre)), axis=-1)

    def step(carry, xs):
        c_st, n_st, m_st = carry
        k_, v_, i_, b_ = xs
        g = b_[..., -1]
        w = g[..., None] - b_ + i_
        m_new = jnp.maximum(g + m_st, jnp.max(w, axis=-1))
        decay = jnp.exp(g + m_st - m_new)
        ws = jnp.exp(w - m_new[..., None])
        c_new = decay[..., None, None] * c_st + jnp.einsum('bhs,bhsk,bhsv->bhkv', ws, k_, v_)
        n_new = decay[..., None] * n_st + jnp.einsum('bhs,bhsk->bhk', ws, k_)
        return (c_new, n_new, m_new), (c_st, n_st, m_st)

    init = (jnp.zeros((bsz, h, dh, dh), jnp.float32),
            jnp.zeros((bsz, h, dh), jnp.float32),
            jnp.zeros((bsz, h), jnp.float32))
    xs = tuple(jnp.moveaxis(a, 2, 0) for a in (kc, vc, ic, bc))
    _, (c_prev, n_prev, m_prev) = lax.scan(step, init, xs)
    c_prev = jnp.moveaxis(c_prev, 0, 2)
    n_prev = jnp.moveaxis(n_prev, 0, 2)
    m_prev = jnp.moveaxis(m_prev, 0, 2)

    a = bc + m_prev[..., None]
    tri = jnp.arange(cl)[:, None] >= jnp.arange(cl)[None, :]
    dmat = jnp.where(tri, bc[..., :, None] - bc[..., None, :] + ic[..., None, :], -jnp.inf)
    m_t = jnp.maximum(a, jnp.max(dmat, axis=-1))
    p = jnp.einsum('bhcld,bhcsd->bhcls', qc, kc) * jnp.exp(dmat - m_t[..., None])
    w_inter = jnp.exp(a - m_t)
    h_num = (jnp.einsum('bhcls,bhcsd->bhcld', p, vc)
             + w_inter[..., None] * jnp.einsum('bhcld,bhcde->bhcle', qc, c_prev))
    n_num = jnp.sum(p, axis=-1) + w_inter * jnp.einsum('bhcld,bhcd->bhcl', qc, n_prev)
    hid = h_num / jnp.maximum(jnp.abs(n_num), jnp.exp(-m_t))[..., None]
    return hid.transpose(0, 2, 3, 1, 4).reshape(bsz, t, h, dh)

def _mlstm_mixer(xn, w_in, b_gates, conv_w, head_g, w_out):
    bsz, t, _ = xn.shape
    proj = (xn @ w_in).astype(jnp.float32)
    qk, v, o, gates = jnp.split(proj, [2 * MLSTM_WIDTH, 3 * MLSTM_WIDTH, 4 * MLSTM_WIDTH], axis=-1)
    qk = jax.nn.silu(_causal_depthwise_conv(qk, conv_w.astype(jnp.float32)))
    q, k = jnp.split(qk, 2, axis=-1)
    gates = gates + b_gates.astype(jnp.float32)
    i_pre, f_pre = gates[..., :N_HEADS_MLSTM], gates[..., N_HEADS_MLSTM:]
    hd = lambda a: a.reshape(bsz, t, N_HEADS_MLSTM, HEAD_DIM_MLSTM)
    hid = _mlstm(hd(q), hd(k), hd(v), i_pre, f_pre)
    hid = hid * lax.rsqrt(jnp.mean(hid * hid, axis=-1, keepdims=True) + EPS)
    hid = hid * head_g.astype(jnp.float32).reshape(N_HEADS_MLSTM, HEAD_DIM_MLSTM)
    hid = hid.reshape(bsz, t, MLSTM_WIDTH) * jax.nn.sigmoid(o)
    return hid.astype(xn.dtype) @ w_out

def first_inputs(seed: int = 0) -> dict:
    key = jax.random.key(seed)
    ks = jax.random.split(key, 16)
    nrm = jax.random.normal
    x = nrm(ks[0], (BATCH, SEQ, D_MODEL), jnp.float32)
    norm_g = 1.0 + 0.02 * nrm(ks[1], (DEPTH, 6, D_MODEL), jnp.float32)
    ffn_w_gate = nrm(ks[2], (DEPTH, 2, D_MODEL, D_FF), jnp.float32) * D_MODEL ** -0.5
    ffn_w_up = nrm(ks[3], (DEPTH, 2, D_MODEL, D_FF), jnp.float32) * D_MODEL ** -0.5
    ffn_w_down = nrm(ks[4], (DEPTH, 2, D_FF, D_MODEL), jnp.float32) * D_FF ** -0.5
    attn_w_in = nrm(ks[5], (N_EVEN, D_MODEL, 3 * ATTN_WIDTH), jnp.float32) * D_MODEL ** -0.5
    attn_w_out = nrm(ks[6], (N_EVEN, ATTN_WIDTH, D_MODEL), jnp.float32) * ATTN_WIDTH ** -0.5
    rel_bias = 0.5 * nrm(ks[7], (NUM_BUCKETS, N_HEADS_DIL), jnp.float32)
    mlstm_w_in = nrm(ks[8], (N_ODD, D_MODEL, 4 * MLSTM_WIDTH + 2 * N_HEADS_MLSTM), jnp.float32) * D_MODEL ** -0.5
    b_i = 0.1 * nrm(ks[9], (N_ODD, N_HEADS_MLSTM), jnp.float32)
    b_f = (jnp.linspace(FORGET_BIAS_LO, FORGET_BIAS_HI, N_HEADS_MLSTM, dtype=jnp.float32)[None]
           + 0.1 * nrm(ks[10], (N_ODD, N_HEADS_MLSTM), jnp.float32))
    mlstm_b_gates = jnp.concatenate([b_i, b_f], axis=-1)
    mlstm_conv_w = nrm(ks[11], (N_ODD, CONV_WIDTH, 2 * MLSTM_WIDTH), jnp.float32) * CONV_WIDTH ** -0.5
    mlstm_head_g = 1.0 + 0.02 * nrm(ks[12], (N_ODD, MLSTM_WIDTH), jnp.float32)
    mlstm_w_out = nrm(ks[13], (N_ODD, MLSTM_WIDTH, D_MODEL), jnp.float32) * MLSTM_WIDTH ** -0.5
    return {'x': x, 'norm_g': norm_g, 'ffn_w_gate': ffn_w_gate, 'ffn_w_up': ffn_w_up,
            'ffn_w_down': ffn_w_down, 'attn_w_in': attn_w_in, 'attn_w_out': attn_w_out,
            'rel_bias': rel_bias, 'mlstm_w_in': mlstm_w_in, 'mlstm_b_gates': mlstm_b_gates,
            'mlstm_conv_w': mlstm_conv_w, 'mlstm_head_g': mlstm_head_g, 'mlstm_w_out': mlstm_w_out}

def first_block(x, norm_g, ffn_w_gate, ffn_w_up, ffn_w_down, attn_w_in, attn_w_out, rel_bias,
              mlstm_w_in, mlstm_b_gates, mlstm_conv_w, mlstm_head_g, mlstm_w_out):
    for layer in range(DEPTH):
        g = norm_g[layer]
        j = layer // 2
        hf = _swiglu(_rms_norm(x, g[0]), ffn_w_gate[layer, 0], ffn_w_up[layer, 0], ffn_w_down[layer, 0])
        x = x + 0.5 * _rms_norm(hf, g[1])
        xn = _rms_norm(x, g[2])
        if layer % 2 == 0:
            mix = _attn_mixer(xn, attn_w_in[j], attn_w_out[j], rel_bias)
        else:
            mix = _mlstm_mixer(xn, mlstm_w_in[j], mlstm_b_gates[j], mlstm_conv_w[j],
                               mlstm_head_g[j], mlstm_w_out[j])
        x = x + _rms_norm(mix, g[3])
        hf = _swiglu(_rms_norm(x, g[4]), ffn_w_gate[layer, 1], ffn_w_up[layer, 1], ffn_w_down[layer, 1])
        x = x + 0.5 * _rms_norm(hf, g[5])
    return x


N_EVEN_2 = (DEPTH + 1) // 2
N_ODD_2 = DEPTH // 2

HEAD_DIM = 64
NEG = -1e30
BIG = 1e30
NORM_EPS = 1e-6

N_BUCKETS = 32
MAX_DISTANCE_2 = 1024
N_BIAS_HEADS = 8

NSA_HEADS = 8
NSA_KV_HEADS = 2
NSA_GROUP = NSA_HEADS // NSA_KV_HEADS
CMP_LEN = 32
CMP_STRIDE = 16
CMP_HIDDEN = 256
SLC_BLOCK = 64
SLC_TOPN = 16
NSA_WINDOW = 512
NSA_QBLOCK = 128

MOBA_HEADS = 8
MOBA_BLOCK = 256
MOBA_TOPK = 3
MOBA_QBLOCK = 32

MLA_HEADS = 4
MLA_Q_RANK = 256
MLA_KV_RANK = 128
MLA_NOPE = 128
MLA_ROPE = 64
MLA_V = 128
ROPE_THETA = 10000.0
DENSE_QBLOCK = 128

SWA_HEADS = 8
SWA_KV_HEADS = 2
SWA_GROUP = SWA_HEADS // SWA_KV_HEADS
SWA_WINDOW = 128
SWA_QBLOCK = 128

N_EXPERTS = 16
N_GROUPS = 4
EXPERTS_PER_GROUP = N_EXPERTS // N_GROUPS
TOP_K = 2
D_EXPERT = 512
MOE_BLOCK = 256

ADA_INIT = 0.5

EVEN_WIDTHS = (NSA_HEADS * HEAD_DIM,) + (NSA_KV_HEADS * HEAD_DIM,) * 6 + (3 * NSA_HEADS,) + (MOBA_HEADS * HEAD_DIM,) * 3
EVEN_IN = sum(EVEN_WIDTHS)
EVEN_OUT = NSA_HEADS * HEAD_DIM + MOBA_HEADS * HEAD_DIM
ODD_WIDTHS = (MLA_Q_RANK, MLA_KV_RANK, MLA_ROPE, SWA_HEADS * HEAD_DIM, SWA_KV_HEADS * HEAD_DIM, SWA_KV_HEADS * HEAD_DIM)
ODD_IN = sum(ODD_WIDTHS)
ODD_OUT = MLA_HEADS * MLA_V + SWA_HEADS * HEAD_DIM


def rmsnorm(x, g):
    xf = x.astype(jnp.float32)
    y = xf * lax.rsqrt(jnp.mean(xf * xf, axis=-1, keepdims=True) + NORM_EPS)
    return (y * g.astype(jnp.float32)).astype(x.dtype)

def split_cols(x, widths):
    idx, acc = [], 0
    for w in widths[:-1]:
        acc += w
        idx.append(acc)
    return jnp.split(x, idx, axis=-1)

def masked_softmax(s, mask):
    s = jnp.where(mask, s.astype(jnp.float32), NEG)
    p = jax.nn.softmax(s, axis=-1)
    return jnp.where(mask, p, 0.0)

def rel_bucket(dist):
    exact = N_BUCKETS // 2
    d = jnp.maximum(dist, 0)
    log_part = exact + (jnp.log(jnp.maximum(d, 1).astype(jnp.float32) / exact)
                        / math.log(MAX_DISTANCE_2 / exact) * (N_BUCKETS - exact)).astype(jnp.int32)
    return jnp.where(d < exact, d, jnp.minimum(log_part, N_BUCKETS - 1))

def shared_bias(rel_table, dist, n_kv):
    b = jnp.moveaxis(rel_table[rel_bucket(dist)], -1, 0).astype(jnp.float32)
    return b.reshape(n_kv, -1, *dist.shape)

def gathered_bias(rel_table, dist, n_kv):
    table = rel_table.reshape(N_BUCKETS, n_kv, -1)
    kv = jnp.arange(n_kv)[None, :, None, None]
    return jnp.moveaxis(table[rel_bucket(dist), kv], -1, 2).astype(jnp.float32)

def rope_tables(S, dim):
    inv = ROPE_THETA ** (-jnp.arange(0, dim, 2, dtype=jnp.float32) / dim)
    ang = jnp.arange(S, dtype=jnp.float32)[:, None] * inv[None, :]
    return jnp.cos(ang), jnp.sin(ang)

def apply_rope(x, cos, sin):
    half = x.shape[-1] // 2
    x1 = x[..., :half].astype(jnp.float32)
    x2 = x[..., half:].astype(jnp.float32)
    return jnp.concatenate([x1 * cos - x2 * sin, x1 * sin + x2 * cos], axis=-1).astype(x.dtype)

def adaln(c, w, b):
    m = jax.nn.silu(c) @ w + b
    return jnp.split(m[:, None, :], 6, axis=-1)

def nsa_attention(q, kc, vc, ks, vs, kw, vw, gates, pos_k, pos_v, ck_w1, ck_w2, cv_w1, cv_w2, rel_table):
    B, S, _ = q.shape
    Hk, G, dh, QB = NSA_KV_HEADS, NSA_GROUP, HEAD_DIM, NSA_QBLOCK
    scale = dh ** -0.5
    q = q.reshape(B, S, Hk, G, dh).transpose(0, 2, 3, 1, 4)
    to_kv = lambda t: t.reshape(B, S, Hk, dh).transpose(0, 2, 1, 3)
    kc, vc, ks, vs, kw, vw = (to_kv(t) for t in (kc, vc, ks, vs, kw, vw))
    g = jax.nn.sigmoid(gates.astype(jnp.float32)).reshape(B, S, Hk, G, 3).transpose(0, 2, 3, 1, 4)

    n_cmp = (S - CMP_LEN) // CMP_STRIDE + 1
    cmp_start = np.arange(n_cmp, dtype=np.int32) * CMP_STRIDE
    win_idx = cmp_start[:, None] + np.arange(CMP_LEN, dtype=np.int32)[None, :]
    cmp_end = cmp_start + CMP_LEN - 1

    def compress(t, pos, w1, w2):
        blocks = t[:, :, win_idx, :] + pos
        flat = blocks.reshape(B, Hk, n_cmp, CMP_LEN * dh)
        return jax.nn.gelu(flat @ w1) @ w2

    k_cmp = compress(kc, pos_k, ck_w1, ck_w2)
    v_cmp = compress(vc, pos_v, cv_w1, cv_w2)

    n_slc = S // SLC_BLOCK
    slc_lo = np.arange(n_slc, dtype=np.int32) * SLC_BLOCK
    overlap = ((cmp_start[:, None] <= slc_lo[None, :] + SLC_BLOCK - 1)
               & (cmp_end[:, None] >= slc_lo[None, :])).astype(np.float32)
    n_sel = min(SLC_TOPN, n_slc)
    ks_blocks = ks.reshape(B, Hk, n_slc, SLC_BLOCK, dh)
    vs_blocks = vs.reshape(B, Hk, n_slc, SLC_BLOCK, dh)

    pad = ((0, 0), (0, 0), (NSA_WINDOW, 0), (0, 0))
    kw_pad, vw_pad = jnp.pad(kw, pad), jnp.pad(vw, pad)

    nq = S // QB
    q_blocks = jnp.moveaxis(q.reshape(B, Hk, G, nq, QB, dh), 3, 0)
    g_blocks = jnp.moveaxis(g.reshape(B, Hk, G, nq, QB, 3), 3, 0)
    b_idx = jnp.arange(B)[:, None, None, None]
    kv_idx = jnp.arange(Hk)[None, :, None, None]

    def block(args):
        qb, gb, i = args
        start = i * QB
        t = start + jnp.arange(QB)
        s_c = jnp.einsum('bkgqd,bknd->bkgqn', qb, k_cmp).astype(jnp.float32) * scale \
            + shared_bias(rel_table, t[:, None] - cmp_end[None, :], Hk)
        p_c = masked_softmax(s_c, cmp_end[None, :] <= t[:, None])
        o_c = jnp.einsum('bkgqn,bknd->bkgqd', p_c.astype(v_cmp.dtype), v_cmp)
        imp = jnp.einsum('bkgqn,nm->bkqm', p_c, overlap)
        blk_t = (t // SLC_BLOCK)[:, None]
        j = jnp.arange(n_slc)[None, :]
        forced = (j == 0) | (j == blk_t) | (j == blk_t - 1)
        score = jnp.where(forced, BIG, jnp.where(j <= blk_t, imp, NEG))
        sel = lax.top_k(score, n_sel)[1]
        k_sel = ks_blocks[b_idx, kv_idx, sel].reshape(B, Hk, QB, n_sel * SLC_BLOCK, dh)
        v_sel = vs_blocks[b_idx, kv_idx, sel].reshape(B, Hk, QB, n_sel * SLC_BLOCK, dh)
        pos_sel = (sel[..., None] * SLC_BLOCK + jnp.arange(SLC_BLOCK)).reshape(B, Hk, QB, -1)
        dist_s = t[:, None] - pos_sel
        s_s = jnp.einsum('bkgqd,bkqsd->bkgqs', qb, k_sel).astype(jnp.float32) * scale \
            + gathered_bias(rel_table, dist_s, Hk)
        p_s = masked_softmax(s_s, (dist_s >= 0)[:, :, None])
        o_s = jnp.einsum('bkgqs,bkqsd->bkgqd', p_s.astype(v_sel.dtype), v_sel)
        k_w = lax.dynamic_slice_in_dim(kw_pad, start, QB + NSA_WINDOW, axis=2)
        v_w = lax.dynamic_slice_in_dim(vw_pad, start, QB + NSA_WINDOW, axis=2)
        dist_w = t[:, None] - (start - NSA_WINDOW + jnp.arange(QB + NSA_WINDOW))[None, :]
        s_w = jnp.einsum('bkgqd,bksd->bkgqs', qb, k_w).astype(jnp.float32) * scale \
            + shared_bias(rel_table, dist_w, Hk)
        p_w = masked_softmax(s_w, (dist_w >= 0) & (dist_w < NSA_WINDOW))
        o_w = jnp.einsum('bkgqs,bksd->bkgqd', p_w.astype(v_w.dtype), v_w)
        return (gb[..., 0:1] * o_c + gb[..., 1:2] * o_s + gb[..., 2:3] * o_w).astype(qb.dtype)

    o = lax.map(block, (q_blocks, g_blocks, jnp.arange(nq)))
    return o.transpose(1, 0, 4, 2, 3, 5).reshape(B, S, NSA_HEADS * dh)

def moba_attention(q, k, v, rel_table):
    B, S, _ = q.shape
    H, dh, QB = MOBA_HEADS, HEAD_DIM, MOBA_QBLOCK
    scale = dh ** -0.5
    q, k, v = (t.reshape(B, S, H, dh).transpose(0, 2, 1, 3) for t in (q, k, v))
    n_blk = -(-S // MOBA_BLOCK)
    pad = ((0, 0), (0, 0), (0, n_blk * MOBA_BLOCK - S), (0, 0))
    k_pad, v_pad = jnp.pad(k, pad), jnp.pad(v, pad)
    k_blocks = k_pad.reshape(B, H, n_blk, MOBA_BLOCK, dh)
    v_blocks = v_pad.reshape(B, H, n_blk, MOBA_BLOCK, dh)
    k_mean = jnp.mean(k_blocks.astype(jnp.float32), axis=3)
    n_top = min(MOBA_TOPK, n_blk)
    n_s = n_top * MOBA_BLOCK
    nq = S // QB
    q_blocks = jnp.moveaxis(q.reshape(B, H, nq, QB, dh), 2, 0)
    b_idx = jnp.arange(B)[:, None, None, None]
    h_idx = jnp.arange(H)[None, :, None, None]

    def block(args):
        qb, i = args
        start = i * QB
        t = start + jnp.arange(QB)
        own = start // MOBA_BLOCK
        gate = jnp.einsum('bhqd,bhnd->bhqn', qb.astype(jnp.float32), k_mean)
        gate = jnp.where(jnp.arange(n_blk) < own, gate, NEG)
        sel = lax.top_k(gate, n_top)[1]
        k_sel = k_blocks[b_idx, h_idx, sel].reshape(B, H, QB, n_s, dh)
        v_sel = v_blocks[b_idx, h_idx, sel].reshape(B, H, QB, n_s, dh)
        pos_sel = (sel[..., None] * MOBA_BLOCK + jnp.arange(MOBA_BLOCK)).reshape(B, H, QB, n_s)
        mask_sel = pos_sel < own * MOBA_BLOCK
        k_own = lax.dynamic_slice_in_dim(k_pad, own * MOBA_BLOCK, MOBA_BLOCK, axis=2)
        v_own = lax.dynamic_slice_in_dim(v_pad, own * MOBA_BLOCK, MOBA_BLOCK, axis=2)
        dist_own = t[:, None] - (own * MOBA_BLOCK + jnp.arange(MOBA_BLOCK))[None, :]
        s_sel = jnp.einsum('bhqd,bhqsd->bhqs', qb, k_sel).astype(jnp.float32) * scale \
            + gathered_bias(rel_table, t[:, None] - pos_sel, H)[:, :, 0]
        s_own = jnp.einsum('bhqd,bhsd->bhqs', qb, k_own).astype(jnp.float32) * scale \
            + shared_bias(rel_table, dist_own, H)[:, 0]
        s = jnp.concatenate([s_sel, s_own], axis=-1)
        mask = jnp.concatenate([mask_sel, jnp.broadcast_to(dist_own >= 0, s_own.shape)], axis=-1)
        p = masked_softmax(s, mask).astype(v.dtype)
        return jnp.einsum('bhqs,bhqsd->bhqd', p[..., :n_s], v_sel) \
            + jnp.einsum('bhqs,bhsd->bhqd', p[..., n_s:], v_own)

    o = lax.map(block, (q_blocks, jnp.arange(nq)))
    return o.transpose(1, 0, 3, 2, 4).reshape(B, S, H * dh)

def mla_attention(c_q, c_kv, k_rope, q_norm, kv_norm, w_q_up, w_kv_up):
    B, S, _ = c_q.shape
    H, QB = MLA_HEADS, DENSE_QBLOCK
    q = (rmsnorm(c_q, q_norm) @ w_q_up).reshape(B, S, H, MLA_NOPE + MLA_ROPE)
    kv = (rmsnorm(c_kv, kv_norm) @ w_kv_up).reshape(B, S, H, MLA_NOPE + MLA_V)
    cos, sin = rope_tables(S, MLA_ROPE)
    q_nope = q[..., :MLA_NOPE]
    q_rope = apply_rope(q[..., MLA_NOPE:], cos[:, None, :], sin[:, None, :])
    k_rope = apply_rope(k_rope, cos, sin)
    k_nope = kv[..., :MLA_NOPE].transpose(0, 2, 1, 3)
    v = kv[..., MLA_NOPE:].transpose(0, 2, 1, 3)
    scale = (MLA_NOPE + MLA_ROPE) ** -0.5
    nq = S // QB
    qn_b = q_nope.reshape(B, nq, QB, H, MLA_NOPE).transpose(1, 0, 3, 2, 4)
    qr_b = q_rope.reshape(B, nq, QB, H, MLA_ROPE).transpose(1, 0, 3, 2, 4)
    kpos = jnp.arange(S)

    def block(args):
        qn, qr, i = args
        t = i * QB + jnp.arange(QB)
        s = (jnp.einsum('bhqd,bhkd->bhqk', qn, k_nope)
             + jnp.einsum('bhqd,bkd->bhqk', qr, k_rope)).astype(jnp.float32) * scale
        s = jnp.where(kpos[None, :] <= t[:, None], s, NEG)
        p = jax.nn.softmax(s, axis=-1).astype(v.dtype)
        return jnp.einsum('bhqk,bhkd->bhqd', p, v)

    o = lax.map(block, (qn_b, qr_b, jnp.arange(nq)))
    return o.transpose(1, 0, 3, 2, 4).reshape(B, S, H * MLA_V)

def swa_sink_attention(q, k, v, sinks, rel_table):
    B, S, _ = q.shape
    Hk, G, dh, QB, W = SWA_KV_HEADS, SWA_GROUP, HEAD_DIM, SWA_QBLOCK, SWA_WINDOW
    scale = dh ** -0.5
    q = q.reshape(B, S, Hk, G, dh).transpose(0, 2, 3, 1, 4)
    k = k.reshape(B, S, Hk, dh).transpose(0, 2, 1, 3)
    v = v.reshape(B, S, Hk, dh).transpose(0, 2, 1, 3)
    pad = ((0, 0), (0, 0), (W, 0), (0, 0))
    k_pad, v_pad = jnp.pad(k, pad), jnp.pad(v, pad)
    nq = S // QB
    q_blocks = jnp.moveaxis(q.reshape(B, Hk, G, nq, QB, dh), 3, 0)
    sink = sinks.astype(jnp.float32).reshape(Hk, G, 1, 1)

    def block(args):
        qb, i = args
        start = i * QB
        t = start + jnp.arange(QB)
        k_w = lax.dynamic_slice_in_dim(k_pad, start, QB + W, axis=2)
        v_w = lax.dynamic_slice_in_dim(v_pad, start, QB + W, axis=2)
        dist = t[:, None] - (start - W + jnp.arange(QB + W))[None, :]
        mask = (dist >= 0) & (dist < W)
        s = jnp.einsum('bkgqd,bksd->bkgqs', qb, k_w).astype(jnp.float32) * scale \
            + shared_bias(rel_table, dist, Hk)
        s = jnp.where(mask, s, NEG)
        m = jnp.maximum(jnp.max(s, axis=-1, keepdims=True), sink)
        e = jnp.exp(s - m)
        p = e / (jnp.sum(e, axis=-1, keepdims=True) + jnp.exp(sink - m))
        return jnp.einsum('bkgqs,bksd->bkgqd', p.astype(v_w.dtype), v_w)

    o = lax.map(block, (q_blocks, jnp.arange(nq)))
    return o.transpose(1, 0, 4, 2, 3, 5).reshape(B, S, SWA_HEADS * dh)

def even_mixer(h, w_in, w_out, pos_k, pos_v, ck_w1, ck_w2, cv_w1, cv_w2, rel_table):
    q_a, kc, vc, ks, vs, kw, vw, gates, q_b, k_b, v_b = split_cols(h @ w_in, EVEN_WIDTHS)
    o_a = nsa_attention(q_a, kc, vc, ks, vs, kw, vw, gates, pos_k, pos_v, ck_w1, ck_w2, cv_w1, cv_w2, rel_table)
    o_b = moba_attention(q_b, k_b, v_b, rel_table)
    return jnp.concatenate([o_a, o_b.astype(o_a.dtype)], axis=-1) @ w_out

def odd_mixer(h, w_in, w_out, q_norm, kv_norm, w_q_up, w_kv_up, sinks, rel_table):
    c_q, c_kv, k_rope, q_d, k_d, v_d = split_cols(h @ w_in, ODD_WIDTHS)
    o_c = mla_attention(c_q, c_kv, k_rope, q_norm, kv_norm, w_q_up, w_kv_up)
    o_d = swa_sink_attention(q_d, k_d, v_d, sinks, rel_table)
    return jnp.concatenate([o_c, o_d.astype(o_c.dtype)], axis=-1) @ w_out

def grouped_moe(h, router_w, router_b, w_gate, w_up, w_down):
    B, S, D = h.shape
    T = B * S
    E = N_EXPERTS
    xf = h.reshape(T, D)
    aff = jax.nn.sigmoid((xf @ router_w).astype(jnp.float32))
    biased = (aff + router_b.astype(jnp.float32)).reshape(T, N_GROUPS, EXPERTS_PER_GROUP)
    grp_score = jnp.sum(lax.top_k(biased, TOP_K)[0], axis=-1)
    g_sel = jnp.argmax(grp_score, axis=-1)
    tok = jnp.arange(T)
    local = lax.top_k(biased[tok, g_sel], TOP_K)[1]
    expert = g_sel[:, None] * EXPERTS_PER_GROUP + local
    w = aff[tok[:, None], expert]
    w = w / jnp.sum(w, axis=-1, keepdims=True)

    A = T * TOP_K
    flat_e = expert.reshape(A)
    flat_tok = jnp.repeat(tok, TOP_K)
    flat_w = w.reshape(A)
    order = jnp.argsort(flat_e)
    se, stok, sw = flat_e[order], flat_tok[order], flat_w[order]
    counts = jnp.zeros((E,), jnp.int32).at[flat_e].add(1)
    padded = (counts + MOE_BLOCK - 1) // MOE_BLOCK * MOE_BLOCK
    start = jnp.cumsum(counts) - counts
    pend = jnp.cumsum(padded)
    pstart = pend - padded
    dest = pstart[se] + jnp.arange(A) - start[se]
    n_blocks = (A + E * (MOE_BLOCK - 1) + MOE_BLOCK - 1) // MOE_BLOCK
    P = n_blocks * MOE_BLOCK
    tok_buf = jnp.zeros((P,), jnp.int32).at[dest].set(stok)
    w_buf = jnp.zeros((P,), jnp.float32).at[dest].set(sw)
    blk_expert = jnp.minimum(jnp.searchsorted(pend, jnp.arange(n_blocks) * MOE_BLOCK, side='right'), E - 1)
    xs = xf[tok_buf].reshape(n_blocks, MOE_BLOCK, D)

    def expert_block(args):
        xb, e = args
        hid = jax.nn.silu(xb @ w_gate[e]) * (xb @ w_up[e])
        return hid @ w_down[e]

    ys = lax.map(expert_block, (xs, blk_expert)).reshape(P, D)
    out = jnp.zeros((T, D), ys.dtype).at[tok_buf].add(ys * w_buf[:, None].astype(ys.dtype))
    return out.reshape(B, S, D).astype(h.dtype)

def second_inputs(seed: int = 0) -> dict:
    key = jax.random.key(seed)
    ks = iter(jax.random.split(key, 40))
    D = D_MODEL

    def nrm(shape, std):
        return jax.random.normal(next(ks), shape, jnp.float32) * std

    def gain(shape):
        return 1.0 + nrm(shape, 0.02)

    return {
        "x": nrm((BATCH, SEQ, D), 1.0),
        "c": nrm((BATCH, D), 1.0),
        "rel_table": nrm((N_BUCKETS, N_BIAS_HEADS), 0.5),
        "router_w": nrm((D, N_EXPERTS), D ** -0.5),
        "router_b": nrm((N_EXPERTS,), 0.01),
        "final_norm": gain((D,)),
        "norm_mix": gain((DEPTH, D)),
        "norm_ffn": gain((DEPTH, D)),
        "ada_w": nrm((DEPTH, D, 6 * D), ADA_INIT * D ** -0.5),
        "ada_b": nrm((DEPTH, 6 * D), 0.02),
        "moe_w_gate": nrm((DEPTH, N_EXPERTS, D, D_EXPERT), D ** -0.5),
        "moe_w_up": nrm((DEPTH, N_EXPERTS, D, D_EXPERT), D ** -0.5),
        "moe_w_down": nrm((DEPTH, N_EXPERTS, D_EXPERT, D), D_EXPERT ** -0.5),
        "ev_w_in": nrm((N_EVEN_2, D, EVEN_IN), D ** -0.5),
        "ev_w_out": nrm((N_EVEN_2, EVEN_OUT, D), EVEN_OUT ** -0.5),
        "nsa_pos_k": nrm((N_EVEN_2, CMP_LEN, HEAD_DIM), 0.1),
        "nsa_pos_v": nrm((N_EVEN_2, CMP_LEN, HEAD_DIM), 0.1),
        "nsa_ck_w1": nrm((N_EVEN_2, CMP_LEN * HEAD_DIM, CMP_HIDDEN), (CMP_LEN * HEAD_DIM) ** -0.5),
        "nsa_ck_w2": nrm((N_EVEN_2, CMP_HIDDEN, HEAD_DIM), CMP_HIDDEN ** -0.5),
        "nsa_cv_w1": nrm((N_EVEN_2, CMP_LEN * HEAD_DIM, CMP_HIDDEN), (CMP_LEN * HEAD_DIM) ** -0.5),
        "nsa_cv_w2": nrm((N_EVEN_2, CMP_HIDDEN, HEAD_DIM), CMP_HIDDEN ** -0.5),
        "od_w_in": nrm((N_ODD_2, D, ODD_IN), D ** -0.5),
        "od_w_out": nrm((N_ODD_2, ODD_OUT, D), ODD_OUT ** -0.5),
        "mla_q_norm": gain((N_ODD_2, MLA_Q_RANK)),
        "mla_kv_norm": gain((N_ODD_2, MLA_KV_RANK)),
        "mla_w_q_up": nrm((N_ODD_2, MLA_Q_RANK, MLA_HEADS * (MLA_NOPE + MLA_ROPE)), MLA_Q_RANK ** -0.5),
        "mla_w_kv_up": nrm((N_ODD_2, MLA_KV_RANK, MLA_HEADS * (MLA_NOPE + MLA_V)), MLA_KV_RANK ** -0.5),
        "swa_sinks": nrm((N_ODD_2, SWA_HEADS), 1.0),
    }

def second_block(x, c, rel_table, router_w, router_b, final_norm, norm_mix, norm_ffn, ada_w, ada_b,
              moe_w_gate, moe_w_up, moe_w_down, ev_w_in, ev_w_out, nsa_pos_k, nsa_pos_v,
              nsa_ck_w1, nsa_ck_w2, nsa_cv_w1, nsa_cv_w2, od_w_in, od_w_out, mla_q_norm,
              mla_kv_norm, mla_w_q_up, mla_w_kv_up, swa_sinks):
    for layer in range(DEPTH):
        shift_m, scale_m, gate_m, shift_f, scale_f, gate_f = adaln(c, ada_w[layer], ada_b[layer])
        h = rmsnorm(x, norm_mix[layer]) * (1.0 + scale_m) + shift_m
        i = layer // 2
        if layer % 2 == 0:
            mix = even_mixer(h, ev_w_in[i], ev_w_out[i], nsa_pos_k[i], nsa_pos_v[i], nsa_ck_w1[i],
                             nsa_ck_w2[i], nsa_cv_w1[i], nsa_cv_w2[i], rel_table)
        else:
            mix = odd_mixer(h, od_w_in[i], od_w_out[i], mla_q_norm[i], mla_kv_norm[i],
                            mla_w_q_up[i], mla_w_kv_up[i], swa_sinks[i], rel_table)
        x = x + gate_m * mix.astype(x.dtype)
        h = rmsnorm(x, norm_ffn[layer]) * (1.0 + scale_f) + shift_f
        x = x + gate_f * grouped_moe(h, router_w, router_b, moe_w_gate[layer], moe_w_up[layer],
                                     moe_w_down[layer]).astype(x.dtype)
    return rmsnorm(x, final_norm)


def setup_inputs(seed=0):
    out = dict(first_inputs(seed))
    for name, value in second_inputs(seed + 1).items():
        if name != "x":
            out[name + "_2"] = value
    return out


def reference(
    x, norm_g, ffn_w_gate, ffn_w_up, ffn_w_down, attn_w_in, attn_w_out, rel_bias, mlstm_w_in,
    mlstm_b_gates, mlstm_conv_w, mlstm_head_g, mlstm_w_out, c_2, rel_table_2, router_w_2,
    router_b_2, final_norm_2, norm_mix_2, norm_ffn_2, ada_w_2, ada_b_2, moe_w_gate_2,
    moe_w_up_2, moe_w_down_2, ev_w_in_2, ev_w_out_2, nsa_pos_k_2, nsa_pos_v_2, nsa_ck_w1_2,
    nsa_ck_w2_2, nsa_cv_w1_2, nsa_cv_w2_2, od_w_in_2, od_w_out_2, mla_q_norm_2, mla_kv_norm_2,
    mla_w_q_up_2, mla_w_kv_up_2, swa_sinks_2,
):
    x = first_block(
        x, norm_g, ffn_w_gate, ffn_w_up, ffn_w_down, attn_w_in, attn_w_out, rel_bias,
        mlstm_w_in, mlstm_b_gates, mlstm_conv_w, mlstm_head_g, mlstm_w_out,
    )
    return second_block(
        x, c_2, rel_table_2, router_w_2, router_b_2, final_norm_2, norm_mix_2, norm_ffn_2,
        ada_w_2, ada_b_2, moe_w_gate_2, moe_w_up_2, moe_w_down_2, ev_w_in_2, ev_w_out_2,
        nsa_pos_k_2, nsa_pos_v_2, nsa_ck_w1_2, nsa_ck_w2_2, nsa_cv_w1_2, nsa_cv_w2_2, od_w_in_2,
        od_w_out_2, mla_q_norm_2, mla_kv_norm_2, mla_w_q_up_2, mla_w_kv_up_2, swa_sinks_2,
    )


_drawn_inputs = setup_inputs


def setup_inputs(seed=0):
    import zlib

    import numpy as np

    out = dict(_drawn_inputs(seed))
    spreads = {}
    factors = {'mlstm_head_g': 3.473,
     'rel_table_2': 3.129,
     'final_norm_2': 8.362,
     'norm_mix_2': 8.0,
     'norm_ffn_2': 3.498,
     'nsa_pos_k_2': 8.0,
     'nsa_pos_v_2': 8.0,
     'nsa_ck_w1_2': 4.53,
     'nsa_ck_w2_2': 5.074,
     'mla_q_norm_2': 8.0,
     'mla_kv_norm_2': 8.0,
     'mla_w_q_up_2': 3.111,
     'swa_sinks_2': 46.57}
    for name, (base, spread) in spreads.items():
        noise = np.random.default_rng([zlib.crc32(name.encode()), seed]).standard_normal(out[name].shape)
        drawn = base * np.exp(spread * noise) if base else spread * noise
        out[name] = jnp.asarray(drawn.astype(out[name].dtype))
    for name, factor in factors.items():
        out[name] = (out[name] * factor).astype(out[name].dtype)
    return out
```

```python
import math
from contextlib import ExitStack

import numpy as np

import concourse.bass as bass
from concourse import mybir

F32 = mybir.dt.float32
ALU = mybir.AluOpType
ACT = mybir.ActivationFunctionType
AX = mybir.AxisListType

P = 128
T = 256
TT = T // P
D = 1024
KT = D // P
DH = 64
H = 8
FF = 2816
FC = FF // 256
E = 16
FE = 512
EC = FE // 256
W3 = 3 * P
NCMP = 15
NEG = -1e30
EPS = 1e-6
RING = 6
SLOT = 2048
MH = 4
VW = P + 1



def bucket_table(max_distance, distances):
    d = np.maximum(distances, 0)
    scaled = np.log(np.maximum(d, 1).astype(np.float32) / np.float32(16)) / np.float32(math.log(max_distance / 16))
    log_part = 16 + (scaled * np.float32(16)).astype(np.int32)
    return np.where(d < 16, d, np.minimum(log_part, 31))


C_IDENT = 0
C_MSTRICT = C_IDENT + P
C_MINCL = C_MSTRICT + W3
C_CAUSAL = C_MINCL + W3
C_AFTER = C_CAUSAL + W3
C_ONES = C_AFTER + P
C_COS = C_ONES + P
C_SIN = C_COS + TT * 32
C_LOWER = C_SIN + TT * 32
C_EPS = C_LOWER + 16
C_FLIP = C_EPS + 1
NCONST = C_FLIP + P


def shape_constants():
    c = np.zeros((P, NCONST), np.float32)
    p, j = np.arange(P)[:, None], np.arange(T)[None, :]
    c[:, C_IDENT:C_IDENT + P] = np.eye(P)
    for at, mask in ((C_MSTRICT, j > p), (C_MINCL, j >= p)):
        c[:, at:at + T] = mask
        c[:, at + T:at + W3] = mask[:, :P]
    c[:, C_CAUSAL:C_CAUSAL + P] = np.where(j[:, :P] <= p, 0, NEG)
    c[:, C_CAUSAL + P:C_CAUSAL + W3] = np.where(j <= p + P, 0, NEG)
    c[:, C_AFTER:C_AFTER + P] = p > j[:, :P]
    c[:, C_ONES:C_ONES + P] = 1
    inv = np.float32(10000.0) ** (-np.arange(0, 64, 2, dtype=np.float32) / np.float32(64))
    angle = (np.arange(T, dtype=np.float32)[:, None] * inv[None, :]).reshape(TT, P, 32).transpose(1, 0, 2)
    c[:, C_COS:C_COS + TT * 32] = np.cos(angle).reshape(P, TT * 32)
    c[:, C_SIN:C_SIN + TT * 32] = np.sin(angle).reshape(P, TT * 32)
    a = np.arange(4)
    c[:, C_LOWER:C_LOWER + 16] = (a[None, :] < a[:, None]).reshape(1, 16)
    c[:, C_EPS] = EPS
    c[:, C_FLIP:C_FLIP + P] = np.eye(P)[::-1]
    d = 255 - np.arange(W3)
    count = (d <= 128) * 1 + (d % 4 == 0) * 1 + (d % 16 == 0) * 1
    count = np.where(d >= 0, count, 0)
    dil = np.where(count > 0, np.log(np.maximum(count, 1)), NEG)
    rel = np.where(d >= 0, 0, NEG)
    swa = np.where((d >= 0) & (d < 128), 0, NEG)
    rows = np.zeros((32, 5, W3), np.float32)
    rows[:, 0] = bucket_table(2048, d)[None, :] == np.arange(32)[:, None]
    rows[:, 1] = bucket_table(1024, d)[None, :] == np.arange(32)[:, None]
    rows[:, 2], rows[:, 3], rows[:, 4] = dil, rel, swa
    d = 511 - np.arange(512)
    pads = np.zeros((32, 2, 512), np.float32)
    pads[:, 0] = bucket_table(1024, d)[None, :] == np.arange(32)[:, None]
    pads[:, 1] = np.where(d < 128, 0, NEG)
    return c, np.concatenate([rows.reshape(32, 5 * W3), pads.reshape(32, 1024)], axis=1)


def spread(ap, axis, n):
    dims = [list(x) for x in ap.ap]
    return bass.AP(ap.tensor, ap.offset, dims[:axis] + [[0, n]] + dims[axis:])


def build(nc, I, out):
    ctx = ExitStack()
    with ctx:
        def sb(name, shape):
            return ctx.enter_context(nc.sbuf_tensor(name, shape, F32))

        def sem(name):
            return ctx.enter_context(nc.semaphore(name))

        ring = [sb(f"ring{i}", [P, SLOT]) for i in range(RING)]
        x = sb("x", [P, TT, D])
        nrm = sb("nrm", [P, TT, D])
        xT = sb("xT", [P, KT, T])
        const = sb("const", [P, NCONST])
        gain = [sb(f"gain{i}", [P, D]) for i in range(2)]
        mod = sb("mod", [P, 6 * D])
        cB = sb("cB", [P, KT, P])
        biasT = sb("biasT", [P, H, W3])
        big = sb("big", [P, 8192])
        wide = sb("wide", [P, 2, H, W3])
        hT = [sb(f"hT{i}", [P, 2, T]) for i in range(2)]
        PT = [sb(f"PT{i}", [P, W3]) for i in range(2)]
        small = sb("small", [P, 512])
        aux = sb("aux", [P, 1664])
        stat = sb("stat", [P, 8])
        psum = ctx.enter_context(nc.psum_tensor("psum", [P, 8, 512], F32))

        rowbuf = nc.dram_tensor("bias_rows", (3, H, P, W3), F32, kind="Internal").ap()

        loaded = [sem(f"slot{i}_loaded") for i in range(RING)]
        piece_used = sem("piece_used")
        crossed = sem("stage_crossed")
        act_step = sem("act_step")
        dve_step = sem("dve_step")
        const_in = sem("const_in")
        gain_in = [sem(f"gain{i}_in") for i in range(2)]
        gain_used = sem("gain_used")
        extra_in = sem("extra_in")
        bias_in = sem("bias_in")
        rows_ready = sem("rows_ready")
        rows_out = sem("rows_out")
        mod_in = sem("mod_in")
        squared = sem("squared")
        turned = sem("turned")
        gated = sem("gated")
        hidden = sem("hidden")
        proj_read = sem("proj_read")
        ada_read = sem("ada_read")
        score = sem("score")
        biased = sem("biased")
        expd = sem("expd")
        p_turned = sem("p_turned")
        p_read = sem("p_read")
        headout = sem("headout")
        out_done = sem("out_done")

        def trio(name):
            return sem(name + "_pe"), sem(name + "_act"), sem(name + "_dve")

        setup_pe, setup_act, setup_dve = trio("setup")
        pad_dve, pad_act = sem("padding_dve"), sem("padding_act")
        stick_pe, stick_act, stick_dve = trio("stick")
        gates_pe, gates_act, gates_dve = trio("gates")
        ml_pe, ml_act, ml_dve = trio("mlstm")
        comp_pe, comp_act, comp_dve = trio("compress")
        cmp_pe, cmp_act, cmp_dve = trio("cmp")
        lat_pe, lat_act, lat_dve = trio("latent")
        route_pe, route_act, route_dve = trio("router")

        ident = const[:, C_IDENT:C_IDENT + P]

        def cols(w, c0, n):
            return w[:, c0:c0 + n].rearrange("(k p) n -> p k n", p=P)

        def slot(n, shape):
            k, w = shape
            return ring[n % RING][:, 0:k * w].rearrange("p (k w) -> p k w", k=k)

        def linear_slots(w, widths):
            at, got = 0, []
            for n in widths:
                got.append(("one", cols(w, at, n), (w.shape[0] // P, n)))
                at += n
            return got

        g_w, u_w, d_w = I["ffn_w_gate"], I["ffn_w_up"], I["ffn_w_down"]

        def ffn_chunk(which, layer, part, c):
            if which == "d":
                w = d_w[layer, part].rearrange("(c s p) n -> c p s n", p=P, s=2)
                return w[c]
            w = {"g": g_w, "u": u_w}[which][layer, part].rearrange("(k p) (c n) -> c p k n", p=P, n=256)
            return w[c]

        mg, mu, md = I["moe_w_gate_2"], I["moe_w_up_2"], I["moe_w_down_2"]

        def moe_chunk(which, layer, c, i):
            e = c // EC if i is None else i + c // EC
            if which == "d":
                return md[layer].rearrange("e (h s p) n -> h e p s n", p=P, s=2, h=EC)[c % EC][e]
            w = {"g": mg, "u": mu}[which]
            return w[layer].rearrange("e (k p) (h n) -> h e p k n", p=P, h=EC)[c % EC][e]

        GU, DN = (KT, 256), (2, D)

        ATTN_IN = [256] * 12
        MLSTM_IN = [256] * 16 + [16]
        EVEN_IN = [256, 256, 256, 256, 256, 24] + [256] * 6
        ODD_IN = [256, 192, 256, 256, 256]
        OUT4 = [256] * 4

        def slot_count(n):
            return 16 * (n // RING + 1)

        def chunk_piece(n0, which, c, chunks):
            if which == "d":
                return n0 + 2 + 3 * c + 2 if c < chunks - 1 else n0 + 3 * chunks - 1
            return n0 + (0 if c == 0 else 2 + 3 * (c - 1)) + (1 if which == "u" else 0)

        def loop_pairs(chunks):
            return (chunks - 2) // 2

        wide_flat = wide[:, :, :, :].rearrange("p a h w -> p (a h w)")

        def wide_at(at, n):
            return wide_flat[0:8, at:at + n]

        S_RB, S_CONVW = 0, 24
        S_NMX, S_SUM, S_INV = 88, 104, 120
        S_G = 136
        S_COL, S_THR, S_DEN = 184, 200, 216
        S_PAD = 440
        S_RW, S_R = 232, 360

        R_DIL, R_REL, R_PAD, R_PADMASK, R_END = 0, W3, 5 * W3, 5 * W3 + 512, 5 * W3 + 1024

        pad_b = [wide_at(1536 + 512 * i, 512) for i in range(2)]
        pad_m = [wide_at(2560 + 640 * i, 513) for i in range(2)]
        pad_a = [wide_at(3840 + 1024 * i, 512) for i in range(2)]
        pad_e = [wide_at(4352 + 1024 * i, 512) for i in range(2)]

        A_I, A_F, A_L, A_B, A_G = 256, 512, 768, 1024, 1280
        A_QRT, A_KRT = 384, 1408

        QA, KA, VA, QD, KD, VD = (1024 * i for i in range(6))
        M_PRE, M_V = 0, 4096
        (N_Q, N_KC, N_VC, N_KS, N_VS, N_KW, N_VW, N_QB, N_KB, N_VB) = (
            0, 1024, 1280, 1536, 1792, 2048, 2304, 2560, 3584, 4608)
        N_F = 5632
        (N_POS, N_U, N_GT, N_KCMP, N_VCMP) = (6656, 6720, 7232, 7360, 7376)
        (O_Q, O_K, O_V, O_CQ, O_CKV, O_KR, O_QM, O_KVM, O_QNT, O_KNT) = (
            0, 1024, 1280, 1536, 2048, 2304, 2432, 3968, 6016, 7040)

        def big_n(at, w):
            return big[:, at:at + TT * w].rearrange("p (t w) -> p t w", t=TT)

        def big_t(at, m):
            return big[:, at + m * T:at + (m + 1) * T]

        def t2(at, scale=1.0):
            return [("TT", 0, 256, big[:, at:at + 512], scale)]

        def n1(dst, c=0, scale=1.0):
            return ("N", c, dst.shape[2], dst, scale)

        def n256(at, w, j):
            return [n1(big_n(at, w)[:, :, j * 256:(j + 1) * 256])]

        def qgroup(kv, at, scale):
            return [("Q", kv, 256, big[64 * kv:64 * kv + 64, at:at + 1024], scale)]

        vM = big[:, M_V:M_V + TT * H * VW].rearrange("p (t h w) -> p t h w", t=TT, h=H)
        oM = mod[:, 0:TT * D].rearrange("p (t w) -> p t w", t=TT)

        def gview(at):
            return small[:, at:at + 48].rearrange("p (t w) -> p t w", t=TT)

        PROJ = {
            "attn": [t2(QA, 0.125), t2(QA + 512, 0.125), t2(KA), t2(KA + 512), n256(VA, 512, 0), n256(VA, 512, 1),
                     t2(QD, 0.125), t2(QD + 512, 0.125), t2(KD), t2(KD + 512), n256(VD, 512, 0), n256(VD, 512, 1)],
            "mlstm": [t2(M_PRE + 512 * j) for j in range(8)]
                     + [[("V", 0, 256, vM[:, :, 2 * j:2 * j + 2, 0:P], 1.0)] for j in range(4)]
                     + [[n1(oM[:, :, 256 * j:256 * j + 256])] for j in range(4)]
                     + [[("T", 0, 8, aux[0:8, A_I:A_I + T], 1.0), ("T", 8, 8, aux[0:8, A_F:A_F + T], 1.0)]],
            "even": [qgroup(0, N_Q, 0.125), qgroup(1, N_Q, 0.125),
                     [("T", 0, P, big_t(N_KC, 0), 1.0), ("T", P, P, big_t(N_VC, 0), 1.0)],
                     [("T", 0, P, big_t(N_KS, 0), 1.0), n1(big_n(N_VS, P), P)],
                     [("T", 0, P, big_t(N_KW, 0), 1.0), n1(big_n(N_VW, P), P)],
                     [n1(gview(S_G))],
                     t2(N_QB, 0.125), t2(N_QB + 512, 0.125), t2(N_KB), t2(N_KB + 512),
                     n256(N_VB, 512, 0), n256(N_VB, 512, 1)],
            "odd": [[n1(big_n(O_CQ, 256))], [n1(big_n(O_CKV, P)), n1(big_n(O_KR, 64), P)],
                    qgroup(0, O_Q, 0.125), qgroup(1, O_Q, 0.125),
                    [("T", 0, P, big_t(O_K, 0), 1.0), n1(big_n(O_V, P), P)]],
        }
        PROJ_AT, at = {}, 0
        for name in PROJ:
            PROJ_AT[name] = at
            at += len(PROJ[name])

        def pair_heads(qat, kat):
            def parts(h):
                p0 = 64 * (h % 2)
                return [(big[p0:p0 + 64, qat + (h // 2) * T:qat + (h // 2 + 1) * T],
                         big[p0:p0 + 64, kat + (h // 2) * T:kat + (h // 2 + 1) * T])]
            return parts

        def group_heads(qat, kat):
            def parts(h):
                p0, g = 64 * (h // 4), h % 4
                return [(big[p0:p0 + 64, qat + g * T:qat + (g + 1) * T], big[p0:p0 + 64, kat:kat + T])]
            return parts

        def mla_heads(h):
            qrT = aux[0:64, A_QRT + h * T:A_QRT + (h + 1) * T]
            return [(big_t(O_QNT, h), big_t(O_KNT, h)), (qrT, aux[0:64, A_KRT:A_KRT + T])]

        vmla = big_n(O_KVM, 1024).rearrange("p t (h w) -> p t h w", h=MH)

        def soft(parts, v, heads, dv, dst, bias=True, scale=1.0, pad=None, gate=None):
            return dict(parts=parts, v=v, heads=heads, dv=dv, dst=dst, bias=bias, scale=scale, pad=pad, gate=gate)

        SOFT = {
            "dilated": soft(pair_heads(QD, KD), lambda h, t: big_n(VD, 512)[:, t, 64 * h:64 * h + 64], H, 64, 512),
            "selected": soft(group_heads(N_Q, N_KS), lambda h, t: big_n(N_VS, P)[:, t, 64 * (h // 4):64 * (h // 4) + 64],
                             H, 64, 0, gate=1),
            "window": soft(group_heads(N_Q, N_KW), lambda h, t: big_n(N_VW, P)[:, t, 64 * (h // 4):64 * (h // 4) + 64],
                           H, 64, 0, gate=2, pad=S_PAD),
            "moba": soft(pair_heads(N_QB, N_KB), lambda h, t: big_n(N_VB, 512)[:, t, 64 * h:64 * h + 64], H, 64, 512),
            "mla": soft(mla_heads, lambda h, t: vmla[:, t, h, P:2 * P], MH, P, 0, bias=False, scale=192.0 ** -0.5),
            "sliding": soft(group_heads(O_Q, O_K), lambda h, t: big_n(O_V, P)[:, t, 64 * (h // 4):64 * (h // 4) + 64],
                            H, 64, 512, pad=S_PAD + 32),
        }
        PADDED = [name for name in SOFT if SOFT[name]["pad"] is not None]
        at, steps = 0, 0
        for spec in SOFT.values():
            spec["head0"], spec["step0"], spec["steps"] = at, steps, 3 if spec["pad"] is None else 5
            at, steps = at + spec["heads"], steps + spec["heads"] * spec["steps"]

        STAGES = [("setup", (), 0)]
        stream = []

        def add(name, *args, gains=0, pieces=()):
            STAGES.append((name, args, gains))
            stream.extend(pieces)

        def mixer_end(weights, residual):
            add("turn")
            add("outproj", pieces=linear_slots(weights, OUT4))
            add(*residual, gains=1 if residual[1] == "norm" else 0)

        for layer in range(2):
            add("norm", None, gains=1)
            add("turn")
            add("ffn", FC, False, pieces=[("ffn", (layer, 0), FC)])
            add("residual", "norm", 0.5, gains=1)
            add("norm", None, gains=1)
            add("turn")
            if layer == 0:
                add("project", "attn", pieces=linear_slots(I["attn_w_in"][0], ATTN_IN))
                add("stick")
                add("soft", "dilated")
                mixer_end(I["attn_w_out"][0], ("residual", "norm", 1.0))
            else:
                add("project", "mlstm", pieces=linear_slots(I["mlstm_w_in"][0], MLSTM_IN))
                add("gates")
                add("mlstm", gains=1)
                mixer_end(I["mlstm_w_out"][0], ("residual", "norm", 1.0))
            add("norm", None, gains=1)
            add("turn")
            add("ffn", FC, False, pieces=[("ffn", (layer, 1), FC)])
            add("residual", "norm", 0.5, gains=1)
        for layer in range(2):
            add("ada", pieces=[("ada", layer, 24)])
            add("norm", 0, gains=1)
            add("turn")
            if layer == 0:
                add("project", "even", pieces=linear_slots(I["ev_w_in_2"][0], EVEN_IN))
                add("compress", pieces=[("one", w1[half * 1024:half * 1024 + 1024, :].rearrange("(k p) n -> p k n", p=P), GU)
                                        for w1 in (I["nsa_ck_w1_2"][0], I["nsa_cv_w1_2"][0]) for half in range(2)])
                add("cmp")
                for name in ("selected", "window", "moba"):
                    add("soft", name)
                mixer_end(I["ev_w_out_2"][0], ("residual", "gate", 2))
            else:
                add("project", "odd", pieces=linear_slots(I["od_w_in_2"][0], ODD_IN))
                add("latent", pieces=[("one", cols(I["mla_w_q_up_2"][0], 0, 768), (2, 768)),
                                      ("one", cols(I["mla_w_kv_up_2"][0], 0, 1024), (1, 1024))])
                add("soft", "mla")
                add("soft", "sliding")
                mixer_end(I["od_w_out_2"][0], ("residual", "gate", 2))
            add("norm", 3, gains=1)
            add("turn")
            add("router")
            add("ffn", E * EC, True, pieces=[("moe", (layer, 0), E * EC)])
            add("residual", "gate", 5)
        add("final", gains=1)

        seen, INSTANCE = {}, []
        for name, _, _ in STAGES:
            INSTANCE.append(seen.get(name, 0))
            seen[name] = INSTANCE[-1] + 1

        GAINS = []
        for layer in range(2):
            g = [I["norm_g"][layer, j] for j in range(6)]
            GAINS += g[0:3] + ([I["mlstm_head_g"][0]] if layer == 1 else []) + g[3:6]
        for layer in range(2):
            GAINS += [I["norm_mix_2"][layer], I["norm_ffn_2"][layer]]
        GAINS.append(I["final_norm_2"])
        assert len(GAINS) == sum(s[2] for s in STAGES)

        def boundary(eng, s):
            eng.drain().then_inc(crossed, 1)
            eng.wait_ge(crossed, 3 * s)

        block = ctx.enter_context(nc.Block())

        @block.sync
        def _(sp):
            def load(n, src, shape, i=None):
                if i is not None:
                    sp.wait_ge(piece_used, i * 6 + max(n - RING + 1, 1))
                elif n >= RING:
                    sp.wait_ge(piece_used, n - RING + 1)
                sp.dma_start(slot(n, shape), src).then_inc(loaded[n % RING], 16)

            def chunked(n, source, chunks):
                def piece(which, c, i=None):
                    load(chunk_piece(n, which, c, chunks), source(which, c, i), DN if which == "d" else GU, i)

                for which, c in (("g", 0), ("u", 0), ("g", 1), ("u", 1), ("d", 0)):
                    piece(which, c)
                with sp.Fori(0, loop_pairs(chunks)) as i:
                    for c in (1, 2):
                        piece("g", c + 1, i)
                        piece("u", c + 1, i)
                        piece("d", c, i)
                for c in range(1 + 2 * loop_pairs(chunks), chunks):
                    if c + 1 < chunks:
                        piece("g", c + 1)
                        piece("u", c + 1)
                    piece("d", c)

            n = 0
            sp.dma_start(const[:, :], I["const"]).then_inc(const_in, 16)
            sp.dma_start(x[:, :, :], I["x"][0].rearrange("(t p) d -> p t d", p=P)).then_inc(const_in, 16)
            for kind, what, more in stream:
                if kind == "one":
                    load(n, what, more)
                    n += 1
                elif kind == "ada":
                    w = I["ada_w_2"][what].rearrange("(k p) (s r n) -> r s p k n", p=P, r=RING, n=256)
                    with sp.Fori(0, 4) as i:
                        for r in range(RING):
                            load(n + r, w[r][i], GU, i)
                    n += 24
                elif kind == "ffn":
                    chunked(n, lambda which, c, i: ffn_chunk(which, *what, c if i is None else i * 2 + c), more)
                    n += 3 * more
                else:
                    chunked(n, lambda which, c, i: moe_chunk(which, what[0], c, i), more)
                    n += 3 * more

        @block.gpsimd
        def _(pool):
            def load_gain(k):
                if k >= 2:
                    pool.wait_ge(gain_used, k - 1)
                pool.dma_start(gain[k % 2][:, :], GAINS[k].rearrange("(a n) -> a n", a=1)
                               .broadcast_to([P, D])).then_inc(gain_in[k % 2], 16)

            def load_bias(kind):
                at = rowbuf[kind].offset + 127
                pool.dma_start(biasT[:, :, P:W3],
                               bass.AP(rowbuf.tensor, at, [[W3 - 1, P], [P * W3, H], [1, T]])).then_inc(bias_in, 16)
                pool.dma_start(biasT[:, :, 0:P],
                               bass.AP(rowbuf.tensor, at + P, [[W3 - 1, P], [P * W3, H], [1, P]])).then_inc(bias_in, 16)

            def small_in(dst, src):
                pool.dma_start(dst, src).then_inc(extra_in, 16)

            def row(ap):
                return ap.rearrange("(a n) -> a n", a=1)

            small_in(aux[0:32, 0:8], I["rel_bias"])
            small_in(aux[0:32, 8:16], I["rel_table_2"])
            small_in(big[0:32, 0:R_END], I["rows"])
            small_in(aux[0:8, 16:144], I["c_2"][0].rearrange("(k p) -> k p", p=P))
            small_in(small[:, S_RB:S_RB + E], row(I["router_b_2"]).broadcast_to([P, E]))
            small_in(aux[0:8, 144:145], I["swa_sinks_2"].rearrange("a h -> h a"))
            small_in(small[:, S_RW:S_RW + P].rearrange("p (k e) -> p k e", k=KT),
                     I["router_w_2"].rearrange("(k p) e -> p k e", p=P))
            load_gain(0)
            load_gain(1)
            g = 2
            for s, (name, args, used) in enumerate(STAGES):
                if name == "setup":
                    pool.wait_ge(rows_out, 48)
                    load_bias(0)
                if name == "project" and args[0] != "attn":
                    pool.wait_ge(crossed, 3 * s)
                if name == "project" and args[0] == "mlstm":
                    small_in(aux[0:8, 0:1], I["mlstm_b_gates"][0, 0:8].rearrange("(p a) -> p a", a=1))
                    small_in(aux[0:8, 1:2], I["mlstm_b_gates"][0, 8:16].rearrange("(p a) -> p a", a=1))
                    small_in(aux[0:64, 16:144], I["mlstm_conv_w"][0].rearrange("j (t p) -> (j t) p", p=P))
                if name == "project" and args[0] == "even":
                    load_bias(1)
                    for at in (0, 64):
                        small_in(aux[0:32, at:at + 64], I["nsa_pos_k_2"][0])
                        small_in(aux[0:32, P + at:P + at + 64], I["nsa_pos_v_2"][0])
                    for at, w in ((256, I["nsa_ck_w2_2"]), (384, I["nsa_cv_w2_2"])):
                        small_in(aux[:, at:at + P].rearrange("p (k n) -> p k n", k=2),
                                 w[0].rearrange("(k p) n -> p k n", p=P))
                if name == "project" and args[0] == "odd":
                    load_bias(2)
                    small_in(aux[:, 0:256], I["mla_q_norm_2"].broadcast_to([P, 256]))
                    small_in(aux[:, 256:384], I["mla_kv_norm_2"].broadcast_to([P, P]))
                if name == "ada":
                    pool.wait_ge(crossed, 3 * s)
                    layer = INSTANCE[s]
                    pool.dma_start(mod[:, :], I["ada_b_2"][layer:layer + 1, :].broadcast_to([P, 6 * D])).then_inc(mod_in, 16)
                for _ in range(used):
                    if g < len(GAINS):
                        load_gain(g)
                        g += 1

        PIECE0, n_piece, extra = [], 0, iter(())
        SLOTS = {"outproj": 4, "compress": 4, "latent": 2, "ada": 24}
        SQ0, n_sq = [], 0
        for name, args, _ in STAGES:
            PIECE0.append(n_piece)
            SQ0.append(n_sq)
            n_piece += (3 * args[0] if name == "ffn" else len(PROJ[args[0]]) if name == "project"
                        else SLOTS.get(name, 0))
            n_sq += 2 if name in ("norm", "final") or (name == "residual" and args[0] == "norm") else 0
        GAIN0 = [sum(u for _, _, u in STAGES[:s]) for s in range(len(STAGES))]
        EXTRA = {"setup": 7 * 16, "mlstm": 10 * 16, "even": 16 * 16, "odd": 18 * 16}

        def ffn_bases(k):
            if k < 4:
                return k * FC, k * FC
            return 4 * FC + (k - 4) * E * EC, 4 * FC + 2 * (k - 4) * E * EC

        def wait_gain(eng, g):
            eng.wait_ge(gain_in[g % 2], 16 * (g // 2 + 1))

        GB, UB = 4, 6
        route = big[:, 4096:8192]
        routing = big[:, 0:4096].rearrange("p (e t) -> p e t", e=E)
        cv = wide_flat[:, 0:4096].rearrange("p (m t) -> p m t", t=T)
        mE = [wide_flat[:, 4096 + W3 * i:4096 + W3 * (i + 1)] for i in range(2)]
        raw = big[:, 0:TT * H * VW].rearrange("p (t h w) -> p t h w", t=TT, h=H)
        hid = nrm[:, :, :].rearrange("p t (h w) -> p t h w", h=H)
        qm = big[:, O_QM:O_QM + 1536].rearrange("p (t h w) -> p t h w", t=TT, h=MH)
        blocksF = [big[:, N_F + 480 * i:N_F + 480 * (i + 1)].rearrange("p (j v n) -> p j v n", j=16, v=2)
                   for i in range(2)]
        cS = wide_flat[:, 0:256].rearrange("p (h t n) -> p h t n", h=H, t=TT)
        cPT = wide_flat[:, 1024:3072]

        @block.tensor
        def _(pe):
            def mm(out_, lhsT, rhs, start, stop, **kw):
                return pe.matmul(out_, lhsT, rhs, start=start, stop=stop, **kw)

            def piece_in(n, i=None):
                if i is None:
                    pe.wait_ge(loaded[n % RING], slot_count(n))
                else:
                    pe.wait_ge(loaded[n % RING], i * 16 + slot_count(n))

            def setup(s, k):
                pe.wait_ge(const_in, 32)
                pe.wait_ge(extra_in, EXTRA["setup"])
                pe.transpose(psum[:, 0, 0:8], aux[0:8, 16:144], ident[0:8, 0:8])
                mm(psum[0:8, 1, 0:W3], aux[0:32, 0:8], big[0:32, 0:W3], True, True)
                mm(psum[0:8, 2, 0:W3], aux[0:32, 8:16], big[0:32, R_REL:R_REL + W3], True, True)
                mm(psum[0:8, 3, :], aux[0:32, 8:16], big[0:32, R_PAD:R_PAD + 512], True, True).then_inc(setup_pe, 1)
                pe.wait_ge(setup_dve, 3)
                for i in range(2):
                    for t in range(TT):
                        lo, at = 383 - P * t, 32 * i + 8 * t
                        pe.transpose(psum[:, 4, at:at + 8], pad_m[i][:, lo + 1:lo + 1 + P], ident[0:8, 0:8])
                        last = pe.transpose(psum[:, 4, at + 16:at + 24], pad_b[i][:, lo:lo + P], ident[0:8, 0:8])
                last.then_inc(setup_pe, 1)
                pe.wait_ge(setup_dve, 4)
                mm(psum[:, 5, 0:64], const[:, C_FLIP:C_FLIP + P], small[:, S_PAD:S_PAD + 64], True, True)\
                    .then_inc(setup_pe, 1)

            def turn(s, k):
                for q in range(4):
                    t, half = q // 2, q % 2
                    for i in range(4):
                        f = (4 * half + i) * P
                        last = pe.transpose(psum[:, q, i * P:(i + 1) * P], nrm[:, t, f:f + P], ident)
                    last.then_inc(turned, 1)

            def ffn(s, k, chunks, moe):
                n0 = PIECE0[s]
                c0, h0 = ffn_bases(k)
                steps = 2 if moe else 1

                def gate_up_products(c, i=None):
                    if c >= 2:
                        v = h0 + steps * (c - 1)
                        pe.wait_ge(hidden, v if i is None else i * (2 * steps) + v)
                    for which, bank in (("g", GB + c % 2), ("u", UB + c % 2)):
                        n = chunk_piece(n0, which, c, chunks)
                        piece_in(n, i)
                        w = slot(n, GU)
                        for f in range(2):
                            for kt in range(KT):
                                last = mm(psum[:, bank, f * T:(f + 1) * T], w[:, kt, f * P:(f + 1) * P],
                                          xT[:, kt, :], kt == 0, kt == KT - 1)
                        last.then_inc(piece_used, 1)

                def down_products(c, i=None):
                    v = h0 + steps * (c + 1)
                    pe.wait_ge(hidden, v if i is None else i * (2 * steps) + v)
                    n = chunk_piece(n0, "d", c, chunks)
                    piece_in(n, i)
                    w = slot(n, DN)
                    for f in range(2):
                        for t in range(TT):
                            for half in range(2):
                                last = mm(psum[:, 2 * t + half, :], hT[c % 2][:, f, t * P:(t + 1) * P],
                                          w[:, f, half * 512:(half + 1) * 512],
                                          c == 0 and f == 0, c == chunks - 1 and f == 1)
                    last.then_inc(piece_used, 1)

                gate_up_products(0)
                gate_up_products(1)
                down_products(0)
                with pe.Fori(0, loop_pairs(chunks)) as i:
                    for c in (1, 2):
                        gate_up_products(c + 1, i)
                        down_products(c, i)
                for c in range(1 + 2 * loop_pairs(chunks), chunks):
                    if c + 1 < chunks:
                        gate_up_products(c + 1)
                    down_products(c)

            def project(s, k, name):
                for j, pieces in enumerate(PROJ[name]):
                    n = PIECE0[s] + j
                    if j >= 2:
                        pe.wait_ge(proj_read, PROJ_AT[name] + j - 1)
                    piece_in(n)
                    w = ring[n % RING]
                    width = {"attn": ATTN_IN, "mlstm": MLSTM_IN, "even": EVEN_IN, "odd": ODD_IN}[name][j]
                    w = slot(n, (KT, width))
                    b, at = 2 * (j % 2), 0
                    for kind, c, m, _, _ in pieces:
                        if kind in ("N", "V"):
                            for t in range(TT):
                                for kt in range(KT):
                                    last = mm(psum[:, b, at:at + m], xT[:, kt, t * P:(t + 1) * P],
                                              w[:, kt, c:c + m], kt == 0, kt == KT - 1)
                                at += m
                            continue
                        tiles = {"TT": [(0, P, 0), (P, P, 0)], "T": [(c, m, 0)],
                                 "Q": [(64 * g, 64, 64 * c) for g in range(4)]}[kind]
                        for c1, m1, p0 in tiles:
                            for kt in range(KT):
                                last = mm(psum[p0:p0 + m1, b + at // 512, at % 512:at % 512 + T],
                                          w[:, kt, c1:c1 + m1], xT[:, kt, :], kt == 0, kt == KT - 1)
                            at += T
                    last.then_inc(piece_used, 1)

            def outproj(s, k):
                for j in range(4):
                    n = PIECE0[s] + j
                    piece_in(n)
                    w = slot(n, GU)
                    for t in range(TT):
                        for kt in range(KT):
                            last = mm(psum[:, 2 * t + j // 2, (j % 2) * 256:(j % 2 + 1) * 256],
                                      xT[:, kt, t * P:(t + 1) * P], w[:, kt, :], kt == 0, kt == KT - 1)
                    last.then_inc(piece_used, 1)

            def stick(s, k):
                def scores(h):
                    if h >= 2:
                        pe.wait_ge(stick_dve, h - 1)
                    p0, c = 64 * (h % 2), (h // 2) * T
                    q, key = big[p0:p0 + 64, QA + c:QA + c + T], big[p0:p0 + 64, KA + c:KA + c + T]
                    mm(psum[:, h % 2, 0:T], key[:, 0:P], q, True, True)
                    mm(psum[:, h % 2, T:W3], key[:, P:T], q[:, P:T], True, True).then_inc(stick_pe, 1)

                def later(h):
                    pe.wait_ge(stick_dve, H + 3 * (h + 1))
                    if h >= 2:
                        pe.wait_ge(stick_dve, 4 * H + h - 1)
                    sp_h, b = wide[:, 1, h, :], 2 + h % 2
                    mm(psum[:, b, 0:T], const[:, C_AFTER:C_AFTER + P], sp_h[:, 0:T], True, False,
                       skip_group_check=True)
                    mm(psum[:, b, P:T], const[:, C_ONES:C_ONES + P], sp_h[:, T:W3], False, True,
                       skip_group_check=True)
                    mm(psum[:, b, T:W3], const[:, C_AFTER:C_AFTER + P], sp_h[:, T:W3], True, True)\
                        .then_inc(stick_pe, 1)

                def values(h):
                    pe.wait_ge(stick_dve, 5 * H + h + 1)
                    w = wide[:, 0, h, :]
                    v = big_n(VA, 512)[:, :, 64 * h:64 * h + 64]
                    mm(psum[:, 4, 64 * h:64 * h + 64], w[:, 0:P], v[:, 0], True, True)
                    mm(psum[:, 5, 64 * h:64 * h + 64], w[:, P:T], v[:, 0], True, False)
                    return mm(psum[:, 5, 64 * h:64 * h + 64], w[:, T:W3], v[:, 1], False, True)

                for h in range(H):
                    scores(h)
                for h in range(H):
                    later(h)
                for h in range(H):
                    last = values(h)
                last.then_inc(stick_pe, 1)

            def soft_attention(s, k, name):
                a = SOFT[name]
                h0, s0, n, dv = a["head0"], a["step0"], a["steps"], a["dv"]

                def scores(h):
                    if h >= 2:
                        pe.wait_ge(biased, s0 + n * (h - 2) + 1)
                    parts = a["parts"](h)
                    for lo, hi, t in ((0, P, 0), (P, W3, 1)):
                        for i, (q, key) in enumerate(parts):
                            last = mm(psum[:, h % 2, lo:hi], q[:, t * P:(t + 1) * P], key[:, 0:hi - lo],
                                      i == 0, i == len(parts) - 1)
                    last.then_inc(score, 1)

                def turn_probs(h):
                    pe.wait_ge(expd, 2 * (h0 + h + 1))
                    if h >= 2:
                        pe.wait_ge(p_read, h0 + h - 1)
                    for i in range(3):
                        last = pe.transpose(psum[:, 2 + h % 2, i * P:(i + 1) * P],
                                            wide[:, 0, h, i * P:(i + 1) * P], ident)
                    last.then_inc(p_turned, 1)

                def values(h):
                    pe.wait_ge(p_read, h0 + h + 1)
                    p, c = PT[h % 2], slice(h * dv, (h + 1) * dv)
                    mm(psum[:, 4, c], p[:, 0:P], a["v"](h, 0), True, True)
                    mm(psum[:, 5, c], p[:, P:T], a["v"](h, 0), True, False)
                    mm(psum[:, 5, c], p[:, T:W3], a["v"](h, 1), False, True).then_inc(headout, 1)

                scores(0)
                scores(1)
                for h in range(a["heads"]):
                    turn_probs(h)
                    if h + 2 < a["heads"]:
                        scores(h + 2)
                    if h >= 1:
                        values(h - 1)
                values(a["heads"] - 1)

            def gates(s, k):
                pe.wait_ge(extra_in, EXTRA["mlstm"])
                pe.transpose(psum[:, 0, 0:64], aux[0:64, 16:144], ident[0:64, 0:64]).then_inc(gates_pe, 1)
                pe.wait_ge(gates_act, 2)
                for t in range(TT):
                    pe.transpose(psum[:, 1, 8 * t:8 * t + 8], aux[0:8, A_G + t * P:A_G + (t + 1) * P], ident[0:8, 0:8])
                    last = pe.transpose(psum[:, 1, 16 + 8 * t:24 + 8 * t],
                                        aux[0:8, A_F + t * P:A_F + (t + 1) * P], ident[0:8, 0:8])
                last.then_inc(gates_pe, 1)

            def mlstm(s, k):
                def products(h):
                    if h >= 2:
                        pe.wait_ge(ml_dve, 4 * (h - 1))
                    mm(psum[:, h % 2, 0:T], spread(ident[0:8, h], 1, P), aux[0:8, A_L:A_L + T], True, True)\
                        .then_inc(ml_pe, 1)
                    mm(psum[:, 2 + h % 2, 0:T], cv[:, 8 + h, 0:P], cv[:, h, :], True, True)
                    mm(psum[:, 2 + h % 2, T:W3], cv[:, 8 + h, P:T], cv[:, h, P:T], True, True).then_inc(ml_pe, 1)

                def values(h):
                    pe.wait_ge(ml_dve, 4 * (h + 1))
                    if h >= 2:
                        pe.wait_ge(ml_act, 2 * h - 1)
                    p, b = PT[h % 2], 4 + h % 2
                    mm(psum[:, b, 0:VW], p[:, 0:P], vM[:, 0, h, :], True, True)
                    mm(psum[:, b, VW:2 * VW], p[:, P:T], vM[:, 0, h, :], True, False)
                    mm(psum[:, b, VW:2 * VW], p[:, T:W3], vM[:, 1, h, :], False, True).then_inc(ml_pe, 1)

                products(0)
                for h in range(H):
                    if h + 1 < H:
                        products(h + 1)
                    values(h)

            def ada(s, k):
                n0 = PIECE0[s]
                with pe.Fori(0, 4) as i:
                    for r in range(RING):
                        pe.wait_ge(ada_read, i * 6 + (26 * k + r + 1))
                        piece_in(n0 + r, i)
                        w = slot(n0 + r, GU)
                        for kt in range(KT):
                            last = mm(psum[:, r % 2, 0:256], cB[:, kt, :], w[:, kt, :], kt == 0, kt == KT - 1)
                        last.then_inc(piece_used, 1)

            def compress(s, k):
                pe.wait_ge(extra_in, EXTRA["even"])
                pe.transpose(psum[:, 0, 0:32], aux[0:32, 0:P], ident[0:32, 0:32])
                pe.transpose(psum[:, 0, 32:64], aux[0:32, P:2 * P], ident[0:32, 0:32]).then_inc(comp_pe, 1)
                pe.wait_ge(comp_dve, 9)
                for i in range(2):
                    for half in range(2):
                        n = PIECE0[s] + 2 * i + half
                        piece_in(n)
                        w = slot(n, GU)
                        for kt in range(KT):
                            j = half * KT + kt
                            last = mm(psum[0:30, 1 + i, 0:256], blocksF[i][:, j, :, :], w[:, kt, :],
                                      j == 0, j == 15)
                        last.then_inc(piece_used, 1)
                pe.wait_ge(comp_act, 1)
                for i in range(2):
                    for half in range(2):
                        at = N_U + 256 * i + P * half
                        last = pe.transpose(psum[:, 3, (2 * i + half) * 30:(2 * i + half + 1) * 30],
                                            big[0:30, at:at + P], ident[0:30, 0:30])
                last.then_inc(comp_pe, 1)
                pe.wait_ge(comp_dve, 10)
                for v in range(2):
                    for half in range(2):
                        g = N_GT + 30 * half + NCMP * v
                        mm(psum[64 * v:64 * v + 64, 4, 0:NCMP], aux[:, 256 + 64 * half:320 + 64 * half],
                           big[:, g:g + NCMP], half == 0, half == 1)
                for v in range(2):
                    for half in range(2):
                        g = N_GT + 60 + 30 * half + NCMP * v
                        last = mm(psum[0:NCMP, 5, 64 * v:64 * v + 64], big[:, g:g + NCMP],
                                  aux[:, 384 + 64 * half:448 + 64 * half], half == 0, half == 1)
                last.then_inc(comp_pe, 1)

            def cmp_attention(s, k):
                for h in range(H):
                    p0, c = 64 * (h // 4), N_Q + (h % 4) * T
                    for t in range(TT):
                        at = (2 * h + t) * 16
                        last = mm(psum[:, (0, 7)[h // 4], at:at + NCMP], big[p0:p0 + 64, c + t * P:c + (t + 1) * P],
                                  big[p0:p0 + 64, N_KCMP:N_KCMP + NCMP], True, True)
                last.then_inc(cmp_pe, 1)
                pe.wait_ge(cmp_act, 2)
                for i in range(2 * H):
                    last = pe.transpose(psum[0:NCMP, 1 + i // 4, (i % 4) * P:(i % 4 + 1) * P],
                                        cS[:, i // 2, i % 2, 0:NCMP], ident)
                last.then_inc(cmp_pe, 1)
                pe.wait_ge(cmp_act, 3)
                for h in range(H):
                    for t in range(TT):
                        i = 2 * h + t
                        v = N_VCMP + 64 * (h // 4)
                        last = mm(psum[:, 5 + t, 64 * h:64 * h + 64], cPT[0:NCMP, i * P:(i + 1) * P],
                                  big[0:NCMP, v:v + 64], True, True)
                last.then_inc(cmp_pe, 1)

            def latent(s, k):
                pe.wait_ge(lat_dve, 1)
                for t in range(TT):
                    for i in range(2):
                        pe.transpose(psum[:, 0, i * T + t * P:i * T + (t + 1) * P],
                                     big_n(O_CQ, 256)[:, t, i * P:(i + 1) * P], ident)
                    last = pe.transpose(psum[:, 1, t * P:(t + 1) * P], big_n(O_CKV, P)[:, t, :], ident)
                last.then_inc(lat_pe, 1)
                pe.wait_ge(lat_dve, 2)
                n = PIECE0[s]
                piece_in(n)
                w = slot(n, (2, 768))
                for t in range(TT):
                    for lo, hi in ((0, 512), (512, 768)):
                        for i in range(2):
                            last = mm(psum[:, 2 + 2 * t + lo // 512, 0:hi - lo], xT[:, i, t * P:(t + 1) * P],
                                      w[:, i, lo:hi], i == 0, i == 1)
                last.then_inc(piece_used, 1)
                piece_in(n + 1)
                w = slot(n + 1, (1, 1024))
                for t in range(TT):
                    for half in range(2):
                        last = mm(psum[:, (6, 0)[t] + half, :], xT[:, 2, t * P:(t + 1) * P],
                                  w[:, 0, half * 512:(half + 1) * 512], True, True)
                last.then_inc(piece_used, 1)
                pe.wait_ge(lat_act, 3)
                pe.wait_ge(lat_dve, 3)
                for h in range(MH):
                    for t in range(TT):
                        at = (h % 2) * T + t * P
                        pe.transpose(psum[:, 2 + h // 2, at:at + P], qm[:, t, h, 0:P], ident)
                        pe.transpose(psum[:, 4 + h // 2, at:at + P], vmla[:, t, h, 0:P], ident)
                        last = pe.transpose(psum[0:64, 6 + h // 2, at:at + P], qm[:, t, h, P:P + 64], ident)
                for t in range(TT):
                    last = pe.transpose(psum[0:64, 0, t * P:(t + 1) * P], big_n(O_KR, 64)[:, t, :], ident)
                last.then_inc(lat_pe, 1)

            def router(s, k):
                for t in range(TT):
                    for kt in range(KT):
                        last = mm(psum[:, 0, E * t:E * t + E], xT[:, kt, t * P:(t + 1) * P],
                                  small[:, S_RW + E * kt:S_RW + E * kt + E], kt == 0, kt == KT - 1)
                last.then_inc(route_pe, 1)
                pe.wait_ge(route_dve, 2 * k + 1)
                for t in range(TT):
                    last = pe.transpose(psum[0:E, 1, t * P:(t + 1) * P], route[:, E * t:E * t + E], ident)
                last.then_inc(route_pe, 1)
                pe.wait_ge(route_dve, 2 * k + 2)
                for e in range(E):
                    last = mm(psum[:, e // 2, (e % 2) * T:(e % 2 + 1) * T], spread(ident[0:E, e], 1, P),
                              route[0:E, 1024:1024 + T], True, True)
                last.then_inc(route_pe, 1)

            fns = {"setup": setup, "turn": turn, "ffn": ffn, "project": project, "outproj": outproj,
                   "stick": stick, "soft": soft_attention, "gates": gates, "mlstm": mlstm, "ada": ada,
                   "compress": compress, "cmp": cmp_attention, "latent": latent, "router": router}
            for s, (name, args, _) in enumerate(STAGES):
                if name in fns:
                    fns[name](s, INSTANCE[s], *args)
                boundary(pe, s + 1)

        @block.scalar
        def _(act):
            steps = [0]

            def link(ins):
                steps[0] += 1
                ins.then_inc(act_step, 1)
                act.wait_ge(act_step, steps[0])

            def root_mean(ss, n):
                return act.activation(ss, ss, ACT.Sqrt, scale=1.0 / n, bias=const[:, C_EPS:C_EPS + 1])

            def setup(s, k):
                act.wait_ge(setup_dve, 1)
                act.activation(small[:, S_R:S_R + 8], small[:, S_R:S_R + 8], ACT.Silu).then_inc(setup_act, 1)
                act.wait_ge(rows_ready, 1)
                for i in range(3):
                    act.dma_start(rowbuf[i], spread(wide[0:8, 0, i, :], 1, P)).then_inc(rows_out, 16)
                act.wait_ge(setup_dve, 2)
                act.activation(wide_at(3840, 2048), wide_at(3840, 2048), ACT.Exp).then_inc(setup_act, 1)
                act.wait_ge(rows_out, 48)

            def norm(s, k, m):
                for t in range(TT):
                    link(act.activation(nrm[:, t, :], x[:, t, :], ACT.Square, accum_out=stat[:, t:t + 1]))
                    root_mean(stat[:, t:t + 1], D).then_inc(squared, 1)

            def turn(s, k):
                for q in (0, 2):
                    act.wait_ge(turned, 4 * k + q + 1)
                    act.activation(xT[:, 0:4, (q // 2) * P:(q // 2 + 1) * P],
                                   psum[:, q, :].rearrange("p (a b) -> p a b", a=4), ACT.Copy)

            def ffn(s, k, chunks, moe):
                n0 = PIECE0[s]

                def silu_of_gate(c, i=None):
                    v = chunk_piece(n0, "g", c, chunks) + 1
                    act.wait_ge(piece_used, v if i is None else i * 6 + v)
                    if c >= 2:
                        v = chunk_piece(n0, "d", c - 2, chunks) + 1
                        act.wait_ge(piece_used, v if i is None else i * 6 + v)
                    act.activation(hT[c % 2][:, :, :], psum[:, GB + c % 2, :].rearrange("p (f t) -> p f t", f=2),
                                   ACT.Silu).then_inc(gated, 1)

                silu_of_gate(0)
                silu_of_gate(1)
                pairs = (chunks - 2) // 2
                with act.Fori(0, pairs) as i:
                    silu_of_gate(2, i)
                    silu_of_gate(3, i)
                for c in range(2 + 2 * pairs, chunks):
                    silu_of_gate(c)

            def project(s, k, name):
                for j, pieces in enumerate(PROJ[name]):
                    act.wait_ge(piece_used, PIECE0[s] + j + 1)
                    b, at = 2 * (j % 2), 0
                    for kind, c, m, dst, scale in pieces:
                        if kind == "N":
                            src = psum[:, b, at:at + TT * m].rearrange("p (t w) -> p t w", t=TT)
                            at += TT * m
                        elif kind == "V":
                            src = psum[:, b, 0:512].rearrange("p (t h w) -> p t h w", t=TT, h=2)
                        elif kind == "TT":
                            src = psum[:, b, 0:512]
                        elif kind == "T":
                            src = psum[0:m, b, at:at + T]
                            at += T
                        else:
                            src = psum[64 * c:64 * c + 64, b:b + 2, :].rearrange("p b w -> p (b w)")
                        last = act.activation(dst, src, ACT.Copy, scale=scale)
                    last.then_inc(proj_read, 1)

            def residual(s, k, kind, coef):
                if kind == "norm":
                    for t in range(TT):
                        link(act.activation(nrm[:, t, :], psum[:, 2 * t:2 * t + 2, :].rearrange("p b w -> p (b w)"),
                                            ACT.Square, accum_out=stat[:, t:t + 1]))
                        root_mean(stat[:, t:t + 1], D).then_inc(squared, 1)

            def stick(s, k):
                for h in range(H):
                    act.wait_ge(stick_dve, h + 1)
                    link(act.activation(wide[:, 1, h, :], wide[:, 0, h, :], ACT.Abs))
                    link(act.activation(wide[:, 1, h, :], wide[:, 1, h, :], ACT.Exp, scale=-1.0))
                for h in range(H):
                    act.activation(wide[:, 1, h, :], wide[:, 1, h, :], ACT.Ln, bias=ones).then_inc(stick_act, 1)
                for h in range(H):
                    act.wait_ge(stick_dve, 4 * H + h + 1)
                    act.activation(wide[:, 0, h, :], wide[:, 0, h, :], ACT.Exp).then_inc(stick_act, 1)
                act.wait_ge(stick_pe, 2 * H + 1)
                for t in range(TT):
                    act.activation(nrm[:, t, 0:512], psum[:, 4 + t, :], ACT.Copy)

            def soft_attention(s, k, name):
                a = SOFT[name]
                for h in range(a["heads"]):
                    act.wait_ge(biased, a["step0"] + a["steps"] * (h + 1))
                    for t, (lo, hi) in enumerate(((0, P), (P, W3))):
                        i = 2 * h + t
                        act.activation(wide[:, 0, h, lo:hi], wide[:, 0, h, lo:hi], ACT.Exp,
                                       bias=small[:, S_NMX + i:S_NMX + i + 1],
                                       accum_out=small[:, S_SUM + i:S_SUM + i + 1]).then_inc(expd, 1)
                if a["pad"] is not None:
                    act.wait_ge(pad_dve, PADDED.index(name) + 1)
                    act.activation(small[:, S_R:S_R + 16], small[:, S_R:S_R + 16], ACT.Exp).then_inc(pad_act, 1)

            def gates(s, k):
                act.wait_ge(gates_dve, 2)
                link(act.activation(aux[0:8, A_L:A_L + T], aux[0:8, A_F:A_F + T], ACT.Abs))
                link(act.activation(aux[0:8, A_L:A_L + T], aux[0:8, A_L:A_L + T], ACT.Exp, scale=-1.0))
                act.activation(aux[0:8, A_L:A_L + T], aux[0:8, A_L:A_L + T], ACT.Ln, bias=ones[0:8, :])\
                    .then_inc(gates_act, 1)
                act.wait_ge(gates_dve, 8)
                act.activation(aux[0:8, A_F:A_F + T], aux[0:8, A_F:A_F + T], ACT.Exp, scale=-1.0)\
                    .then_inc(gates_act, 1)
                for j in range(4):
                    act.wait_ge(gates_dve, 8 + 48 + 4 * (j + 1))
                    act.activation(wide_flat[:, 1024 * j:1024 * (j + 1)], wide_flat[:, 1024 * j:1024 * (j + 1)],
                                   ACT.Silu)
                act.activation(mod[:, 0:2048], mod[:, 0:2048], ACT.Sigmoid)

            def mlstm(s, k):
                def outputs(h):
                    act.wait_ge(ml_pe, 3 * h + 5 if h < H - 1 else 3 * H)
                    act.activation(raw[:, :, h, :], psum[:, 4 + h % 2, 0:2 * VW].rearrange("p (t w) -> p t w", t=TT),
                                   ACT.Copy).then_inc(ml_act, 1)

                for h in range(H):
                    act.wait_ge(ml_dve, 4 * h + 2)
                    act.activation(mE[h % 2], mE[h % 2], ACT.Exp, scale=-1.0).then_inc(ml_act, 1)
                    if h >= 1:
                        outputs(h - 1)
                outputs(H - 1)
                act.wait_ge(ml_dve, 4 * H + 1)
                root_mean(small[:, S_DEN:S_DEN + 16], P).then_inc(ml_act, 1)

            def compress(s, k):
                act.wait_ge(piece_used, PIECE0[s] + 4)
                act.activation(big[0:30, N_U:N_U + 512].rearrange("p (a b) -> p a b", a=2), psum[0:30, 1:3, 0:256],
                               ACT.Gelu_apprx_tanh).then_inc(comp_act, 1)

            def cmp_attention(s, k):
                act.activation(gview(S_G), gview(S_G), ACT.Sigmoid).then_inc(cmp_act, 1)
                act.wait_ge(cmp_dve, 1)
                act.activation(cS, cS, ACT.Exp).then_inc(cmp_act, 1)
                act.wait_ge(cmp_pe, 2)
                act.activation(cPT[0:NCMP, :], psum[0:NCMP, 1:5, :].rearrange("p b w -> p (b w)"), ACT.Copy)\
                    .then_inc(cmp_act, 1)

            def latent(s, k):
                for t in range(TT):
                    act.activation(nrm[:, t, 0:256], big_n(O_CQ, 256)[:, t, :], ACT.Square,
                                   accum_out=stat[:, t:t + 1])
                    last = act.activation(nrm[:, t, 256:384], big_n(O_CKV, P)[:, t, :], ACT.Square,
                                          accum_out=stat[:, 2 + t:3 + t])
                link(last)
                root_mean(stat[:, 0:2], 256)
                root_mean(stat[:, 2:4], P).then_inc(lat_act, 1)
                n = PIECE0[s]
                act.wait_ge(piece_used, n + 1)
                for t in range(TT):
                    last = act.activation(qm[:, t, :, :], psum[:, 2 + 2 * t:4 + 2 * t, :]
                                          .rearrange("p b w -> p (b w)")[:, 0:768].rearrange("p (h w) -> p h w", h=MH),
                                          ACT.Copy)
                last.then_inc(lat_act, 1)
                act.wait_ge(piece_used, n + 2)
                for t in range(TT):
                    b = (6, 0)[t]
                    last = act.activation(big_n(O_KVM, 1024)[:, t, :],
                                          psum[:, b:b + 2, :].rearrange("p b w -> p (b w)"), ACT.Copy)
                last.then_inc(lat_act, 1)
                act.wait_ge(lat_pe, 2)
                act.activation(big[:, O_QNT:O_QNT + 1024], psum[:, 2:4, :].rearrange("p b w -> p (b w)"), ACT.Copy)
                act.activation(big[:, O_KNT:O_KNT + 1024], psum[:, 4:6, :].rearrange("p b w -> p (b w)"), ACT.Copy)

            def router(s, k):
                act.wait_ge(route_pe, 3 * k + 1)
                act.activation(route[:, 0:2 * E], psum[:, 0, 0:2 * E], ACT.Sigmoid).then_inc(route_act, 1)
                act.wait_ge(route_pe, 3 * k + 3)
                act.activation(big[:, 0:2048], psum[:, 0:4, :].rearrange("p b w -> p (b w)"), ACT.Copy)

            def final(s, k):
                norm(s, k, None)

            ones = const[:, C_ONES:C_ONES + 1]
            fns = {"setup": setup, "norm": norm, "turn": turn, "ffn": ffn, "project": project,
                   "residual": residual, "stick": stick, "soft": soft_attention, "gates": gates,
                   "mlstm": mlstm, "compress": compress, "cmp": cmp_attention, "latent": latent,
                   "router": router, "final": final}
            for s, (name, args, _) in enumerate(STAGES):
                if name in fns:
                    fns[name](s, INSTANCE[s], *args)
                boundary(act, s + 1)
            act.dma_start(out.rearrange("(t p) d -> p t d", p=P), nrm[:, :, :]).then_inc(out_done, 16)
            act.wait_ge(out_done, 16)

        @block.vector
        def _(dve):
            steps = [0]

            def link(ins):
                steps[0] += 1
                ins.then_inc(dve_step, 1)
                dve.wait_ge(dve_step, steps[0])

            def mark(ins, signal, value):
                ins.then_inc(signal, 1)
                dve.wait_ge(signal, value)

            def tt(out_, a, b, op):
                return dve.tensor_tensor(out_, a, b, op)

            def setup(s, k):
                dve.wait_ge(setup_pe, 1)
                c = small[:, S_R:S_R + 8]
                dve.tensor_copy(c, psum[:, 0, 0:8]).then_inc(setup_dve, 1)
                dil, rel, swa = (big[0:8, (2 + i) * W3:(3 + i) * W3] for i in range(3))
                tt(wide[0:8, 0, 0, :], psum[0:8, 1, 0:W3], dil, ALU.add)
                tt(wide[0:8, 0, 1, :], psum[0:8, 2, 0:W3], rel, ALU.add)
                tt(wide[0:8, 0, 2, :], psum[0:8, 2, 0:W3], swa, ALU.add).then_inc(rows_ready, 1)
                dve.wait_ge(setup_act, 1)
                dve.tensor_copy(cB[:, :, :], spread(c, 2, P))
                link(dve.tensor_copy(pad_b[0], psum[0:8, 3, :]))
                link(tt(pad_b[1], psum[0:8, 3, :], big[0:8, R_PADMASK:R_PADMASK + 512], ALU.add))
                sink = aux[0:8, 144:145]
                dve.memset(pad_m[0][:, 0:1], NEG)
                link(dve.tensor_copy(pad_m[1][:, 0:1], sink))
                for b, m, first in zip(pad_b, pad_m, (NEG, sink)):
                    link(dve.tensor_tensor_scan(m[:, 1:513], b, b, first, ALU.max, ALU.max))
                for i in range(2):
                    tt(pad_a[i], pad_m[i][:, 0:512], pad_m[i][:, 1:513], ALU.subtract)
                    ins = tt(pad_e[i], pad_b[i], pad_m[i][:, 1:513], ALU.subtract)
                ins.then_inc(setup_dve, 1)
                dve.wait_ge(setup_act, 2)
                for i in range(2):
                    ins = dve.tensor_tensor_scan(pad_b[i], pad_a[i], pad_e[i], float(i), ALU.mult, ALU.add)
                ins.then_inc(setup_dve, 1)
                dve.wait_ge(setup_pe, 2)
                mark(dve.tensor_copy(small[:, S_PAD:S_PAD + 64], psum[:, 4, 0:64]), setup_dve, 4)
                dve.wait_ge(setup_pe, 3)
                link(dve.tensor_copy(small[:, S_PAD:S_PAD + 64], psum[:, 5, 0:64]))
                for i in range(2):
                    m = small[:, S_PAD + 32 * i:S_PAD + 32 * i + 16]
                    dve.tensor_scalar(m, m, -1.0, None, ALU.mult)

            def norm(s, k, m):
                g = GAIN0[s]
                wait_gain(dve, g)
                for t in range(TT):
                    dve.wait_ge(squared, SQ0[s] + t + 1)
                    link(dve.reciprocal(stat[:, t:t + 1], stat[:, t:t + 1]))
                    ins = dve.scalar_tensor_tensor(out=nrm[:, t, :], in0=x[:, t, :], scalar=stat[:, t:t + 1],
                                                   in1=gain[g % 2][:, :], op0=ALU.mult, op1=ALU.mult)
                    if t == TT - 1:
                        mark(ins, gain_used, g + 1)
                    else:
                        link(ins)
                    if m is not None:
                        link(dve.scalar_tensor_tensor(out=nrm[:, t, :], in0=mod[:, (m + 1) * D:(m + 2) * D], scalar=1.0,
                                                      in1=nrm[:, t, :], op0=ALU.add, op1=ALU.mult))
                        link(tt(nrm[:, t, :], nrm[:, t, :], mod[:, m * D:(m + 1) * D], ALU.add))

            def turn(s, k):
                for q in (1, 3):
                    dve.wait_ge(turned, 4 * k + q + 1)
                    dve.tensor_copy(xT[:, 4:8, (q // 2) * P:(q // 2 + 1) * P],
                                    psum[:, q, :].rearrange("p (a b) -> p a b", a=4))

            def ffn(s, k, chunks, moe):
                n0 = PIECE0[s]
                c0, h0 = ffn_bases(k)
                n = 2 if moe else 1

                def hidden_features(c, i=None, e=None):
                    def at(v, per_pair):
                        return v if i is None else i * per_pair + v

                    h = hT[c % 2]
                    up = psum[:, UB + c % 2, :].rearrange("p (f t) -> p f t", f=2)
                    dve.wait_ge(gated, at(c0 + c + 1, 2))
                    dve.wait_ge(piece_used, at(chunk_piece(n0, "u", c, chunks) + 1, 6))
                    tt(h[:, :, :], h[:, :, :], up, ALU.mult).then_inc(hidden, 1)
                    if moe:
                        dve.wait_ge(hidden, at(h0 + n * c + 1, 2 * n))
                        tt(h[:, :, :], h[:, :, :], spread(routing[:, e, :], 1, 2), ALU.mult).then_inc(hidden, 1)

                hidden_features(0, None, 0)
                hidden_features(1, None, 0)
                pairs = (chunks - 2) // 2
                with dve.Fori(0, pairs) as i:
                    hidden_features(2, i, i + 1)
                    hidden_features(3, i, i + 1)
                for c in range(2 + 2 * pairs, chunks):
                    hidden_features(c, None, c // EC if moe else None)

            def residual(s, k, kind, coef):
                dve.wait_ge(piece_used, PIECE0[s])
                for t in range(TT):
                    y = psum[:, 2 * t:2 * t + 2, :].rearrange("p b w -> p (b w)")
                    if kind == "norm":
                        g = GAIN0[s]
                        if t == 0:
                            wait_gain(dve, g)
                        dve.wait_ge(squared, SQ0[s] + t + 1)
                        link(dve.reciprocal(stat[:, t:t + 1], stat[:, t:t + 1]))
                        ins = dve.scalar_tensor_tensor(out=nrm[:, t, :], in0=y, scalar=stat[:, t:t + 1],
                                                       in1=gain[g % 2][:, :], op0=ALU.mult, op1=ALU.mult)
                        if t == TT - 1:
                            mark(ins, gain_used, g + 1)
                        else:
                            link(ins)
                        dve.scalar_tensor_tensor(out=x[:, t, :], in0=nrm[:, t, :], scalar=coef, in1=x[:, t, :],
                                                 op0=ALU.mult, op1=ALU.add)
                    else:
                        link(tt(nrm[:, t, :], y, mod[:, coef * D:(coef + 1) * D], ALU.mult))
                        tt(x[:, t, :], x[:, t, :], nrm[:, t, :], ALU.add)

            def stick(s, k):
                for h in range(H):
                    dve.wait_ge(stick_pe, h + 1)
                    dve.tensor_copy(wide[:, 0, h, :], psum[:, h % 2, 0:W3]).then_inc(stick_dve, 1)
                for h in range(H):
                    z, sp_h = wide[:, 0, h, :], wide[:, 1, h, :]
                    at = H + 3 * h
                    dve.wait_ge(stick_act, h + 1)
                    mark(dve.scalar_tensor_tensor(out=sp_h, in0=z, scalar=0.0, in1=sp_h, op0=ALU.max, op1=ALU.add),
                         stick_dve, at + 1)
                    mark(tt(z, z, sp_h, ALU.subtract), stick_dve, at + 2)
                    mark(tt(sp_h, sp_h, const[:, C_MSTRICT:C_MSTRICT + W3], ALU.mult), stick_dve, at + 3)
                for h in range(H):
                    dve.wait_ge(stick_pe, H + h + 1)
                    tt(wide[:, 0, h, :], wide[:, 0, h, :], psum[:, 2 + h % 2, 0:W3], ALU.subtract)\
                        .then_inc(stick_dve, 1)
                for h in range(H):
                    dve.wait_ge(stick_act, H + h + 1)
                    tt(wide[:, 0, h, :], wide[:, 0, h, :], const[:, C_MSTRICT:C_MSTRICT + W3], ALU.mult)\
                        .then_inc(stick_dve, 1)

            def soft_attention(s, k, name):
                a = SOFT[name]
                h0, s0, n, heads, dv = a["head0"], a["step0"], a["steps"], a["heads"], a["dv"]
                if a["bias"]:
                    dve.wait_ge(bias_in, {"dilated": 32, "sliding": 96}.get(name, 64))

                def scores(h):
                    S, at = wide[:, 0, h, :], s0 + n * h
                    add = biasT[:, h, :] if a["bias"] else const[:, C_CAUSAL:C_CAUSAL + W3]
                    dve.wait_ge(score, h0 + h + 1)
                    mark(dve.scalar_tensor_tensor(out=S, in0=psum[:, h % 2, 0:W3], scalar=a["scale"], in1=add,
                                                  op0=ALU.mult, op1=ALU.add), biased, at + 1)
                    for t, (lo, hi) in enumerate(((0, P), (P, W3))):
                        i = S_NMX + 2 * h + t
                        mark(dve.tensor_reduce(small[:, i:i + 1], S[:, lo:hi], AX.X, ALU.max, negate=True),
                             biased, at + 2 + t)
                    if a["pad"] is not None:
                        for t in range(TT):
                            i, m = S_NMX + 2 * h + t, a["pad"] + 8 * t + h
                            mark(tt(small[:, i:i + 1], small[:, i:i + 1], small[:, m:m + 1], ALU.min), biased, at + 4 + t)

                def probs(h):
                    dve.wait_ge(p_turned, h0 + h + 1)
                    if h >= 2:
                        dve.wait_ge(headout, h0 + h - 1)
                    dve.tensor_copy(PT[h % 2][:, :], psum[:, 2 + h % 2, 0:W3]).then_inc(p_read, 1)

                scores(0)
                scores(1)
                for h in range(heads):
                    if h + 2 < heads:
                        scores(h + 2)
                    probs(h)
                dve.wait_ge(expd, 2 * (h0 + heads))
                cols_ = 2 * heads
                sums = small[:, S_SUM:S_SUM + cols_].rearrange("p (h t) -> p h t", t=TT)
                inv = small[:, S_INV:S_INV + cols_].rearrange("p (h t) -> p h t", t=TT)
                nmx = small[:, S_NMX:S_NMX + cols_].rearrange("p (h t) -> p h t", t=TT)
                tmp = small[:, S_R:S_R + 16].rearrange("p (h t) -> p h t", t=TT)
                if a["pad"] is not None:
                    m, total = (small[:, c:c + 16].rearrange("p (t h) -> p h t", t=TT) for c in (a["pad"], a["pad"] + 16))
                    n_pad = PADDED.index(name) + 1
                    tt(tmp, nmx, m, ALU.subtract).then_inc(pad_dve, 1)
                    dve.wait_ge(pad_act, n_pad)
                    link(tt(tmp, tmp, total, ALU.mult))
                    link(tt(sums, sums, tmp, ALU.add))
                link(dve.reciprocal(inv, sums))
                if a["gate"] is not None:
                    link(tt(inv, inv, gate_of(a["gate"]), ALU.mult))
                dve.wait_ge(headout, h0 + heads)
                for t in range(TT):
                    y = psum[:, 4 + t, :].rearrange("p (h w) -> p h w", h=heads)
                    o = nrm[:, t, a["dst"]:a["dst"] + 512].rearrange("p (h w) -> p h w", h=heads)
                    f = spread(inv[:, :, t], 2, dv)
                    if a["gate"] is None:
                        tt(o, y, f, ALU.mult)
                    else:
                        part = wide_flat[:, 3072 + 512 * t:3584 + 512 * t].rearrange("p (h w) -> p h w", h=heads)
                        link(tt(part, y, f, ALU.mult))
                        tt(o, o, part, ALU.add)

            def gate_of(c):
                return gview(S_G).rearrange("p t (h c) -> p h t c", c=3)[:, :, :, c]

            def gates(s, k):
                I_, F_, L_, B_, G_ = (aux[0:8, at:at + T] for at in (A_I, A_F, A_L, A_B, A_G))
                dve.memset(vM[:, :, :, P:VW], 1.0)
                dve.wait_ge(gates_pe, 1)
                mark(dve.tensor_copy(small[:, S_CONVW:S_CONVW + 64], psum[:, 0, 0:64]), gates_dve, 1)
                mark(dve.tensor_scalar(F_, F_, aux[0:8, 1:2], None, ALU.add), gates_dve, 2)
                dve.wait_ge(gates_act, 1)
                mark(dve.tensor_scalar(F_, F_, 0.0, None, ALU.min), gates_dve, 3)
                mark(tt(F_, F_, L_, ALU.subtract), gates_dve, 4)
                mark(dve.tensor_tensor_scan(B_, const[0:8, C_ONES:C_ONES + 1].to_broadcast([8, T]), F_, 0.0,
                                            ALU.mult, ALU.add), gates_dve, 5)
                mark(dve.scalar_tensor_tensor(out=G_, in0=I_, scalar=aux[0:8, 0:1], in1=B_, op0=ALU.add,
                                              op1=ALU.subtract), gates_dve, 6)
                mark(dve.tensor_tensor_scan(L_, G_, G_, 0.0, ALU.max, ALU.max), gates_dve, 7)
                mark(tt(F_, B_, L_, ALU.add), gates_dve, 8)
                for tap in range(4):
                    for m in range(16):
                        w = small[:, S_CONVW + 16 * (3 - tap) + m:S_CONVW + 16 * (3 - tap) + m + 1]
                        src = big_t(M_PRE, m)
                        if tap:
                            dve.wait_ge(gates_dve, 8 + 16 * (tap - 1) + m + 1)
                            dve.scalar_tensor_tensor(out=cv[:, m, tap:T], in0=src[:, 0:T - tap], scalar=w,
                                                     in1=cv[:, m, tap:T], op0=ALU.mult, op1=ALU.add)\
                                .then_inc(gates_dve, 1)
                        else:
                            dve.tensor_scalar(cv[:, m, :], src, w, None, ALU.mult).then_inc(gates_dve, 1)
                dve.wait_ge(gates_pe, 2)
                dve.tensor_copy(small[:, S_COL:S_COL + 32], psum[:, 1, 0:32])

            def mlstm(s, k):
                scale = 1.0 / math.sqrt(P)
                for h in range(H):
                    e = mE[h % 2]
                    col = [small[:, S_COL + 8 * t + h:S_COL + 8 * t + h + 1] for t in range(TT)]
                    dve.wait_ge(ml_pe, 3 * h if h else 1)
                    dve.tensor_scalar(e[:, 0:T], psum[:, h % 2, 0:T], col[0], 0.0, ALU.subtract, ALU.max)\
                        .then_inc(ml_dve, 1)
                    dve.tensor_scalar(e[:, T:W3], psum[:, h % 2, P:T], col[1], 0.0, ALU.subtract, ALU.max)\
                        .then_inc(ml_dve, 1)
                    dve.wait_ge(ml_act, 2 * h if h else 1)
                    mark(tt(e, e, const[:, C_MINCL:C_MINCL + W3], ALU.mult), ml_dve, 4 * h + 3)
                    dve.wait_ge(ml_pe, 3 * h + 1 if h else 2)
                    if h >= 2:
                        dve.wait_ge(ml_pe, 3 * (h - 2) + 5)
                    dve.scalar_tensor_tensor(out=PT[h % 2][:, :], in0=psum[:, 2 + h % 2, 0:W3], scalar=scale, in1=e,
                                             op0=ALU.mult, op1=ALU.mult).then_inc(ml_dve, 1)
                dve.wait_ge(ml_act, 2 * H)
                den = small[:, S_DEN:S_DEN + 16].rearrange("p (t h) -> p t h", t=TT)
                thr = small[:, S_THR:S_THR + 16].rearrange("p (t h) -> p t h", t=TT)
                n_num = raw[:, :, :, P]
                link(dve.scalar_tensor_tensor(out=den, in0=n_num, scalar=-1.0, in1=n_num, op0=ALU.mult, op1=ALU.max))
                link(tt(den, den, thr, ALU.max))
                link(dve.reciprocal(den, den))
                sq = wide_flat[:, 0:2048].rearrange("p (t h w) -> p t h w", t=TT, h=H)
                g = GAIN0[s]
                wait_gain(dve, g)
                for t in range(TT):
                    link(tt(hid[:, t], raw[:, t, :, 0:P], spread(den[:, t, :], 2, P), ALU.mult))
                for t in range(TT):
                    link(tt(sq[:, t], hid[:, t], hid[:, t], ALU.mult))
                dve.tensor_reduce(den[:, 0, :], sq[:, 0], AX.X, ALU.add)
                dve.tensor_reduce(den[:, 1, :], sq[:, 1], AX.X, ALU.add).then_inc(ml_dve, 1)
                dve.wait_ge(ml_act, 2 * H + 1)
                link(dve.reciprocal(den, den))
                for t in range(TT):
                    link(tt(hid[:, t], hid[:, t], spread(den[:, t, :], 2, P), ALU.mult))
                for t in range(TT):
                    ins = tt(nrm[:, t, :], nrm[:, t, :], gain[g % 2][:, :], ALU.mult)
                    if t == TT - 1:
                        mark(ins, gain_used, g + 1)
                    else:
                        link(ins)
                tt(nrm[:, :, :], nrm[:, :, :], oM, ALU.mult)

            def ada(s, k):
                n0 = PIECE0[s]
                for _ in range(2):
                    dve.nop().then_inc(ada_read, 1)
                dve.wait_ge(mod_in, 16 * (k + 1))
                with dve.Fori(0, 4) as i:
                    for r in range(RING):
                        dve.wait_ge(piece_used, i * 6 + (n0 + r + 1))
                        m = mod[:, bass.ds(i * (RING * 256) + r * 256, 256)]
                        tt(m, m, psum[:, r % 2, 0:256], ALU.add).then_inc(ada_read, 1)

            def compress(s, k):
                pos = big[:, N_POS:N_POS + 64]
                dve.wait_ge(comp_pe, 1)
                mark(dve.tensor_copy(pos, psum[:, 0, 0:64]), comp_dve, 1)
                for i, at in enumerate((N_KC, N_VC)):
                    for v in range(2):
                        for odd in range(2):
                            p0 = 64 * v
                            part = big[p0:p0 + 64, at + odd:at + odd + 1]
                            tokens = bass.AP(part.tensor, part.offset, [list(part.ap[0]), [2, 16], [16, NCMP]])
                            place = pos[p0:p0 + 64, 32 * i + odd:32 * i + 32:2]
                            tt(blocksF[i][64 * odd:64 * odd + 64, :, v, :], tokens, spread(place, 2, NCMP), ALU.add)\
                                .then_inc(comp_dve, 1)
                dve.wait_ge(comp_pe, 2)
                mark(dve.tensor_copy(big[:, N_GT:N_GT + 120], psum[:, 3, 0:120]), comp_dve, 10)
                dve.wait_ge(comp_pe, 3)
                dve.tensor_copy(big[:, N_KCMP:N_KCMP + NCMP], psum[:, 4, 0:NCMP])
                dve.tensor_copy(big[0:NCMP, N_VCMP:N_VCMP + P], psum[0:NCMP, 5, 0:P])

            def cmp_attention(s, k):
                dve.wait_ge(bias_in, 64)
                link(dve.memset(cS, NEG))
                dve.wait_ge(cmp_pe, 1)
                for v in range(2):
                    g = slice(4 * v, 4 * v + 4)
                    ps = psum[:, (0, 7)[v], 0:256].rearrange("p (h t n) -> p h t n", h=H, t=TT)
                    for t, n in ((0, 7), (1, NCMP)):
                        lo = P * t + 31
                        link(tt(cS[:, g, t, 0:n], ps[:, g, t, 0:n], biasT[:, g, lo:lo + 16 * (n - 1) + 1:16],
                                ALU.add))
                mx = small[:, S_NMX:S_NMX + 16].rearrange("p (h t) -> p h t", t=TT)
                sums = small[:, S_SUM:S_SUM + 16].rearrange("p (h t) -> p h t", t=TT)
                inv = small[:, S_INV:S_INV + 16].rearrange("p (h t) -> p h t", t=TT)
                link(dve.tensor_reduce(mx, cS, AX.X, ALU.max))
                link(dve.tensor_scalar(mx, mx, -1e20, None, ALU.max))
                for t in range(TT):
                    ins = tt(cS[:, :, t, :], cS[:, :, t, :], spread(mx[:, :, t], 2, 16), ALU.subtract)
                ins.then_inc(cmp_dve, 1)
                dve.wait_ge(cmp_act, 2)
                link(dve.tensor_reduce(sums, cS, AX.X, ALU.add))
                link(dve.tensor_scalar(sums, sums, 1e-30, None, ALU.max))
                link(dve.reciprocal(inv, sums))
                link(tt(inv, inv, gate_of(0), ALU.mult))
                dve.wait_ge(cmp_pe, 3)
                for t in range(TT):
                    tt(nrm[:, t, 0:512].rearrange("p (h w) -> p h w", h=H),
                       psum[:, 5 + t, :].rearrange("p (h w) -> p h w", h=H), spread(inv[:, :, t], 2, 64), ALU.mult)

            def rope(x_, t, tmp):
                heads = x_.shape[1] if len(x_.shape) == 3 else 0
                cos = const[:, C_COS + 32 * t:C_COS + 32 * t + 32]
                sin = const[:, C_SIN + 32 * t:C_SIN + 32 * t + 32]
                if heads:
                    cos, sin = spread(cos, 1, heads), spread(sin, 1, heads)
                    x1, x2 = x_[:, :, 0:32], x_[:, :, 32:64]
                else:
                    x1, x2 = x_[:, 0:32], x_[:, 32:64]
                tt(tmp[0], x1, cos, ALU.mult)
                tt(tmp[1], x2, sin, ALU.mult)
                tt(tmp[2], x1, sin, ALU.mult)
                link(tt(tmp[3], x2, cos, ALU.mult))
                tt(x1, tmp[0], tmp[1], ALU.subtract)
                return tt(x2, tmp[2], tmp[3], ALU.add)

            def latent(s, k):
                dve.wait_ge(lat_act, 1)
                link(dve.reciprocal(stat[:, 0:4], stat[:, 0:4]))
                dve.wait_ge(extra_in, EXTRA["odd"])
                for t in range(TT):
                    cq, ckv = big_n(O_CQ, 256)[:, t, :], big_n(O_CKV, P)[:, t, :]
                    dve.scalar_tensor_tensor(out=cq, in0=cq, scalar=stat[:, t:t + 1], in1=aux[:, 0:256],
                                             op0=ALU.mult, op1=ALU.mult)
                    ins = dve.scalar_tensor_tensor(out=ckv, in0=ckv, scalar=stat[:, 2 + t:3 + t], in1=aux[:, 256:384],
                                                   op0=ALU.mult, op1=ALU.mult)
                ins.then_inc(lat_dve, 1)
                dve.wait_ge(lat_pe, 1)
                dve.tensor_copy(xT[:, 0:2, :], psum[:, 0, :].rearrange("p (a b) -> p a b", a=2))
                dve.tensor_copy(xT[:, 2, :], psum[:, 1, 0:T]).then_inc(lat_dve, 1)
                for t in range(TT):
                    tmp = [hT[i // 2][:, i % 2, 32 * t:32 * t + 32] for i in range(4)]
                    last = rope(big_n(O_KR, 64)[:, t, :], t, tmp)
                link(last)
                dve.wait_ge(lat_act, 2)
                for t in range(TT):
                    tmp = [hT[t][:, i // 2, P * (i % 2):P * (i % 2) + P].rearrange("p (h w) -> p h w", h=MH)
                           for i in range(4)]
                    ins = rope(qm[:, t, :, P:P + 64], t, tmp)
                ins.then_inc(lat_dve, 1)
                dve.wait_ge(lat_pe, 2)
                dve.tensor_copy(aux[0:64, A_QRT:A_QRT + 1024], psum[0:64, 6:8, :].rearrange("p b w -> p (b w)"))
                dve.tensor_copy(aux[0:64, A_KRT:A_KRT + T], psum[0:64, 0, 0:T])

            def router(s, k):
                def at(a, *dims):
                    n = int(np.prod(dims))
                    names = "abc"[:len(dims)]
                    return route[:, a:a + n].rearrange(f"p ({' '.join(names)}) -> p {' '.join(names)}",
                                                       **dict(zip(names, dims)))

                aff, biased_ = at(0, 8, 4), at(64, 8, 4)
                gt, eq = at(128, 8, 4, 4), at(256, 8, 4, 4)
                sel, top, rank = at(384, 8, 4), at(448, 8, 4), at(512, 8, 4)
                group, grank = at(576, 2, 4), at(592, 2, 4)
                ggt, geq = at(608, 2, 4, 4), at(640, 2, 4, 4)
                total = at(672, 2)
                lower = const[:, C_LOWER:C_LOWER + 16].rearrange("p (a b) -> p a b", a=4)
                dve.wait_ge(route_act, k + 1)
                rb = small[:, S_RB:S_RB + E].rearrange("p (g e) -> p g e", g=4)
                for t in range(TT):
                    link(tt(biased_[:, 4 * t:4 * t + 4], aff[:, 4 * t:4 * t + 4], rb, ALU.add))

                def ranks(values, n, g_, e_, out_):
                    for j in range(4):
                        other = spread(values[:, :, j], 2, 4)
                        tt(g_[:, :, j, :], values, other, ALU.is_gt)
                        last = tt(e_[:, :, j, :], values, other, ALU.is_equal)
                    link(last)
                    link(tt(e_, e_, spread(lower, 1, n), ALU.mult))
                    link(tt(g_, g_, e_, ALU.add))
                    link(dve.tensor_reduce(out_, g_, AX.X, ALU.add))

                ranks(biased_, 8, gt, eq, rank)
                link(dve.tensor_scalar(sel, rank, 1.5, None, ALU.is_lt))
                link(tt(top, sel, biased_, ALU.mult))
                link(dve.tensor_reduce(group.rearrange("p a b -> p (a b)"), top, AX.X, ALU.add))
                ranks(group, 2, ggt, geq, grank)
                link(dve.tensor_scalar(grank, grank, 0.5, None, ALU.is_lt))
                link(tt(sel, sel, spread(grank.rearrange("p a b -> p (a b)"), 2, 4), ALU.mult))
                link(tt(aff, aff, sel, ALU.mult))
                link(dve.tensor_reduce(total, route[:, 0:32].rearrange("p (t e) -> p t e", t=TT), AX.X, ALU.add))
                link(dve.reciprocal(total, total))
                w = route[:, 0:32].rearrange("p (t e) -> p t e", t=TT)
                tt(w, w, spread(total, 2, E), ALU.mult).then_inc(route_dve, 1)
                dve.wait_ge(route_pe, 3 * k + 2)
                dve.tensor_copy(route[0:E, 1024:1024 + T], psum[0:E, 1, 0:T]).then_inc(route_dve, 1)
                dve.wait_ge(route_pe, 3 * k + 3)
                dve.tensor_copy(big[:, 2048:4096], psum[:, 4:8, :].rearrange("p b w -> p (b w)"))

            def final(s, k):
                norm(s, k, None)

            fns = {"setup": setup, "norm": norm, "turn": turn, "ffn": ffn, "residual": residual, "stick": stick, "soft": soft_attention, "gates": gates,
                   "mlstm": mlstm, "ada": ada, "compress": compress, "cmp": cmp_attention,
                   "latent": latent, "router": router, "final": final}
            for s, (name, args, _) in enumerate(STAGES):
                if name in fns:
                    fns[name](s, INSTANCE[s], *args)
                boundary(dve, s + 1)


_INS = ['x', 'norm_g', 'ffn_w_gate', 'ffn_w_up', 'ffn_w_down', 'attn_w_in', 'attn_w_out', 'rel_bias',
        'mlstm_w_in', 'mlstm_b_gates', 'mlstm_conv_w', 'mlstm_head_g', 'mlstm_w_out', 'c_2', 'rel_table_2',
        'router_w_2', 'router_b_2', 'final_norm_2', 'norm_mix_2', 'norm_ffn_2', 'ada_w_2', 'ada_b_2',
        'moe_w_gate_2', 'moe_w_up_2', 'moe_w_down_2', 'ev_w_in_2', 'ev_w_out_2', 'nsa_pos_k_2', 'nsa_pos_v_2',
        'nsa_ck_w1_2', 'nsa_ck_w2_2', 'nsa_cv_w1_2', 'nsa_cv_w2_2', 'od_w_in_2', 'od_w_out_2', 'mla_q_norm_2',
        'mla_kv_norm_2', 'mla_w_q_up_2', 'mla_w_kv_up_2', 'swa_sinks_2']


def kernel(**inputs):
    import concourse.bacc as _bacc
    from concourse.bass_utils import run_bass_kernel_spmd as _run

    nc = _bacc.Bacc("TRN2", target_bir_lowering=False, num_devices=1)
    arrays = {name: np.ascontiguousarray(inputs[name]) for name in _INS}
    arrays["const"], arrays["rows"] = shape_constants()
    I = {name: nc.dram_tensor(f"in_{name}", a.shape, F32, kind="ExternalInput").ap() for name, a in arrays.items()}
    out = nc.dram_tensor("out_0_dram", (T, D), F32, kind="ExternalOutput").ap()
    build(nc, I, out)
    r = _run(nc, [{f"in_{name}": a for name, a in arrays.items()}], core_ids=[0])
    return r.results[0]["out_0_dram"].reshape(1, T, D)
```

```python
import math
from contextlib import ExitStack

import numpy as np

import concourse.bass as bass
from concourse import mybir

F32 = mybir.dt.float32
F32R = mybir.dt.float32r
ALU = mybir.AluOpType
ACT = mybir.ActivationFunctionType
AX = mybir.AxisListType

P = 128
T = 256
TT = T // P
D = 1024
KT = D // P
DH = 64
H = 8
FF = 2816
FC = FF // 256
E = 16
FE = 512
EC = FE // 256
W3 = 3 * P
NCMP = 15
NEG = -1e30
EPS = 1e-6
RING = 3
PARTS = 3
LOOP = 6
GAINBUFS = 4
SLOT = 2048
MH = 4
VW = P + 1



def bucket_table(max_distance, distances):
    d = np.maximum(distances, 0)
    scaled = np.log(np.maximum(d, 1).astype(np.float32) / np.float32(16)) / np.float32(math.log(max_distance / 16))
    log_part = 16 + (scaled * np.float32(16)).astype(np.int32)
    return np.where(d < 16, d, np.minimum(log_part, 31))


C_IDENT = 0
C_MSTRICT = C_IDENT + P
C_MINCL = C_MSTRICT + W3
C_CAUSAL = C_MINCL + W3
C_AFTER = C_CAUSAL + W3
C_ONES = C_AFTER + P
C_COS = C_ONES + P
C_SIN = C_COS + TT * 32
C_LOWER = C_SIN + TT * 32
C_EPS = C_LOWER + 16
C_FLIP = C_EPS + 1
NCONST = C_FLIP + P


def shape_constants():
    c = np.zeros((P, NCONST), np.float32)
    p, j = np.arange(P)[:, None], np.arange(T)[None, :]
    c[:, C_IDENT:C_IDENT + P] = np.eye(P)
    for at, mask in ((C_MSTRICT, j > p), (C_MINCL, j >= p)):
        c[:, at:at + T] = mask
        c[:, at + T:at + W3] = mask[:, :P]
    c[:, C_CAUSAL:C_CAUSAL + P] = np.where(j[:, :P] <= p, 0, NEG)
    c[:, C_CAUSAL + P:C_CAUSAL + W3] = np.where(j <= p + P, 0, NEG)
    c[:, C_AFTER:C_AFTER + P] = p > j[:, :P]
    c[:, C_ONES:C_ONES + P] = 1
    inv = np.float32(10000.0) ** (-np.arange(0, 64, 2, dtype=np.float32) / np.float32(64))
    angle = (np.arange(T, dtype=np.float32)[:, None] * inv[None, :]).reshape(TT, P, 32).transpose(1, 0, 2)
    c[:, C_COS:C_COS + TT * 32] = np.cos(angle).reshape(P, TT * 32)
    c[:, C_SIN:C_SIN + TT * 32] = np.sin(angle).reshape(P, TT * 32)
    a = np.arange(4)
    c[:, C_LOWER:C_LOWER + 16] = (a[None, :] < a[:, None]).reshape(1, 16)
    c[:, C_EPS] = EPS
    c[:, C_FLIP:C_FLIP + P] = np.eye(P)[::-1]
    d = 255 - np.arange(W3)
    count = (d <= 128) * 1 + (d % 4 == 0) * 1 + (d % 16 == 0) * 1
    count = np.where(d >= 0, count, 0)
    dil = np.where(count > 0, np.log(np.maximum(count, 1)), NEG)
    rel = np.where(d >= 0, 0, NEG)
    swa = np.where((d >= 0) & (d < 128), 0, NEG)
    rows = np.zeros((32, 5, W3), np.float32)
    rows[:, 0] = bucket_table(2048, d)[None, :] == np.arange(32)[:, None]
    rows[:, 1] = bucket_table(1024, d)[None, :] == np.arange(32)[:, None]
    rows[:, 2], rows[:, 3], rows[:, 4] = dil, rel, swa
    d = 511 - np.arange(512)
    pads = np.zeros((32, 2, 512), np.float32)
    pads[:, 0] = bucket_table(1024, d)[None, :] == np.arange(32)[:, None]
    pads[:, 1] = np.where(d < 128, 0, NEG)
    return c, np.concatenate([rows.reshape(32, 5 * W3), pads.reshape(32, 1024)], axis=1)


def spread(ap, axis, n):
    dims = [list(x) for x in ap.ap]
    return bass.AP(ap.tensor, ap.offset, dims[:axis] + [[0, n]] + dims[axis:])


def build(nc, I, out):
    ctx = ExitStack()
    with ctx:
        def sb(name, shape, dt=F32):
            return ctx.enter_context(nc.sbuf_tensor(name, shape, dt))

        def sem(name):
            return ctx.enter_context(nc.semaphore(name))

        ring = [sb(f"ring{i}", [P, SLOT]) for i in range(RING)]
        x = sb("x", [P, TT, D])
        nrm = sb("nrm", [P, TT, D])
        xh = sb("xh", [P, KT, T], F32R)
        xl = sb("xl", [P, KT, T], F32R)
        const = sb("const", [P, NCONST])
        gain = [sb(f"gain{i}", [P, D]) for i in range(GAINBUFS)]
        ccol = sb("ccol", [P, KT])
        biasT = sb("biasT", [P, H, W3])
        big = sb("big", [P, 8192])
        wide_addr = -(-nc.sbuf_base // 32) * 32
        wide = sb("wide", [P, 2, H, W3])
        hT = [sb(f"hT{i}", [P, 2, T]) for i in range(2)]
        hh = [sb(f"hh{i}", [P, 2, T], F32R) for i in range(2)]
        hl = [sb(f"hl{i}", [P, 2, T], F32R) for i in range(2)]
        PT = [sb(f"PT{i}", [P, W3]) for i in range(2)]
        small = sb("small", [P, 512])
        aux = sb("aux", [P, 1664])
        stat = sb("stat", [P, 8])
        psum = ctx.enter_context(nc.psum_tensor("psum", [P, 8, 512], F32))

        wh = [sb(f"wh{i}", [P, SLOT], F32R) for i in range(PARTS - 1)]
        wl = [sb(f"wl{i}", [P, SLOT], F32R) for i in range(PARTS - 1)]
        wh.append(nc.alloc_sbuf_tensor_at("wh2", [P, SLOT], F32R, offset=wide_addr))
        wl.append(nc.alloc_sbuf_tensor_at("wl2", [P, SLOT], F32R, offset=wide_addr + 4 * SLOT))

        modrow = nc.dram_tensor("adaln_rows", (2, 6 * D), F32, kind="Internal").ap()
        rowbuf = nc.dram_tensor("bias_rows", (3, H, P, W3), F32, kind="Internal").ap()

        loaded = [sem(f"slot{i}_loaded") for i in range(RING)]
        piece_used = sem("piece_used")
        freed = sem("slot_freed")
        high = sem("high")
        crossed = sem("stage_crossed")
        act_step = sem("act_step")
        dve_step = sem("dve_step")
        const_in = sem("const_in")
        gain_in = [sem(f"gain{i}_in") for i in range(GAINBUFS)]
        gain_used = sem("gain_used")
        extra_in = sem("extra_in")
        bias_in = sem("bias_in")
        rows_ready = sem("rows_ready")
        rows_out = sem("rows_out")
        mod_in = sem("mod_in")
        mod_done = sem("mod_done")
        mod_out = sem("mod_out")
        squared = sem("squared")
        turned = sem("turned")
        turn_high = sem("turn_high")
        gated = sem("gated")
        hidden = sem("hidden")
        proj_read = sem("proj_read")
        ada_read = sem("ada_read")
        score = sem("score")
        biased = sem("biased")
        expd = sem("expd")
        p_turned = sem("p_turned")
        p_read = sem("p_read")
        headout = sem("headout")
        out_done = sem("out_done")

        def trio(name):
            return sem(name + "_pe"), sem(name + "_act"), sem(name + "_dve")

        setup_pe, setup_act, setup_dve = trio("setup")
        pad_dve, pad_act = sem("padding_dve"), sem("padding_act")
        stick_pe, stick_act, stick_dve = trio("stick")
        gates_pe, gates_act, gates_dve = trio("gates")
        ml_pe, ml_act, ml_dve = trio("mlstm")
        comp_pe, comp_act, comp_dve = trio("compress")
        cmp_pe, cmp_act, cmp_dve = trio("cmp")
        lat_pe, lat_act, lat_dve = trio("latent")
        route_pe, route_act, route_dve = trio("router")

        ident = const[:, C_IDENT:C_IDENT + P]

        def cols(w, c0, n):
            return w[:, c0:c0 + n].rearrange("(k p) n -> p k n", p=P)

        def slot(n, shape):
            k, w = shape
            return ring[n % RING][:, 0:k * w].rearrange("p (k w) -> p k w", k=k)

        def linear_slots(w, widths):
            at, got = 0, []
            for n in widths:
                got.append(("one", cols(w, at, n), (w.shape[0] // P, n)))
                at += n
            return got

        g_w, u_w, d_w = I["ffn_w_gate"], I["ffn_w_up"], I["ffn_w_down"]

        def ffn_chunk(which, layer, part, c):
            if which == "d":
                w = d_w[layer, part].rearrange("(c s p) n -> c p s n", p=P, s=2)
                return w[c]
            w = {"g": g_w, "u": u_w}[which][layer, part].rearrange("(k p) (c n) -> c p k n", p=P, n=256)
            return w[c]

        mg, mu, md = I["moe_w_gate_2"], I["moe_w_up_2"], I["moe_w_down_2"]

        def moe_chunk(which, layer, c, i):
            e = c // EC if i is None else i + c // EC
            if which == "d":
                return md[layer].rearrange("e (h s p) n -> h e p s n", p=P, s=2, h=EC)[c % EC][e]
            w = {"g": mg, "u": mu}[which]
            return w[layer].rearrange("e (k p) (h n) -> h e p k n", p=P, h=EC)[c % EC][e]

        GU, DN = (KT, 256), (2, D)

        ATTN_IN = [256] * 12
        MLSTM_IN = [256] * 16 + [16]
        EVEN_IN = [256, 256, 256, 256, 256, 24] + [256] * 6
        ODD_IN = [256, 192, 256, 256, 256]
        OUT4 = [256] * 4

        def parts(n, shape):
            k, w = shape
            return [b[n % PARTS][:, 0:k * w].rearrange("p (k w) -> p k w", k=k) for b in (wh, wl)]

        def slot_count(n):
            return 16 * (n // RING + 1)

        def chunk_piece(n0, which, c, chunks):
            if which == "d":
                return n0 + 2 + 3 * c + 2 if c < chunks - 1 else n0 + 3 * chunks - 1
            return n0 + (0 if c == 0 else 2 + 3 * (c - 1)) + (1 if which == "u" else 0)

        def loop_pairs(chunks):
            return (chunks - 2) // 2

        wide_flat = wide[:, :, :, :].rearrange("p a h w -> p (a h w)")

        def wide_at(at, n):
            return wide_flat[0:8, at:at + n]

        S_RB, S_CONVW = 0, 24
        S_NMX, S_SUM, S_INV = 88, 104, 120
        S_G = 136
        S_COL, S_THR, S_DEN = 184, 200, 216
        S_MG = 136
        S_PAD = 440
        S_RW, S_R = 232, 360

        R_DIL, R_REL, R_PAD, R_PADMASK, R_END = 0, W3, 5 * W3, 5 * W3 + 512, 5 * W3 + 1024

        pad_b = [wide_at(1536 + 512 * i, 512) for i in range(2)]
        pad_m = [wide_at(2560 + 640 * i, 513) for i in range(2)]
        pad_a = [wide_at(3840 + 1024 * i, 512) for i in range(2)]
        pad_e = [wide_at(4352 + 1024 * i, 512) for i in range(2)]

        A_I, A_F, A_L, A_B, A_G = 256, 512, 768, 1024, 1280
        A_QRT, A_KRT = 384, 1408

        QA, KA, VA, QD, KD, VD = (1024 * i for i in range(6))
        M_PRE, M_V = 0, 4096
        (N_Q, N_KC, N_VC, N_KS, N_VS, N_KW, N_VW, N_QB, N_KB, N_VB) = (
            0, 1024, 1280, 1536, 1792, 2048, 2304, 2560, 3584, 4608)
        N_F = 5632
        (N_POS, N_U, N_GT, N_KCMP, N_VCMP) = (6656, 6720, 7232, 7360, 7376)
        (O_Q, O_K, O_V, O_CQ, O_CKV, O_KR, O_QM, O_KVM, O_QNT, O_KNT) = (
            0, 1024, 1280, 1536, 2048, 2304, 2432, 3968, 6016, 7040)

        def big_n(at, w):
            return big[:, at:at + TT * w].rearrange("p (t w) -> p t w", t=TT)

        def big_t(at, m):
            return big[:, at + m * T:at + (m + 1) * T]

        def t2(at, scale=1.0):
            return [("TT", 0, 256, big[:, at:at + 512], scale)]

        def n1(dst, c=0, scale=1.0):
            return ("N", c, dst.shape[2], dst, scale)

        def n256(at, w, j):
            return [n1(big_n(at, w)[:, :, j * 256:(j + 1) * 256])]

        def qgroup(kv, at, scale):
            return [("Q", 0, 256, big[64 * kv:64 * kv + 64, at:at + 1024], scale)]

        vM = big[:, M_V:M_V + TT * H * VW].rearrange("p (t h w) -> p t h w", t=TT, h=H)
        o_flat = biasT[:, :, :].rearrange("p h w -> p (h w)")[:, 0:TT * D]
        oM = o_flat.rearrange("p (t w) -> p t w", t=TT)

        def gview(at):
            return small[:, at:at + 48].rearrange("p (t w) -> p t w", t=TT)

        PROJ = {
            "attn": [t2(QA, 0.125), t2(QA + 512, 0.125), t2(KA), t2(KA + 512), n256(VA, 512, 0), n256(VA, 512, 1),
                     t2(QD, 0.125), t2(QD + 512, 0.125), t2(KD), t2(KD + 512), n256(VD, 512, 0), n256(VD, 512, 1)],
            "mlstm": [t2(M_PRE + 512 * j) for j in range(8)]
                     + [[("V", 0, 256, vM[:, :, 2 * j:2 * j + 2, 0:P], 1.0)] for j in range(4)]
                     + [[n1(oM[:, :, 256 * j:256 * j + 256])] for j in range(4)]
                     + [[n1(small[:, S_MG:S_MG + 32].rearrange("p (t w) -> p t w", t=TT))]],
            "even": [qgroup(0, N_Q, 0.125), qgroup(1, N_Q, 0.125),
                     [("T", 0, P, big_t(N_KC, 0), 1.0), ("T", P, P, big_t(N_VC, 0), 1.0)],
                     [("T", 0, P, big_t(N_KS, 0), 1.0), n1(big_n(N_VS, P), P)],
                     [("T", 0, P, big_t(N_KW, 0), 1.0), n1(big_n(N_VW, P), P)],
                     [n1(gview(S_G))],
                     t2(N_QB, 0.125), t2(N_QB + 512, 0.125), t2(N_KB), t2(N_KB + 512),
                     n256(N_VB, 512, 0), n256(N_VB, 512, 1)],
            "odd": [[n1(big_n(O_CQ, 256))], [n1(big_n(O_CKV, P)), n1(big_n(O_KR, 64), P)],
                    qgroup(0, O_Q, 0.125), qgroup(1, O_Q, 0.125),
                    [("T", 0, P, big_t(O_K, 0), 1.0), n1(big_n(O_V, P), P)]],
        }
        PROJ_AT, at = {}, 0
        for name in PROJ:
            PROJ_AT[name] = at
            at += len(PROJ[name])

        def pair_heads(qat, kat):
            def parts(h):
                p0 = 64 * (h % 2)
                return [(big[p0:p0 + 64, qat + (h // 2) * T:qat + (h // 2 + 1) * T],
                         big[p0:p0 + 64, kat + (h // 2) * T:kat + (h // 2 + 1) * T])]
            return parts

        def group_heads(qat, kat):
            def parts(h):
                p0, g = 64 * (h // 4), h % 4
                return [(big[p0:p0 + 64, qat + g * T:qat + (g + 1) * T], big[p0:p0 + 64, kat:kat + T])]
            return parts

        def mla_heads(h):
            qrT = aux[0:64, A_QRT + h * T:A_QRT + (h + 1) * T]
            return [(big_t(O_QNT, h), big_t(O_KNT, h)), (qrT, aux[0:64, A_KRT:A_KRT + T])]

        vmla = big_n(O_KVM, 1024).rearrange("p t (h w) -> p t h w", h=MH)

        def soft(parts, v, heads, dv, dst, bias=True, scale=1.0, pad=None, gate=None):
            return dict(parts=parts, v=v, heads=heads, dv=dv, dst=dst, bias=bias, scale=scale, pad=pad, gate=gate)

        SOFT = {
            "dilated": soft(pair_heads(QD, KD), lambda h, t: big_n(VD, 512)[:, t, 64 * h:64 * h + 64], H, 64, 512),
            "selected": soft(group_heads(N_Q, N_KS), lambda h, t: big_n(N_VS, P)[:, t, 64 * (h // 4):64 * (h // 4) + 64],
                             H, 64, 0, gate=1),
            "window": soft(group_heads(N_Q, N_KW), lambda h, t: big_n(N_VW, P)[:, t, 64 * (h // 4):64 * (h // 4) + 64],
                           H, 64, 0, gate=2, pad=S_PAD),
            "moba": soft(pair_heads(N_QB, N_KB), lambda h, t: big_n(N_VB, 512)[:, t, 64 * h:64 * h + 64], H, 64, 512),
            "mla": soft(mla_heads, lambda h, t: vmla[:, t, h, P:2 * P], MH, P, 0, bias=False, scale=192.0 ** -0.5),
            "sliding": soft(group_heads(O_Q, O_K), lambda h, t: big_n(O_V, P)[:, t, 64 * (h // 4):64 * (h // 4) + 64],
                            H, 64, 512, pad=S_PAD + 32),
        }
        PADDED = [name for name in SOFT if SOFT[name]["pad"] is not None]
        at, steps = 0, 0
        for spec in SOFT.values():
            spec["head0"], spec["step0"], spec["steps"] = at, steps, 3 if spec["pad"] is None else 5
            at, steps = at + spec["heads"], steps + spec["heads"] * spec["steps"]

        STAGES = [("setup", (), 0)]
        stream = []

        def add(name, *args, gains=0, pieces=()):
            STAGES.append((name, args, gains))
            stream.extend(pieces)

        def mixer_end(weights, residual):
            add("turn")
            add("outproj", pieces=linear_slots(weights, OUT4))
            add(*residual, gains=1)

        for layer in range(2):
            add("ada", pieces=[("ada", layer, 24)])

        for layer in range(2):
            add("norm", None, gains=1)
            add("turn")
            add("ffn", FC, False, pieces=[("ffn", (layer, 0), FC)])
            add("residual", "norm", 0.5, gains=1)
            add("norm", None, gains=1)
            add("turn")
            if layer == 0:
                add("project", "attn", pieces=linear_slots(I["attn_w_in"][0], ATTN_IN))
                add("stick")
                add("soft", "dilated")
                mixer_end(I["attn_w_out"][0], ("residual", "norm", 1.0))
            else:
                add("project", "mlstm", pieces=linear_slots(I["mlstm_w_in"][0], MLSTM_IN))
                add("gates")
                add("mlstm", gains=1)
                mixer_end(I["mlstm_w_out"][0], ("residual", "norm", 1.0))
            add("norm", None, gains=1)
            add("turn")
            add("ffn", FC, False, pieces=[("ffn", (layer, 1), FC)])
            add("residual", "norm", 0.5, gains=1)
        for layer in range(2):
            add("norm", "ada", gains=3)
            add("turn")
            if layer == 0:
                add("project", "even", pieces=linear_slots(I["ev_w_in_2"][0], EVEN_IN))
                add("compress", pieces=[("one", w1[half * 1024:half * 1024 + 1024, :].rearrange("(k p) n -> p k n", p=P), GU)
                                        for w1 in (I["nsa_ck_w1_2"][0], I["nsa_cv_w1_2"][0]) for half in range(2)])
                add("cmp")
                for name in ("selected", "window", "moba"):
                    add("soft", name)
                mixer_end(I["ev_w_out_2"][0], ("residual", "gate", None))
            else:
                add("project", "odd", pieces=linear_slots(I["od_w_in_2"][0], ODD_IN))
                add("latent", pieces=[("one", cols(I["mla_w_q_up_2"][0], 0, 768), (2, 768)),
                                      ("one", cols(I["mla_w_kv_up_2"][0], 0, 1024), (1, 1024))])
                add("soft", "mla")
                add("soft", "sliding")
                mixer_end(I["od_w_out_2"][0], ("residual", "gate", None))
            add("norm", "ada", gains=3)
            add("turn")
            add("router")
            add("ffn", E * EC, True, pieces=[("moe", (layer, 0), E * EC)])
            add("residual", "gate", None, gains=1)
        add("final", gains=1)

        seen, INSTANCE = {}, []
        for name, _, _ in STAGES:
            INSTANCE.append(seen.get(name, 0))
            seen[name] = INSTANCE[-1] + 1

        GAINS = []
        for layer in range(2):
            g = [I["norm_g"][layer, j] for j in range(6)]
            GAINS += g[0:3] + ([I["mlstm_head_g"][0]] if layer == 1 else []) + g[3:6]
        for layer in range(2):
            for name, m in (("norm_mix_2", 0), ("norm_ffn_2", 3)):
                GAINS += [I[name][layer]] + [modrow[layer, v * D:(v + 1) * D] for v in (m + 1, m, m + 2)]
        GAINS.append(I["final_norm_2"])
        assert len(GAINS) == sum(s[2] for s in STAGES)

        mod_row = wide_flat[0:1, 0:6 * D]

        def boundary(eng, s):
            eng.drain().then_inc(crossed, 1)
            eng.wait_ge(crossed, 3 * s)

        block = ctx.enter_context(nc.Block())

        @block.sync
        def _(sp):
            def load(n, src, shape, i=None):
                if i is not None:
                    sp.wait_ge(freed, i * LOOP + (n - RING + 1))
                elif n >= RING:
                    sp.wait_ge(freed, n - RING + 1)
                sp.dma_start(slot(n, shape), src).then_inc(loaded[n % RING], 16)

            def chunked(n, source, chunks):
                def piece(which, c, i=None):
                    load(chunk_piece(n, which, c, chunks), source(which, c, i), DN if which == "d" else GU, i)

                for which, c in (("g", 0), ("u", 0), ("g", 1), ("u", 1), ("d", 0)):
                    piece(which, c)
                with sp.Fori(0, loop_pairs(chunks)) as i:
                    for c in (1, 2):
                        piece("g", c + 1, i)
                        piece("u", c + 1, i)
                        piece("d", c, i)
                for c in range(1 + 2 * loop_pairs(chunks), chunks):
                    if c + 1 < chunks:
                        piece("g", c + 1)
                        piece("u", c + 1)
                    piece("d", c)

            n = 0
            sp.dma_start(const[:, :], I["const"]).then_inc(const_in, 16)
            sp.dma_start(x[:, :, :], I["x"][0].rearrange("(t p) d -> p t d", p=P)).then_inc(const_in, 16)
            for kind, what, more in stream:
                if kind == "one":
                    load(n, what, more)
                    n += 1
                elif kind == "ada":
                    w = I["ada_w_2"][what].rearrange("(k p) (s r n) -> r s p k n", p=P, r=LOOP, n=256)
                    for r in range(LOOP):
                        load(n + r, w[r][0], GU)
                    with sp.Fori(1, 4) as i:
                        for r in range(LOOP):
                            load(n + r, w[r][i], GU, i)
                    n += 24
                elif kind == "ffn":
                    chunked(n, lambda which, c, i: ffn_chunk(which, *what, c if i is None else i * 2 + c), more)
                    n += 3 * more
                else:
                    chunked(n, lambda which, c, i: moe_chunk(which, what[0], c, i), more)
                    n += 3 * more

        @block.gpsimd
        def _(pool):
            def load_gain(k):
                if k >= GAINBUFS:
                    pool.wait_ge(gain_used, k - GAINBUFS + 1)
                pool.dma_start(gain[k % GAINBUFS][:, :], GAINS[k].rearrange("(a n) -> a n", a=1)
                               .broadcast_to([P, D])).then_inc(gain_in[k % GAINBUFS], 16)

            def load_bias(kind):
                at = rowbuf[kind].offset + 127
                pool.dma_start(biasT[:, :, P:W3],
                               bass.AP(rowbuf.tensor, at, [[W3 - 1, P], [P * W3, H], [1, T]])).then_inc(bias_in, 16)
                pool.dma_start(biasT[:, :, 0:P],
                               bass.AP(rowbuf.tensor, at + P, [[W3 - 1, P], [P * W3, H], [1, P]])).then_inc(bias_in, 16)

            def small_in(dst, src):
                pool.dma_start(dst, src).then_inc(extra_in, 16)

            def row(ap):
                return ap.rearrange("(a n) -> a n", a=1)

            small_in(aux[0:32, 0:8], I["rel_bias"])
            small_in(aux[0:32, 8:16], I["rel_table_2"])
            small_in(big[0:32, 0:R_END], I["rows"])
            small_in(aux[0:8, 16:144], I["c_2"][0].rearrange("(k p) -> k p", p=P))
            small_in(small[:, S_RB:S_RB + E], row(I["router_b_2"]).broadcast_to([P, E]))
            small_in(aux[0:8, 144:145], I["swa_sinks_2"].rearrange("a h -> h a"))
            small_in(small[:, S_RW:S_RW + P].rearrange("p (k e) -> p k e", k=KT),
                     I["router_w_2"].rearrange("(k p) e -> p k e", p=P))
            for g in range(GAINBUFS):
                load_gain(g)
            g = GAINBUFS
            for s, (name, args, used) in enumerate(STAGES):
                if name == "setup":
                    pool.wait_ge(rows_out, 48)
                    load_bias(0)
                if name == "project" and args[0] != "attn":
                    pool.wait_ge(crossed, 3 * s)
                if name == "project" and args[0] == "mlstm":
                    small_in(aux[0:8, 0:1], I["mlstm_b_gates"][0, 0:8].rearrange("(p a) -> p a", a=1))
                    small_in(aux[0:8, 1:2], I["mlstm_b_gates"][0, 8:16].rearrange("(p a) -> p a", a=1))
                    small_in(aux[0:64, 16:144], I["mlstm_conv_w"][0].rearrange("j (t p) -> (j t) p", p=P))
                if name == "project" and args[0] == "even":
                    load_bias(1)
                    for at in (0, 64):
                        small_in(aux[0:32, at:at + 64], I["nsa_pos_k_2"][0])
                        small_in(aux[0:32, P + at:P + at + 64], I["nsa_pos_v_2"][0])
                    for at, w in ((256, I["nsa_ck_w2_2"]), (384, I["nsa_cv_w2_2"])):
                        small_in(aux[:, at:at + P].rearrange("p (k n) -> p k n", k=2),
                                 w[0].rearrange("(k p) n -> p k n", p=P))
                if name == "project" and args[0] == "odd":
                    load_bias(2)
                    small_in(aux[:, 0:256], I["mla_q_norm_2"].broadcast_to([P, 256]))
                    small_in(aux[:, 256:384], I["mla_kv_norm_2"].broadcast_to([P, P]))
                if name == "ada":
                    pool.wait_ge(crossed, 3 * s)
                    pool.dma_start(mod_row, I["ada_b_2"][INSTANCE[s]:INSTANCE[s] + 1, :]).then_inc(mod_in, 16)
                if name == "ada" and INSTANCE[s] == 1:
                    pool.wait_ge(mod_out, 32)
                for _ in range(used):
                    if g < len(GAINS):
                        load_gain(g)
                        g += 1

        PIECE0, n_piece, extra = [], 0, iter(())
        SLOTS = {"outproj": 4, "compress": 4, "latent": 2, "ada": 24}
        SQ0, n_sq = [], 0
        for name, args, _ in STAGES:
            PIECE0.append(n_piece)
            SQ0.append(n_sq)
            n_piece += (3 * args[0] if name == "ffn" else len(PROJ[args[0]]) if name == "project"
                        else SLOTS.get(name, 0))
            n_sq += 2 if name in ("norm", "final") or (name == "residual" and args[0] == "norm") else 0
        SPLIT0 = [PIECE0[s] - sum(SLOTS.get(n, 0) for n, _, _ in STAGES[:s] if n != "outproj")
                  for s in range(len(STAGES))]
        GAIN0 = [sum(u for _, _, u in STAGES[:s]) for s in range(len(STAGES))]
        EXTRA = {"setup": 7 * 16, "mlstm": 10 * 16, "even": 16 * 16, "odd": 18 * 16}

        def ffn_bases(k):
            if k < 4:
                return k * FC, 3 * k * FC
            return 4 * FC + (k - 4) * E * EC, 12 * FC + 4 * (k - 4) * E * EC

        def wait_gain(eng, g):
            eng.wait_ge(gain_in[g % GAINBUFS], 16 * (g // GAINBUFS + 1))

        GB, UB = 4, 6
        route = big[:, 4096:8192]
        routing = big[:, 0:4096].rearrange("p (e t) -> p e t", e=E)
        cv = wide_flat[:, 0:4096].rearrange("p (m t) -> p m t", t=T)
        mE = [wide_flat[:, 4096 + W3 * i:4096 + W3 * (i + 1)] for i in range(2)]
        raw = big[:, 0:TT * H * VW].rearrange("p (t h w) -> p t h w", t=TT, h=H)
        hid = nrm[:, :, :].rearrange("p t (h w) -> p t h w", h=H)
        qm = big[:, O_QM:O_QM + 1536].rearrange("p (t h w) -> p t h w", t=TT, h=MH)
        blocksF = [big[:, N_F + 480 * i:N_F + 480 * (i + 1)].rearrange("p (j v n) -> p j v n", j=16, v=2)
                   for i in range(2)]
        cS = wide_flat[:, 0:256].rearrange("p (h t n) -> p h t n", h=H, t=TT)
        cPT = wide_flat[:, 1024:3072]
        cqT = wide_flat[:, 0:3 * T].rearrange("p (k t) -> p k t", t=T)

        @block.tensor
        def _(pe):
            def mm(out_, lhsT, rhs, start, stop, **kw):
                return pe.matmul(out_, lhsT, rhs, start=start, stop=stop, **kw)

            def piece_in(n, i=None):
                if i is None:
                    pe.wait_ge(loaded[n % RING], slot_count(n))
                else:
                    pe.wait_ge(loaded[n % RING], i * (16 * LOOP // RING) + slot_count(n))

            def used(last, n, i=None):
                last.then_inc(piece_used, 1)
                pe.wait_ge(piece_used, n + 1 if i is None else i * LOOP + (n + 1))
                pe.nop().then_inc(freed, 1)

            def split_in(n, i=None):
                pe.wait_ge(freed, n + 1 if i is None else i * LOOP + (n + 1))

            def three(out_, stationary, moving, first, last):
                (sh, sl), (mh, ml) = stationary, moving
                mm(out_, sh, mh, first, False)
                mm(out_, sh, ml, False, False)
                return mm(out_, sl, mh, False, last)

            def both(ap, *index):
                return [a[index] for a in ap]

            xs = (xh, xl)

            def setup(s, k):
                pe.wait_ge(const_in, 32)
                pe.wait_ge(extra_in, EXTRA["setup"])
                pe.transpose(psum[:, 0, 0:8], aux[0:8, 16:144], ident[0:8, 0:8])
                mm(psum[0:8, 1, 0:W3], aux[0:32, 0:8], big[0:32, 0:W3], True, True)
                mm(psum[0:8, 2, 0:W3], aux[0:32, 8:16], big[0:32, R_REL:R_REL + W3], True, True)
                mm(psum[0:8, 3, :], aux[0:32, 8:16], big[0:32, R_PAD:R_PAD + 512], True, True).then_inc(setup_pe, 1)
                pe.wait_ge(setup_dve, 3)
                for i in range(2):
                    for t in range(TT):
                        lo, at = 383 - P * t, 32 * i + 8 * t
                        pe.transpose(psum[:, 4, at:at + 8], pad_m[i][:, lo + 1:lo + 1 + P], ident[0:8, 0:8])
                        last = pe.transpose(psum[:, 4, at + 16:at + 24], pad_b[i][:, lo:lo + P], ident[0:8, 0:8])
                last.then_inc(setup_pe, 1)
                pe.wait_ge(setup_dve, 4)
                mm(psum[:, 5, 0:64], const[:, C_FLIP:C_FLIP + P], small[:, S_PAD:S_PAD + 64], True, True)\
                    .then_inc(setup_pe, 1)

            def turn(s, k):
                for q in range(4):
                    t, half = q // 2, q % 2
                    for i in range(4):
                        f = (4 * half + i) * P
                        last = pe.transpose(psum[:, q, i * P:(i + 1) * P], nrm[:, t, f:f + P], ident)
                    last.then_inc(turned, 1)

            def ffn(s, k, chunks, moe):
                n0 = PIECE0[s]
                c0, h0 = ffn_bases(k)
                steps = 4 if moe else 3

                def gate_up_products(c, i=None):
                    if c >= 2:
                        v = h0 + steps * (c - 1)
                        pe.wait_ge(hidden, v if i is None else i * (2 * steps) + v)
                    for which, bank in (("g", GB + c % 2), ("u", UB + c % 2)):
                        n = chunk_piece(n0, which, c, chunks)
                        split_in(n, i)
                        w = parts(n, GU)
                        for f in range(2):
                            for kt in range(KT):
                                last = three(psum[:, bank, f * T:(f + 1) * T],
                                             both(w, slice(0, P), kt, slice(f * P, (f + 1) * P)),
                                             both(xs, slice(0, P), kt, slice(0, T)), kt == 0, kt == KT - 1)
                        last.then_inc(piece_used, 1)

                def down_products(c, i=None):
                    v = h0 + steps * (c + 1)
                    pe.wait_ge(hidden, v if i is None else i * (2 * steps) + v)
                    n = chunk_piece(n0, "d", c, chunks)
                    split_in(n, i)
                    w, h = parts(n, DN), (hh[c % 2], hl[c % 2])
                    for f in range(2):
                        for t in range(TT):
                            for half in range(2):
                                last = three(psum[:, 2 * t + half, :],
                                             both(h, slice(0, P), f, slice(t * P, (t + 1) * P)),
                                             both(w, slice(0, P), f, slice(half * 512, (half + 1) * 512)),
                                             c == 0 and f == 0, c == chunks - 1 and f == 1)
                    last.then_inc(piece_used, 1)

                gate_up_products(0)
                gate_up_products(1)
                down_products(0)
                with pe.Fori(0, loop_pairs(chunks)) as i:
                    for c in (1, 2):
                        gate_up_products(c + 1, i)
                        down_products(c, i)
                for c in range(1 + 2 * loop_pairs(chunks), chunks):
                    if c + 1 < chunks:
                        gate_up_products(c + 1)
                    down_products(c)

            def project(s, k, name):
                widths = {"attn": ATTN_IN, "mlstm": MLSTM_IN, "even": EVEN_IN, "odd": ODD_IN}[name]
                for j, pieces in enumerate(PROJ[name]):
                    n = PIECE0[s] + j
                    if j >= 4:
                        pe.wait_ge(proj_read, PROJ_AT[name] + j - 3)
                    split_in(n)
                    w = parts(n, (KT, widths[j]))
                    at = 0
                    for kind, c, m, _, _ in pieces:
                        for t in range(TT if kind in ("N", "V") else m // P):
                            for kt in range(KT):
                                if kind in ("N", "V"):
                                    width, a, b = m, both(xs, slice(0, P), kt, slice(t * P, (t + 1) * P)), \
                                        both(w, slice(0, P), kt, slice(c, c + m))
                                else:
                                    width, b, a = T, both(xs, slice(0, P), kt, slice(0, T)), \
                                        both(w, slice(0, P), kt, slice(c + t * P, c + (t + 1) * P))
                                last = three(psum[:, j % 4, at:at + width], a, b, kt == 0, kt == KT - 1)
                            at += width
                    last.then_inc(piece_used, 1)

            def outproj(s, k):
                for j in range(4):
                    n = PIECE0[s] + j
                    split_in(n)
                    w = parts(n, GU)
                    for t in range(TT):
                        for kt in range(KT):
                            last = three(psum[:, 2 * t + j // 2, (j % 2) * 256:(j % 2 + 1) * 256],
                                         both(xs, slice(0, P), kt, slice(t * P, (t + 1) * P)),
                                         both(w, slice(0, P), kt, slice(0, 256)), kt == 0, kt == KT - 1)
                    last.then_inc(piece_used, 1)

            def stick(s, k):
                def scores(h):
                    if h >= 2:
                        pe.wait_ge(stick_dve, h - 1)
                    p0, c = 64 * (h % 2), (h // 2) * T
                    q, key = big[p0:p0 + 64, QA + c:QA + c + T], big[p0:p0 + 64, KA + c:KA + c + T]
                    mm(psum[:, h % 2, 0:T], key[:, 0:P], q, True, True)
                    mm(psum[:, h % 2, T:W3], key[:, P:T], q[:, P:T], True, True).then_inc(stick_pe, 1)

                def later(h):
                    pe.wait_ge(stick_dve, H + 3 * (h + 1))
                    if h >= 2:
                        pe.wait_ge(stick_dve, 4 * H + h - 1)
                    sp_h, b = wide[:, 1, h, :], 2 + h % 2
                    mm(psum[:, b, 0:T], const[:, C_AFTER:C_AFTER + P], sp_h[:, 0:T], True, False,
                       skip_group_check=True)
                    mm(psum[:, b, P:T], const[:, C_ONES:C_ONES + P], sp_h[:, T:W3], False, True,
                       skip_group_check=True)
                    mm(psum[:, b, T:W3], const[:, C_AFTER:C_AFTER + P], sp_h[:, T:W3], True, True)\
                        .then_inc(stick_pe, 1)

                def values(h):
                    pe.wait_ge(stick_dve, 5 * H + h + 1)
                    w = wide[:, 0, h, :]
                    v = big_n(VA, 512)[:, :, 64 * h:64 * h + 64]
                    mm(psum[:, 4, 64 * h:64 * h + 64], w[:, 0:P], v[:, 0], True, True)
                    mm(psum[:, 5, 64 * h:64 * h + 64], w[:, P:T], v[:, 0], True, False)
                    return mm(psum[:, 5, 64 * h:64 * h + 64], w[:, T:W3], v[:, 1], False, True)

                for h in range(H):
                    scores(h)
                for h in range(H):
                    later(h)
                for h in range(H):
                    last = values(h)
                last.then_inc(stick_pe, 1)

            def soft_attention(s, k, name):
                a = SOFT[name]
                h0, s0, n, dv = a["head0"], a["step0"], a["steps"], a["dv"]

                def scores(h):
                    if h >= 2:
                        pe.wait_ge(biased, s0 + n * (h - 2) + 1)
                    parts = a["parts"](h)
                    for lo, hi, t in ((0, P, 0), (P, W3, 1)):
                        for i, (q, key) in enumerate(parts):
                            last = mm(psum[:, h % 2, lo:hi], q[:, t * P:(t + 1) * P], key[:, 0:hi - lo],
                                      i == 0, i == len(parts) - 1)
                    last.then_inc(score, 1)

                def turn_probs(h):
                    pe.wait_ge(expd, 2 * (h0 + h + 1))
                    if h >= 2:
                        pe.wait_ge(p_read, h0 + h - 1)
                    for i in range(3):
                        last = pe.transpose(psum[:, 2 + h % 2, i * P:(i + 1) * P],
                                            wide[:, 0, h, i * P:(i + 1) * P], ident)
                    last.then_inc(p_turned, 1)

                def values(h):
                    pe.wait_ge(p_read, h0 + h + 1)
                    p, c = PT[h % 2], slice(h * dv, (h + 1) * dv)
                    mm(psum[:, 4, c], p[:, 0:P], a["v"](h, 0), True, True)
                    mm(psum[:, 5, c], p[:, P:T], a["v"](h, 0), True, False)
                    mm(psum[:, 5, c], p[:, T:W3], a["v"](h, 1), False, True).then_inc(headout, 1)

                scores(0)
                scores(1)
                for h in range(a["heads"]):
                    turn_probs(h)
                    if h + 2 < a["heads"]:
                        scores(h + 2)
                    if h >= 1:
                        values(h - 1)
                values(a["heads"] - 1)

            def gates(s, k):
                pe.wait_ge(extra_in, EXTRA["mlstm"])
                pe.transpose(psum[:, 0, 0:64], aux[0:64, 16:144], ident[0:64, 0:64])
                for t in range(TT):
                    for i in range(2):
                        at = S_MG + 16 * t + 8 * i
                        last = pe.transpose(psum[0:8, 2 + i, t * P:(t + 1) * P], small[:, at:at + 8], ident)
                last.then_inc(gates_pe, 1)
                pe.wait_ge(gates_act, 2)
                for t in range(TT):
                    pe.transpose(psum[:, 1, 8 * t:8 * t + 8], aux[0:8, A_G + t * P:A_G + (t + 1) * P], ident[0:8, 0:8])
                    last = pe.transpose(psum[:, 1, 16 + 8 * t:24 + 8 * t],
                                        aux[0:8, A_F + t * P:A_F + (t + 1) * P], ident[0:8, 0:8])
                last.then_inc(gates_pe, 1)

            def mlstm(s, k):
                def products(h):
                    if h >= 2:
                        pe.wait_ge(ml_dve, 4 * (h - 1))
                    mm(psum[:, h % 2, 0:T], spread(ident[0:8, h], 1, P), aux[0:8, A_L:A_L + T], True, True)\
                        .then_inc(ml_pe, 1)
                    mm(psum[:, 2 + h % 2, 0:T], cv[:, 8 + h, 0:P], cv[:, h, :], True, True)
                    mm(psum[:, 2 + h % 2, T:W3], cv[:, 8 + h, P:T], cv[:, h, P:T], True, True).then_inc(ml_pe, 1)

                def values(h):
                    pe.wait_ge(ml_dve, 4 * (h + 1))
                    if h >= 2:
                        pe.wait_ge(ml_act, 2 * h - 1)
                    p, b = PT[h % 2], 4 + h % 2
                    mm(psum[:, b, 0:VW], p[:, 0:P], vM[:, 0, h, :], True, True)
                    mm(psum[:, b, VW:2 * VW], p[:, P:T], vM[:, 0, h, :], True, False)
                    mm(psum[:, b, VW:2 * VW], p[:, T:W3], vM[:, 1, h, :], False, True).then_inc(ml_pe, 1)

                products(0)
                for h in range(H):
                    if h + 1 < H:
                        products(h + 1)
                    values(h)

            def ada(s, k):
                n0 = PIECE0[s]
                with pe.Fori(0, 4) as i:
                    for r in range(LOOP):
                        pe.wait_ge(ada_read, i * LOOP + (26 * k + r + 1))
                        piece_in(n0 + r, i)
                        w = slot(n0 + r, GU)
                        for kt in range(KT):
                            last = mm(psum[0:1, r % 2, 0:256], ccol[:, kt:kt + 1], w[:, kt, :], kt == 0, kt == KT - 1)
                        used(last, n0 + r, i)

            def compress(s, k):
                pe.wait_ge(extra_in, EXTRA["even"])
                pe.transpose(psum[:, 0, 0:32], aux[0:32, 0:P], ident[0:32, 0:32])
                pe.transpose(psum[:, 0, 32:64], aux[0:32, P:2 * P], ident[0:32, 0:32]).then_inc(comp_pe, 1)
                pe.wait_ge(comp_dve, 9)
                for i in range(2):
                    for half in range(2):
                        n = PIECE0[s] + 2 * i + half
                        piece_in(n)
                        w = slot(n, GU)
                        for kt in range(KT):
                            j = half * KT + kt
                            last = mm(psum[0:30, 1 + i, 0:256], blocksF[i][:, j, :, :], w[:, kt, :],
                                      j == 0, j == 15)
                        used(last, n)
                pe.wait_ge(comp_act, 1)
                for i in range(2):
                    for half in range(2):
                        at = N_U + 256 * i + P * half
                        last = pe.transpose(psum[:, 3, (2 * i + half) * 30:(2 * i + half + 1) * 30],
                                            big[0:30, at:at + P], ident[0:30, 0:30])
                last.then_inc(comp_pe, 1)
                pe.wait_ge(comp_dve, 10)
                for v in range(2):
                    for half in range(2):
                        g = N_GT + 30 * half + NCMP * v
                        mm(psum[64 * v:64 * v + 64, 4, 0:NCMP], aux[:, 256 + 64 * half:320 + 64 * half],
                           big[:, g:g + NCMP], half == 0, half == 1)
                for v in range(2):
                    for half in range(2):
                        g = N_GT + 60 + 30 * half + NCMP * v
                        last = mm(psum[0:NCMP, 5, 64 * v:64 * v + 64], big[:, g:g + NCMP],
                                  aux[:, 384 + 64 * half:448 + 64 * half], half == 0, half == 1)
                last.then_inc(comp_pe, 1)

            def cmp_attention(s, k):
                for h in range(H):
                    p0, c = 64 * (h // 4), N_Q + (h % 4) * T
                    for t in range(TT):
                        at = (2 * h + t) * 16
                        last = mm(psum[:, (0, 7)[h // 4], at:at + NCMP], big[p0:p0 + 64, c + t * P:c + (t + 1) * P],
                                  big[p0:p0 + 64, N_KCMP:N_KCMP + NCMP], True, True)
                last.then_inc(cmp_pe, 1)
                pe.wait_ge(cmp_act, 2)
                for i in range(2 * H):
                    last = pe.transpose(psum[0:NCMP, 1 + i // 4, (i % 4) * P:(i % 4 + 1) * P],
                                        cS[:, i // 2, i % 2, 0:NCMP], ident)
                last.then_inc(cmp_pe, 1)
                pe.wait_ge(cmp_act, 3)
                for h in range(H):
                    for t in range(TT):
                        i = 2 * h + t
                        v = N_VCMP + 64 * (h // 4)
                        last = mm(psum[:, 5 + t, 64 * h:64 * h + 64], cPT[0:NCMP, i * P:(i + 1) * P],
                                  big[0:NCMP, v:v + 64], True, True)
                last.then_inc(cmp_pe, 1)

            def latent(s, k):
                pe.wait_ge(lat_dve, 1)
                for t in range(TT):
                    for i in range(2):
                        pe.transpose(psum[:, 0, i * T + t * P:i * T + (t + 1) * P],
                                     big_n(O_CQ, 256)[:, t, i * P:(i + 1) * P], ident)
                    last = pe.transpose(psum[:, 1, t * P:(t + 1) * P], big_n(O_CKV, P)[:, t, :], ident)
                last.then_inc(lat_pe, 1)
                pe.wait_ge(lat_dve, 2)
                n = PIECE0[s]
                piece_in(n)
                w = slot(n, (2, 768))
                for t in range(TT):
                    for lo, hi in ((0, 512), (512, 768)):
                        for i in range(2):
                            last = mm(psum[:, 2 + 2 * t + lo // 512, 0:hi - lo], cqT[:, i, t * P:(t + 1) * P],
                                      w[:, i, lo:hi], i == 0, i == 1)
                used(last, n)
                piece_in(n + 1)
                w = slot(n + 1, (1, 1024))
                for t in range(TT):
                    for half in range(2):
                        last = mm(psum[:, (6, 0)[t] + half, :], cqT[:, 2, t * P:(t + 1) * P],
                                  w[:, 0, half * 512:(half + 1) * 512], True, True)
                used(last, n + 1)
                pe.wait_ge(lat_act, 3)
                pe.wait_ge(lat_dve, 3)
                for h in range(MH):
                    for t in range(TT):
                        at = (h % 2) * T + t * P
                        pe.transpose(psum[:, 2 + h // 2, at:at + P], qm[:, t, h, 0:P], ident)
                        pe.transpose(psum[:, 4 + h // 2, at:at + P], vmla[:, t, h, 0:P], ident)
                        last = pe.transpose(psum[0:64, 6 + h // 2, at:at + P], qm[:, t, h, P:P + 64], ident)
                for t in range(TT):
                    last = pe.transpose(psum[0:64, 0, t * P:(t + 1) * P], big_n(O_KR, 64)[:, t, :], ident)
                last.then_inc(lat_pe, 1)

            def router(s, k):
                for t in range(TT):
                    for i in range(2 * KT):
                        kt, part = i // 2, xs[i % 2]
                        last = mm(psum[:, 0, E * t:E * t + E], part[:, kt, t * P:(t + 1) * P].bitcast(F32),
                                  small[:, S_RW + E * kt:S_RW + E * kt + E], i == 0, i == 2 * KT - 1)
                last.then_inc(route_pe, 1)
                pe.wait_ge(route_dve, 2 * k + 1)
                for t in range(TT):
                    last = pe.transpose(psum[0:E, 1, t * P:(t + 1) * P], route[:, E * t:E * t + E], ident)
                last.then_inc(route_pe, 1)
                pe.wait_ge(route_dve, 2 * k + 2)
                for e in range(E):
                    last = mm(psum[:, e // 2, (e % 2) * T:(e % 2 + 1) * T], spread(ident[0:E, e], 1, P),
                              route[0:E, 1024:1024 + T], True, True)
                last.then_inc(route_pe, 1)

            fns = {"setup": setup, "turn": turn, "ffn": ffn, "project": project, "outproj": outproj,
                   "stick": stick, "soft": soft_attention, "gates": gates, "mlstm": mlstm, "ada": ada,
                   "compress": compress, "cmp": cmp_attention, "latent": latent, "router": router}
            for s, (name, args, _) in enumerate(STAGES):
                if name in fns:
                    fns[name](s, INSTANCE[s], *args)
                boundary(pe, s + 1)

        @block.scalar
        def _(act):
            steps = [0]

            def link(ins):
                steps[0] += 1
                ins.then_inc(act_step, 1)
                act.wait_ge(act_step, steps[0])

            def high_part(n, shape, i=None):
                act.wait_ge(loaded[n % RING], slot_count(n) if i is None
                            else i * (16 * LOOP // RING) + slot_count(n))
                if n >= PARTS:
                    v = n - PARTS + 1
                    act.wait_ge(piece_used, v if i is None else i * LOOP + v)
                w = shape[0] * shape[1]
                act.activation(wh[n % PARTS][:, 0:w], ring[n % RING][:, 0:w], ACT.Copy).then_inc(high, 1)

            def root_mean(ss, n):
                return act.activation(ss, ss, ACT.Sqrt, scale=1.0 / n, bias=const[:, C_EPS:C_EPS + 1])

            def setup(s, k):
                act.wait_ge(setup_dve, 1)
                act.activation(small[:, S_R:S_R + 8], small[:, S_R:S_R + 8], ACT.Silu).then_inc(setup_act, 1)
                act.wait_ge(rows_ready, 1)
                for i in range(3):
                    act.dma_start(rowbuf[i], spread(wide[0:8, 0, i, :], 1, P)).then_inc(rows_out, 16)
                act.wait_ge(setup_dve, 2)
                act.activation(wide_at(3840, 2048), wide_at(3840, 2048), ACT.Exp).then_inc(setup_act, 1)
                act.wait_ge(rows_out, 48)

            def norm(s, k, m):
                for t in range(TT):
                    link(act.activation(nrm[:, t, :], x[:, t, :], ACT.Square, accum_out=stat[:, t:t + 1]))
                    root_mean(stat[:, t:t + 1], D).then_inc(squared, 1)

            def turn(s, k):
                for q in range(4):
                    f = 4 * (q % 2)
                    act.wait_ge(turned, 4 * k + q + 1)
                    act.activation(xh[:, f:f + 4, (q // 2) * P:(q // 2 + 1) * P],
                                   psum[:, q, :].rearrange("p (a b) -> p a b", a=4), ACT.Copy).then_inc(turn_high, 1)

            def ffn(s, k, chunks, moe):
                n0 = PIECE0[s]
                c0, h0 = ffn_bases(k)
                n = 4 if moe else 3

                def high_of(which, c, i=None):
                    high_part(chunk_piece(n0, which, c, chunks), DN if which == "d" else GU, i)

                def silu_of_gate(c, i=None):
                    v = chunk_piece(n0, "g", c, chunks) + 1
                    act.wait_ge(piece_used, v if i is None else i * LOOP + v)
                    if c >= 2:
                        v = h0 + n * (c - 1)
                        act.wait_ge(hidden, v if i is None else i * (2 * n) + v)
                    act.activation(hT[c % 2][:, :, :], psum[:, GB + c % 2, :].rearrange("p (f t) -> p f t", f=2),
                                   ACT.Silu).then_inc(gated, 1)

                def step(c, i=None):
                    if c + 1 < chunks:
                        high_of("g", c + 1, i)
                        high_of("u", c + 1, i)
                    silu_of_gate(c, i)
                    high_of("d", c, i)

                high_of("g", 0)
                high_of("u", 0)
                for c in range(4 if moe else 3):
                    step(c)
                first = 4 if moe else 3
                pairs = (chunks - 1 - first) // 2
                with act.Fori(0, pairs) as i:
                    step(first, i)
                    step(first + 1, i)
                for c in range(first + 2 * pairs, chunks):
                    step(c)

            def project(s, k, name):
                widths = {"attn": ATTN_IN, "mlstm": MLSTM_IN, "even": EVEN_IN, "odd": ODD_IN}[name]
                for j in range(2):
                    high_part(PIECE0[s] + j, (KT, widths[j]))
                for j, pieces in enumerate(PROJ[name]):
                    if j + 2 < len(widths):
                        high_part(PIECE0[s] + j + 2, (KT, widths[j + 2]))
                    act.wait_ge(piece_used, PIECE0[s] + j + 1)
                    b, at = j % 4, 0
                    for kind, c, m, dst, scale in pieces:
                        if kind == "N":
                            src = psum[:, b, at:at + TT * m].rearrange("p (t w) -> p t w", t=TT)
                            at += TT * m
                        elif kind == "V":
                            src = psum[:, b, 0:512].rearrange("p (t h w) -> p t h w", t=TT, h=2)
                        elif kind == "TT":
                            src = psum[:, b, 0:512]
                        elif kind == "T":
                            src = psum[0:m, b, at:at + T]
                            at += T
                        else:
                            dst = dst.rearrange("p (i o t) -> p i o t", i=2, o=2)
                            src = psum[64:P, b, :].rearrange("p (i t) -> p i t", i=2)
                            act.activation(dst[:, :, 1, :], src, ACT.Copy, scale=scale)
                            dst, src = dst[:, :, 0, :], psum[0:64, b, :].rearrange("p (i t) -> p i t", i=2)
                        last = act.activation(dst, src, ACT.Copy, scale=scale)
                    last.then_inc(proj_read, 1)

            def outproj(s, k):
                for j in range(4):
                    high_part(PIECE0[s] + j, GU)

            def ada(s, k):
                act.wait_ge(mod_done, k + 1)
                act.dma_start(modrow[k:k + 1, :], mod_row).then_inc(mod_out, 16)
                act.wait_ge(mod_out, 16 * (k + 1))

            def residual(s, k, kind, coef):
                if kind == "norm":
                    for t in range(TT):
                        link(act.activation(nrm[:, t, :], psum[:, 2 * t:2 * t + 2, :].rearrange("p b w -> p (b w)"),
                                            ACT.Square, accum_out=stat[:, t:t + 1]))
                        root_mean(stat[:, t:t + 1], D).then_inc(squared, 1)

            def stick(s, k):
                for h in range(H):
                    act.wait_ge(stick_dve, h + 1)
                    link(act.activation(wide[:, 1, h, :], wide[:, 0, h, :], ACT.Abs))
                    link(act.activation(wide[:, 1, h, :], wide[:, 1, h, :], ACT.Exp, scale=-1.0))
                for h in range(H):
                    act.activation(wide[:, 1, h, :], wide[:, 1, h, :], ACT.Ln, bias=ones).then_inc(stick_act, 1)
                for h in range(H):
                    act.wait_ge(stick_dve, 4 * H + h + 1)
                    act.activation(wide[:, 0, h, :], wide[:, 0, h, :], ACT.Exp).then_inc(stick_act, 1)
                act.wait_ge(stick_pe, 2 * H + 1)
                for t in range(TT):
                    act.activation(nrm[:, t, 0:512], psum[:, 4 + t, :], ACT.Copy)

            def soft_attention(s, k, name):
                a = SOFT[name]
                for h in range(a["heads"]):
                    act.wait_ge(biased, a["step0"] + a["steps"] * (h + 1))
                    for t, (lo, hi) in enumerate(((0, P), (P, W3))):
                        i = 2 * h + t
                        act.activation(wide[:, 0, h, lo:hi], wide[:, 0, h, lo:hi], ACT.Exp,
                                       bias=small[:, S_NMX + i:S_NMX + i + 1],
                                       accum_out=small[:, S_SUM + i:S_SUM + i + 1]).then_inc(expd, 1)
                if a["pad"] is not None:
                    act.wait_ge(pad_dve, PADDED.index(name) + 1)
                    act.activation(small[:, S_R:S_R + 16], small[:, S_R:S_R + 16], ACT.Exp).then_inc(pad_act, 1)

            def gates(s, k):
                act.wait_ge(gates_dve, 2)
                link(act.activation(aux[0:8, A_L:A_L + T], aux[0:8, A_F:A_F + T], ACT.Abs))
                link(act.activation(aux[0:8, A_L:A_L + T], aux[0:8, A_L:A_L + T], ACT.Exp, scale=-1.0))
                act.activation(aux[0:8, A_L:A_L + T], aux[0:8, A_L:A_L + T], ACT.Ln, bias=ones[0:8, :])\
                    .then_inc(gates_act, 1)
                act.wait_ge(gates_dve, 8)
                act.activation(aux[0:8, A_F:A_F + T], aux[0:8, A_F:A_F + T], ACT.Exp, scale=-1.0)\
                    .then_inc(gates_act, 1)
                for j in range(4):
                    act.wait_ge(gates_dve, 8 + 48 + 4 * (j + 1))
                    act.activation(wide_flat[:, 1024 * j:1024 * (j + 1)], wide_flat[:, 1024 * j:1024 * (j + 1)],
                                   ACT.Silu)
                act.activation(o_flat, o_flat, ACT.Sigmoid)

            def mlstm(s, k):
                def outputs(h):
                    act.wait_ge(ml_pe, 3 * h + 5 if h < H - 1 else 3 * H)
                    act.activation(raw[:, :, h, :], psum[:, 4 + h % 2, 0:2 * VW].rearrange("p (t w) -> p t w", t=TT),
                                   ACT.Copy).then_inc(ml_act, 1)

                for h in range(H):
                    act.wait_ge(ml_dve, 4 * h + 2)
                    act.activation(mE[h % 2], mE[h % 2], ACT.Exp, scale=-1.0).then_inc(ml_act, 1)
                    if h >= 1:
                        outputs(h - 1)
                outputs(H - 1)
                act.wait_ge(ml_dve, 4 * H + 1)
                root_mean(small[:, S_DEN:S_DEN + 16], P).then_inc(ml_act, 1)

            def compress(s, k):
                act.wait_ge(piece_used, PIECE0[s] + 4)
                act.activation(big[0:30, N_U:N_U + 512].rearrange("p (a b) -> p a b", a=2), psum[0:30, 1:3, 0:256],
                               ACT.Gelu_apprx_tanh).then_inc(comp_act, 1)

            def cmp_attention(s, k):
                act.activation(gview(S_G), gview(S_G), ACT.Sigmoid).then_inc(cmp_act, 1)
                act.wait_ge(cmp_dve, 1)
                act.activation(cS, cS, ACT.Exp).then_inc(cmp_act, 1)
                act.wait_ge(cmp_pe, 2)
                act.activation(cPT[0:NCMP, :], psum[0:NCMP, 1:5, :].rearrange("p b w -> p (b w)"), ACT.Copy)\
                    .then_inc(cmp_act, 1)

            def latent(s, k):
                for t in range(TT):
                    act.activation(nrm[:, t, 0:256], big_n(O_CQ, 256)[:, t, :], ACT.Square,
                                   accum_out=stat[:, t:t + 1])
                    last = act.activation(nrm[:, t, 256:384], big_n(O_CKV, P)[:, t, :], ACT.Square,
                                          accum_out=stat[:, 2 + t:3 + t])
                link(last)
                root_mean(stat[:, 0:2], 256)
                root_mean(stat[:, 2:4], P).then_inc(lat_act, 1)
                n = PIECE0[s]
                act.wait_ge(piece_used, n + 1)
                for t in range(TT):
                    last = act.activation(qm[:, t, :, :], psum[:, 2 + 2 * t:4 + 2 * t, :]
                                          .rearrange("p b w -> p (b w)")[:, 0:768].rearrange("p (h w) -> p h w", h=MH),
                                          ACT.Copy)
                last.then_inc(lat_act, 1)
                act.wait_ge(piece_used, n + 2)
                for t in range(TT):
                    b = (6, 0)[t]
                    last = act.activation(big_n(O_KVM, 1024)[:, t, :],
                                          psum[:, b:b + 2, :].rearrange("p b w -> p (b w)"), ACT.Copy)
                last.then_inc(lat_act, 1)
                act.wait_ge(lat_pe, 2)
                act.activation(big[:, O_QNT:O_QNT + 1024], psum[:, 2:4, :].rearrange("p b w -> p (b w)"), ACT.Copy)
                act.activation(big[:, O_KNT:O_KNT + 1024], psum[:, 4:6, :].rearrange("p b w -> p (b w)"), ACT.Copy)

            def router(s, k):
                act.wait_ge(route_pe, 3 * k + 1)
                act.activation(route[:, 0:2 * E], psum[:, 0, 0:2 * E], ACT.Sigmoid).then_inc(route_act, 1)
                act.wait_ge(route_pe, 3 * k + 3)
                act.activation(big[:, 0:2048], psum[:, 0:4, :].rearrange("p b w -> p (b w)"), ACT.Copy)

            def final(s, k):
                norm(s, k, None)

            ones = const[:, C_ONES:C_ONES + 1]
            fns = {"setup": setup, "norm": norm, "turn": turn, "ffn": ffn, "project": project,
                   "outproj": outproj, "ada": ada, "residual": residual, "stick": stick, "soft": soft_attention, "gates": gates,
                   "mlstm": mlstm, "compress": compress, "cmp": cmp_attention, "latent": latent,
                   "router": router, "final": final}
            for s, (name, args, _) in enumerate(STAGES):
                if name in fns:
                    fns[name](s, INSTANCE[s], *args)
                boundary(act, s + 1)
            act.dma_start(out.rearrange("(t p) d -> p t d", p=P), nrm[:, :, :]).then_inc(out_done, 16)
            act.wait_ge(out_done, 16)

        @block.vector
        def _(dve):
            steps = [0]

            def link(ins):
                steps[0] += 1
                ins.then_inc(dve_step, 1)
                dve.wait_ge(dve_step, steps[0])

            def mark(ins, signal, value):
                ins.then_inc(signal, 1)
                dve.wait_ge(signal, value)

            def tt(out_, a, b, op):
                return dve.tensor_tensor(out_, a, b, op)

            def setup(s, k):
                dve.wait_ge(setup_pe, 1)
                c = small[:, S_R:S_R + 8]
                dve.tensor_copy(c, psum[:, 0, 0:8]).then_inc(setup_dve, 1)
                dil, rel, swa = (big[0:8, (2 + i) * W3:(3 + i) * W3] for i in range(3))
                tt(wide[0:8, 0, 0, :], psum[0:8, 1, 0:W3], dil, ALU.add)
                tt(wide[0:8, 0, 1, :], psum[0:8, 2, 0:W3], rel, ALU.add)
                tt(wide[0:8, 0, 2, :], psum[0:8, 2, 0:W3], swa, ALU.add).then_inc(rows_ready, 1)
                dve.wait_ge(setup_act, 1)
                dve.tensor_copy(ccol[:, :], c)
                link(dve.tensor_copy(pad_b[0], psum[0:8, 3, :]))
                link(tt(pad_b[1], psum[0:8, 3, :], big[0:8, R_PADMASK:R_PADMASK + 512], ALU.add))
                sink = aux[0:8, 144:145]
                dve.memset(pad_m[0][:, 0:1], NEG)
                link(dve.tensor_copy(pad_m[1][:, 0:1], sink))
                for b, m, first in zip(pad_b, pad_m, (NEG, sink)):
                    link(dve.tensor_tensor_scan(m[:, 1:513], b, b, first, ALU.max, ALU.max))
                for i in range(2):
                    tt(pad_a[i], pad_m[i][:, 0:512], pad_m[i][:, 1:513], ALU.subtract)
                    ins = tt(pad_e[i], pad_b[i], pad_m[i][:, 1:513], ALU.subtract)
                ins.then_inc(setup_dve, 1)
                dve.wait_ge(setup_act, 2)
                for i in range(2):
                    ins = dve.tensor_tensor_scan(pad_b[i], pad_a[i], pad_e[i], float(i), ALU.mult, ALU.add)
                ins.then_inc(setup_dve, 1)
                dve.wait_ge(setup_pe, 2)
                mark(dve.tensor_copy(small[:, S_PAD:S_PAD + 64], psum[:, 4, 0:64]), setup_dve, 4)
                dve.wait_ge(setup_pe, 3)
                link(dve.tensor_copy(small[:, S_PAD:S_PAD + 64], psum[:, 5, 0:64]))
                for i in range(2):
                    m = small[:, S_PAD + 32 * i:S_PAD + 32 * i + 16]
                    dve.tensor_scalar(m, m, -1.0, None, ALU.mult)

            def norm(s, k, m):
                g = GAIN0[s]
                wait_gain(dve, g)
                scale, shift = gain[(g + 1) % GAINBUFS], gain[(g + 2) % GAINBUFS]
                for t in range(TT):
                    dve.wait_ge(squared, SQ0[s] + t + 1)
                    link(dve.reciprocal(stat[:, t:t + 1], stat[:, t:t + 1]))
                    ins = dve.scalar_tensor_tensor(out=nrm[:, t, :], in0=x[:, t, :], scalar=stat[:, t:t + 1],
                                                   in1=gain[g % GAINBUFS][:, :], op0=ALU.mult, op1=ALU.mult)
                    if m is None and t == TT - 1:
                        mark(ins, gain_used, g + 1)
                    else:
                        link(ins)
                    if m is not None:
                        if t == 0:
                            wait_gain(dve, g + 1)
                            wait_gain(dve, g + 2)
                        link(dve.scalar_tensor_tensor(out=nrm[:, t, :], in0=scale[:, :], scalar=1.0,
                                                      in1=nrm[:, t, :], op0=ALU.add, op1=ALU.mult))
                        link(tt(nrm[:, t, :], nrm[:, t, :], shift[:, :], ALU.add))
                if m is not None:
                    for _ in range(3):
                        dve.nop().then_inc(gain_used, 1)

            def turn(s, k):
                for q in range(4):
                    f = 4 * (q % 2)
                    place = (slice(0, P), slice(f, f + 4), slice((q // 2) * P, (q // 2 + 1) * P))
                    dve.wait_ge(turn_high, 4 * k + q + 1)
                    tt(xl[place], psum[:, q, :].rearrange("p (a b) -> p a b", a=4), xh[place].bitcast(F32),
                       ALU.subtract)

            def low_part(s, n, shape, i=None):
                v = SPLIT0[s] + n - PIECE0[s] + 1
                dve.wait_ge(high, v if i is None else i * LOOP + v)
                w = shape[0] * shape[1]
                tt(wl[n % PARTS][:, 0:w], ring[n % RING][:, 0:w], wh[n % PARTS][:, 0:w].bitcast(F32), ALU.subtract)\
                    .then_inc(freed, 1)

            def outproj(s, k):
                for j in range(4):
                    low_part(s, PIECE0[s] + j, GU)

            def project(s, k, name):
                widths = {"attn": ATTN_IN, "mlstm": MLSTM_IN, "even": EVEN_IN, "odd": ODD_IN}[name]
                for j, width in enumerate(widths):
                    low_part(s, PIECE0[s] + j, (KT, width))

            def ffn(s, k, chunks, moe):
                n0 = PIECE0[s]
                c0, h0 = ffn_bases(k)
                n = 4 if moe else 3

                def hidden_features(c, i=None, e=None):
                    def at(v, per_pair):
                        return v if i is None else i * per_pair + v

                    h, v = hT[c % 2][:, :, :], h0 + n * c
                    up = psum[:, UB + c % 2, :].rearrange("p (f t) -> p f t", f=2)
                    dve.wait_ge(gated, at(c0 + c + 1, 2))
                    dve.wait_ge(piece_used, at(chunk_piece(n0, "u", c, chunks) + 1, LOOP))
                    tt(h, h, up, ALU.mult).then_inc(hidden, 1)
                    if moe:
                        dve.wait_ge(hidden, at(v + 1, 2 * n))
                        tt(h, h, spread(routing[:, e, :], 1, 2), ALU.mult).then_inc(hidden, 1)
                    dve.wait_ge(hidden, at(v + n - 2, 2 * n))
                    if c >= 2:
                        dve.wait_ge(piece_used, at(chunk_piece(n0, "d", c - 2, chunks) + 1, LOOP))
                    dve.tensor_copy(hh[c % 2][:, :, :], h).then_inc(hidden, 1)
                    dve.wait_ge(hidden, at(v + n - 1, 2 * n))
                    tt(hl[c % 2][:, :, :], h, hh[c % 2][:, :, :].bitcast(F32), ALU.subtract).then_inc(hidden, 1)

                def low_of(which, c, i=None):
                    low_part(s, chunk_piece(n0, which, c, chunks), DN if which == "d" else GU, i)

                def step(c, i=None, e=None):
                    if c + 1 < chunks:
                        low_of("g", c + 1, i)
                        low_of("u", c + 1, i)
                    hidden_features(c, i, e)
                    low_of("d", c, i)

                low_of("g", 0)
                low_of("u", 0)
                first = 4 if moe else 3
                for c in range(first):
                    step(c, None, c // EC)
                pairs = (chunks - 1 - first) // 2
                with dve.Fori(0, pairs) as i:
                    step(first, i, i + first // EC)
                    step(first + 1, i, i + first // EC)
                for c in range(first + 2 * pairs, chunks):
                    step(c, None, c // EC)

            def residual(s, k, kind, coef):
                dve.wait_ge(piece_used, PIECE0[s])
                g = GAIN0[s]
                wait_gain(dve, g)
                factor = gain[g % GAINBUFS][:, :]
                for t in range(TT):
                    y = psum[:, 2 * t:2 * t + 2, :].rearrange("p b w -> p (b w)")
                    if kind == "norm":
                        dve.wait_ge(squared, SQ0[s] + t + 1)
                        link(dve.reciprocal(stat[:, t:t + 1], stat[:, t:t + 1]))
                        ins = dve.scalar_tensor_tensor(out=nrm[:, t, :], in0=y, scalar=stat[:, t:t + 1],
                                                       in1=factor, op0=ALU.mult, op1=ALU.mult)
                    else:
                        ins = tt(nrm[:, t, :], y, factor, ALU.mult)
                    if t == TT - 1:
                        mark(ins, gain_used, g + 1)
                    else:
                        link(ins)
                    if kind == "norm":
                        dve.scalar_tensor_tensor(out=x[:, t, :], in0=nrm[:, t, :], scalar=coef, in1=x[:, t, :],
                                                 op0=ALU.mult, op1=ALU.add)
                    else:
                        tt(x[:, t, :], x[:, t, :], nrm[:, t, :], ALU.add)

            def stick(s, k):
                for h in range(H):
                    dve.wait_ge(stick_pe, h + 1)
                    dve.tensor_copy(wide[:, 0, h, :], psum[:, h % 2, 0:W3]).then_inc(stick_dve, 1)
                for h in range(H):
                    z, sp_h = wide[:, 0, h, :], wide[:, 1, h, :]
                    at = H + 3 * h
                    dve.wait_ge(stick_act, h + 1)
                    mark(dve.scalar_tensor_tensor(out=sp_h, in0=z, scalar=0.0, in1=sp_h, op0=ALU.max, op1=ALU.add),
                         stick_dve, at + 1)
                    mark(tt(z, z, sp_h, ALU.subtract), stick_dve, at + 2)
                    mark(tt(sp_h, sp_h, const[:, C_MSTRICT:C_MSTRICT + W3], ALU.mult), stick_dve, at + 3)
                for h in range(H):
                    dve.wait_ge(stick_pe, H + h + 1)
                    tt(wide[:, 0, h, :], wide[:, 0, h, :], psum[:, 2 + h % 2, 0:W3], ALU.subtract)\
                        .then_inc(stick_dve, 1)
                for h in range(H):
                    dve.wait_ge(stick_act, H + h + 1)
                    tt(wide[:, 0, h, :], wide[:, 0, h, :], const[:, C_MSTRICT:C_MSTRICT + W3], ALU.mult)\
                        .then_inc(stick_dve, 1)

            def soft_attention(s, k, name):
                a = SOFT[name]
                h0, s0, n, heads, dv = a["head0"], a["step0"], a["steps"], a["heads"], a["dv"]
                if a["bias"]:
                    dve.wait_ge(bias_in, {"dilated": 32, "sliding": 96}.get(name, 64))

                def scores(h):
                    S, at = wide[:, 0, h, :], s0 + n * h
                    add = biasT[:, h, :] if a["bias"] else const[:, C_CAUSAL:C_CAUSAL + W3]
                    dve.wait_ge(score, h0 + h + 1)
                    mark(dve.scalar_tensor_tensor(out=S, in0=psum[:, h % 2, 0:W3], scalar=a["scale"], in1=add,
                                                  op0=ALU.mult, op1=ALU.add), biased, at + 1)
                    for t, (lo, hi) in enumerate(((0, P), (P, W3))):
                        i = S_NMX + 2 * h + t
                        mark(dve.tensor_reduce(small[:, i:i + 1], S[:, lo:hi], AX.X, ALU.max, negate=True),
                             biased, at + 2 + t)
                    if a["pad"] is not None:
                        for t in range(TT):
                            i, m = S_NMX + 2 * h + t, a["pad"] + 8 * t + h
                            mark(tt(small[:, i:i + 1], small[:, i:i + 1], small[:, m:m + 1], ALU.min), biased, at + 4 + t)

                def probs(h):
                    dve.wait_ge(p_turned, h0 + h + 1)
                    if h >= 2:
                        dve.wait_ge(headout, h0 + h - 1)
                    dve.tensor_copy(PT[h % 2][:, :], psum[:, 2 + h % 2, 0:W3]).then_inc(p_read, 1)

                scores(0)
                scores(1)
                for h in range(heads):
                    if h + 2 < heads:
                        scores(h + 2)
                    probs(h)
                dve.wait_ge(expd, 2 * (h0 + heads))
                cols_ = 2 * heads
                sums = small[:, S_SUM:S_SUM + cols_].rearrange("p (h t) -> p h t", t=TT)
                inv = small[:, S_INV:S_INV + cols_].rearrange("p (h t) -> p h t", t=TT)
                nmx = small[:, S_NMX:S_NMX + cols_].rearrange("p (h t) -> p h t", t=TT)
                tmp = small[:, S_R:S_R + 16].rearrange("p (h t) -> p h t", t=TT)
                if a["pad"] is not None:
                    m, total = (small[:, c:c + 16].rearrange("p (t h) -> p h t", t=TT) for c in (a["pad"], a["pad"] + 16))
                    n_pad = PADDED.index(name) + 1
                    tt(tmp, nmx, m, ALU.subtract).then_inc(pad_dve, 1)
                    dve.wait_ge(pad_act, n_pad)
                    link(tt(tmp, tmp, total, ALU.mult))
                    link(tt(sums, sums, tmp, ALU.add))
                link(dve.reciprocal(inv, sums))
                if a["gate"] is not None:
                    link(tt(inv, inv, gate_of(a["gate"]), ALU.mult))
                dve.wait_ge(headout, h0 + heads)
                for t in range(TT):
                    y = psum[:, 4 + t, :].rearrange("p (h w) -> p h w", h=heads)
                    o = nrm[:, t, a["dst"]:a["dst"] + 512].rearrange("p (h w) -> p h w", h=heads)
                    f = spread(inv[:, :, t], 2, dv)
                    if a["gate"] is None:
                        tt(o, y, f, ALU.mult)
                    else:
                        part = wide_flat[:, 3072 + 512 * t:3584 + 512 * t].rearrange("p (h w) -> p h w", h=heads)
                        link(tt(part, y, f, ALU.mult))
                        tt(o, o, part, ALU.add)

            def gate_of(c):
                return gview(S_G).rearrange("p t (h c) -> p h t c", c=3)[:, :, :, c]

            def gates(s, k):
                I_, F_, L_, B_, G_ = (aux[0:8, at:at + T] for at in (A_I, A_F, A_L, A_B, A_G))
                dve.memset(vM[:, :, :, P:VW], 1.0)
                dve.wait_ge(gates_pe, 1)
                mark(dve.tensor_copy(small[:, S_CONVW:S_CONVW + 64], psum[:, 0, 0:64]), gates_dve, 1)
                dve.tensor_copy(I_, psum[0:8, 2, 0:T])
                mark(dve.tensor_scalar(F_, psum[0:8, 3, 0:T], aux[0:8, 1:2], None, ALU.add), gates_dve, 2)
                dve.wait_ge(gates_act, 1)
                mark(dve.tensor_scalar(F_, F_, 0.0, None, ALU.min), gates_dve, 3)
                mark(tt(F_, F_, L_, ALU.subtract), gates_dve, 4)
                mark(dve.tensor_tensor_scan(B_, const[0:8, C_ONES:C_ONES + 1].to_broadcast([8, T]), F_, 0.0,
                                            ALU.mult, ALU.add), gates_dve, 5)
                mark(dve.scalar_tensor_tensor(out=G_, in0=I_, scalar=aux[0:8, 0:1], in1=B_, op0=ALU.add,
                                              op1=ALU.subtract), gates_dve, 6)
                mark(dve.tensor_tensor_scan(L_, G_, G_, 0.0, ALU.max, ALU.max), gates_dve, 7)
                mark(tt(F_, B_, L_, ALU.add), gates_dve, 8)
                for tap in range(4):
                    for m in range(16):
                        w = small[:, S_CONVW + 16 * (3 - tap) + m:S_CONVW + 16 * (3 - tap) + m + 1]
                        src = big_t(M_PRE, m)
                        if tap:
                            dve.wait_ge(gates_dve, 8 + 16 * (tap - 1) + m + 1)
                            dve.scalar_tensor_tensor(out=cv[:, m, tap:T], in0=src[:, 0:T - tap], scalar=w,
                                                     in1=cv[:, m, tap:T], op0=ALU.mult, op1=ALU.add)\
                                .then_inc(gates_dve, 1)
                        else:
                            dve.tensor_scalar(cv[:, m, :], src, w, None, ALU.mult).then_inc(gates_dve, 1)
                dve.wait_ge(gates_pe, 2)
                dve.tensor_copy(small[:, S_COL:S_COL + 32], psum[:, 1, 0:32])

            def mlstm(s, k):
                scale = 1.0 / math.sqrt(P)
                for h in range(H):
                    e = mE[h % 2]
                    col = [small[:, S_COL + 8 * t + h:S_COL + 8 * t + h + 1] for t in range(TT)]
                    dve.wait_ge(ml_pe, 3 * h if h else 1)
                    dve.tensor_scalar(e[:, 0:T], psum[:, h % 2, 0:T], col[0], 0.0, ALU.subtract, ALU.max)\
                        .then_inc(ml_dve, 1)
                    dve.tensor_scalar(e[:, T:W3], psum[:, h % 2, P:T], col[1], 0.0, ALU.subtract, ALU.max)\
                        .then_inc(ml_dve, 1)
                    dve.wait_ge(ml_act, 2 * h if h else 1)
                    mark(tt(e, e, const[:, C_MINCL:C_MINCL + W3], ALU.mult), ml_dve, 4 * h + 3)
                    dve.wait_ge(ml_pe, 3 * h + 1 if h else 2)
                    if h >= 2:
                        dve.wait_ge(ml_pe, 3 * (h - 2) + 5)
                    dve.scalar_tensor_tensor(out=PT[h % 2][:, :], in0=psum[:, 2 + h % 2, 0:W3], scalar=scale, in1=e,
                                             op0=ALU.mult, op1=ALU.mult).then_inc(ml_dve, 1)
                dve.wait_ge(ml_act, 2 * H)
                den = small[:, S_DEN:S_DEN + 16].rearrange("p (t h) -> p t h", t=TT)
                thr = small[:, S_THR:S_THR + 16].rearrange("p (t h) -> p t h", t=TT)
                n_num = raw[:, :, :, P]
                link(dve.scalar_tensor_tensor(out=den, in0=n_num, scalar=-1.0, in1=n_num, op0=ALU.mult, op1=ALU.max))
                link(tt(den, den, thr, ALU.max))
                link(dve.reciprocal(den, den))
                sq = wide_flat[:, 0:2048].rearrange("p (t h w) -> p t h w", t=TT, h=H)
                g = GAIN0[s]
                wait_gain(dve, g)
                for t in range(TT):
                    link(tt(hid[:, t], raw[:, t, :, 0:P], spread(den[:, t, :], 2, P), ALU.mult))
                for t in range(TT):
                    link(tt(sq[:, t], hid[:, t], hid[:, t], ALU.mult))
                dve.tensor_reduce(den[:, 0, :], sq[:, 0], AX.X, ALU.add)
                dve.tensor_reduce(den[:, 1, :], sq[:, 1], AX.X, ALU.add).then_inc(ml_dve, 1)
                dve.wait_ge(ml_act, 2 * H + 1)
                link(dve.reciprocal(den, den))
                for t in range(TT):
                    link(tt(hid[:, t], hid[:, t], spread(den[:, t, :], 2, P), ALU.mult))
                for t in range(TT):
                    ins = tt(nrm[:, t, :], nrm[:, t, :], gain[g % GAINBUFS][:, :], ALU.mult)
                    if t == TT - 1:
                        mark(ins, gain_used, g + 1)
                    else:
                        link(ins)
                tt(nrm[:, :, :], nrm[:, :, :], oM, ALU.mult)

            def ada(s, k):
                n0 = PIECE0[s]
                for _ in range(2):
                    dve.nop().then_inc(ada_read, 1)
                dve.wait_ge(mod_in, 16 * (k + 1))
                with dve.Fori(0, 4) as i:
                    for r in range(LOOP):
                        dve.wait_ge(piece_used, i * LOOP + (n0 + r + 1))
                        m = wide_flat[0:1, bass.ds(i * (LOOP * 256) + r * 256, 256)]
                        tt(m, m, psum[0:1, r % 2, 0:256], ALU.add).then_inc(ada_read, 1)
                dve.wait_ge(ada_read, 26 * (k + 1))
                dve.nop().then_inc(mod_done, 1)

            def compress(s, k):
                pos = big[:, N_POS:N_POS + 64]
                dve.wait_ge(comp_pe, 1)
                mark(dve.tensor_copy(pos, psum[:, 0, 0:64]), comp_dve, 1)
                for i, at in enumerate((N_KC, N_VC)):
                    for v in range(2):
                        for odd in range(2):
                            p0 = 64 * v
                            part = big[p0:p0 + 64, at + odd:at + odd + 1]
                            tokens = bass.AP(part.tensor, part.offset, [list(part.ap[0]), [2, 16], [16, NCMP]])
                            place = pos[p0:p0 + 64, 32 * i + odd:32 * i + 32:2]
                            tt(blocksF[i][64 * odd:64 * odd + 64, :, v, :], tokens, spread(place, 2, NCMP), ALU.add)\
                                .then_inc(comp_dve, 1)
                dve.wait_ge(comp_pe, 2)
                mark(dve.tensor_copy(big[:, N_GT:N_GT + 120], psum[:, 3, 0:120]), comp_dve, 10)
                dve.wait_ge(comp_pe, 3)
                dve.tensor_copy(big[:, N_KCMP:N_KCMP + NCMP], psum[:, 4, 0:NCMP])
                dve.tensor_copy(big[0:NCMP, N_VCMP:N_VCMP + P], psum[0:NCMP, 5, 0:P])

            def cmp_attention(s, k):
                dve.wait_ge(bias_in, 64)
                link(dve.memset(cS, NEG))
                dve.wait_ge(cmp_pe, 1)
                for v in range(2):
                    g = slice(4 * v, 4 * v + 4)
                    ps = psum[:, (0, 7)[v], 0:256].rearrange("p (h t n) -> p h t n", h=H, t=TT)
                    for t, n in ((0, 7), (1, NCMP)):
                        lo = P * t + 31
                        link(tt(cS[:, g, t, 0:n], ps[:, g, t, 0:n], biasT[:, g, lo:lo + 16 * (n - 1) + 1:16],
                                ALU.add))
                mx = small[:, S_NMX:S_NMX + 16].rearrange("p (h t) -> p h t", t=TT)
                sums = small[:, S_SUM:S_SUM + 16].rearrange("p (h t) -> p h t", t=TT)
                inv = small[:, S_INV:S_INV + 16].rearrange("p (h t) -> p h t", t=TT)
                link(dve.tensor_reduce(mx, cS, AX.X, ALU.max))
                link(dve.tensor_scalar(mx, mx, -1e20, None, ALU.max))
                for t in range(TT):
                    ins = tt(cS[:, :, t, :], cS[:, :, t, :], spread(mx[:, :, t], 2, 16), ALU.subtract)
                ins.then_inc(cmp_dve, 1)
                dve.wait_ge(cmp_act, 2)
                link(dve.tensor_reduce(sums, cS, AX.X, ALU.add))
                link(dve.tensor_scalar(sums, sums, 1e-30, None, ALU.max))
                link(dve.reciprocal(inv, sums))
                link(tt(inv, inv, gate_of(0), ALU.mult))
                dve.wait_ge(cmp_pe, 3)
                for t in range(TT):
                    tt(nrm[:, t, 0:512].rearrange("p (h w) -> p h w", h=H),
                       psum[:, 5 + t, :].rearrange("p (h w) -> p h w", h=H), spread(inv[:, :, t], 2, 64), ALU.mult)

            def rope(x_, t, tmp):
                heads = x_.shape[1] if len(x_.shape) == 3 else 0
                cos = const[:, C_COS + 32 * t:C_COS + 32 * t + 32]
                sin = const[:, C_SIN + 32 * t:C_SIN + 32 * t + 32]
                if heads:
                    cos, sin = spread(cos, 1, heads), spread(sin, 1, heads)
                    x1, x2 = x_[:, :, 0:32], x_[:, :, 32:64]
                else:
                    x1, x2 = x_[:, 0:32], x_[:, 32:64]
                tt(tmp[0], x1, cos, ALU.mult)
                tt(tmp[1], x2, sin, ALU.mult)
                tt(tmp[2], x1, sin, ALU.mult)
                link(tt(tmp[3], x2, cos, ALU.mult))
                tt(x1, tmp[0], tmp[1], ALU.subtract)
                return tt(x2, tmp[2], tmp[3], ALU.add)

            def latent(s, k):
                dve.wait_ge(lat_act, 1)
                link(dve.reciprocal(stat[:, 0:4], stat[:, 0:4]))
                dve.wait_ge(extra_in, EXTRA["odd"])
                for t in range(TT):
                    cq, ckv = big_n(O_CQ, 256)[:, t, :], big_n(O_CKV, P)[:, t, :]
                    dve.scalar_tensor_tensor(out=cq, in0=cq, scalar=stat[:, t:t + 1], in1=aux[:, 0:256],
                                             op0=ALU.mult, op1=ALU.mult)
                    ins = dve.scalar_tensor_tensor(out=ckv, in0=ckv, scalar=stat[:, 2 + t:3 + t], in1=aux[:, 256:384],
                                                   op0=ALU.mult, op1=ALU.mult)
                ins.then_inc(lat_dve, 1)
                dve.wait_ge(lat_pe, 1)
                dve.tensor_copy(cqT[:, 0:2, :], psum[:, 0, :].rearrange("p (a b) -> p a b", a=2))
                dve.tensor_copy(cqT[:, 2, :], psum[:, 1, 0:T]).then_inc(lat_dve, 1)
                for t in range(TT):
                    tmp = [hT[i // 2][:, i % 2, 32 * t:32 * t + 32] for i in range(4)]
                    last = rope(big_n(O_KR, 64)[:, t, :], t, tmp)
                link(last)
                dve.wait_ge(lat_act, 2)
                for t in range(TT):
                    tmp = [hT[t][:, i // 2, P * (i % 2):P * (i % 2) + P].rearrange("p (h w) -> p h w", h=MH)
                           for i in range(4)]
                    ins = rope(qm[:, t, :, P:P + 64], t, tmp)
                ins.then_inc(lat_dve, 1)
                dve.wait_ge(lat_pe, 2)
                dve.tensor_copy(aux[0:64, A_QRT:A_QRT + 1024], psum[0:64, 6:8, :].rearrange("p b w -> p (b w)"))
                dve.tensor_copy(aux[0:64, A_KRT:A_KRT + T], psum[0:64, 0, 0:T])

            def router(s, k):
                def at(a, *dims):
                    n = int(np.prod(dims))
                    names = "abc"[:len(dims)]
                    return route[:, a:a + n].rearrange(f"p ({' '.join(names)}) -> p {' '.join(names)}",
                                                       **dict(zip(names, dims)))

                aff, biased_ = at(0, 8, 4), at(64, 8, 4)
                gt, eq = at(128, 8, 4, 4), at(256, 8, 4, 4)
                sel, top, rank = at(384, 8, 4), at(448, 8, 4), at(512, 8, 4)
                group, grank = at(576, 2, 4), at(592, 2, 4)
                ggt, geq = at(608, 2, 4, 4), at(640, 2, 4, 4)
                total = at(672, 2)
                lower = const[:, C_LOWER:C_LOWER + 16].rearrange("p (a b) -> p a b", a=4)
                dve.wait_ge(route_act, k + 1)
                rb = small[:, S_RB:S_RB + E].rearrange("p (g e) -> p g e", g=4)
                for t in range(TT):
                    link(tt(biased_[:, 4 * t:4 * t + 4], aff[:, 4 * t:4 * t + 4], rb, ALU.add))

                def ranks(values, n, g_, e_, out_):
                    for j in range(4):
                        other = spread(values[:, :, j], 2, 4)
                        tt(g_[:, :, j, :], values, other, ALU.is_gt)
                        last = tt(e_[:, :, j, :], values, other, ALU.is_equal)
                    link(last)
                    link(tt(e_, e_, spread(lower, 1, n), ALU.mult))
                    link(tt(g_, g_, e_, ALU.add))
                    link(dve.tensor_reduce(out_, g_, AX.X, ALU.add))

                ranks(biased_, 8, gt, eq, rank)
                link(dve.tensor_scalar(sel, rank, 1.5, None, ALU.is_lt))
                link(tt(top, sel, biased_, ALU.mult))
                link(dve.tensor_reduce(group.rearrange("p a b -> p (a b)"), top, AX.X, ALU.add))
                ranks(group, 2, ggt, geq, grank)
                link(dve.tensor_scalar(grank, grank, 0.5, None, ALU.is_lt))
                link(tt(sel, sel, spread(grank.rearrange("p a b -> p (a b)"), 2, 4), ALU.mult))
                link(tt(aff, aff, sel, ALU.mult))
                link(dve.tensor_reduce(total, route[:, 0:32].rearrange("p (t e) -> p t e", t=TT), AX.X, ALU.add))
                link(dve.reciprocal(total, total))
                w = route[:, 0:32].rearrange("p (t e) -> p t e", t=TT)
                tt(w, w, spread(total, 2, E), ALU.mult).then_inc(route_dve, 1)
                dve.wait_ge(route_pe, 3 * k + 2)
                dve.tensor_copy(route[0:E, 1024:1024 + T], psum[0:E, 1, 0:T]).then_inc(route_dve, 1)
                dve.wait_ge(route_pe, 3 * k + 3)
                dve.tensor_copy(big[:, 2048:4096], psum[:, 4:8, :].rearrange("p b w -> p (b w)"))

            def final(s, k):
                norm(s, k, None)

            fns = {"setup": setup, "norm": norm, "turn": turn, "ffn": ffn, "project": project,
                   "outproj": outproj, "residual": residual, "stick": stick, "soft": soft_attention, "gates": gates,
                   "mlstm": mlstm, "ada": ada, "compress": compress, "cmp": cmp_attention,
                   "latent": latent, "router": router, "final": final}
            for s, (name, args, _) in enumerate(STAGES):
                if name in fns:
                    fns[name](s, INSTANCE[s], *args)
                boundary(dve, s + 1)


_INS = ['x', 'norm_g', 'ffn_w_gate', 'ffn_w_up', 'ffn_w_down', 'attn_w_in', 'attn_w_out', 'rel_bias',
        'mlstm_w_in', 'mlstm_b_gates', 'mlstm_conv_w', 'mlstm_head_g', 'mlstm_w_out', 'c_2', 'rel_table_2',
        'router_w_2', 'router_b_2', 'final_norm_2', 'norm_mix_2', 'norm_ffn_2', 'ada_w_2', 'ada_b_2',
        'moe_w_gate_2', 'moe_w_up_2', 'moe_w_down_2', 'ev_w_in_2', 'ev_w_out_2', 'nsa_pos_k_2', 'nsa_pos_v_2',
        'nsa_ck_w1_2', 'nsa_ck_w2_2', 'nsa_cv_w1_2', 'nsa_cv_w2_2', 'od_w_in_2', 'od_w_out_2', 'mla_q_norm_2',
        'mla_kv_norm_2', 'mla_w_q_up_2', 'mla_w_kv_up_2', 'swa_sinks_2']


def kernel(**inputs):
    import concourse.bacc as _bacc
    from concourse.bass_utils import run_bass_kernel_spmd as _run

    nc = _bacc.Bacc("TRN2", target_bir_lowering=False, num_devices=1)
    arrays = {name: np.ascontiguousarray(inputs[name]) for name in _INS}
    arrays["const"], arrays["rows"] = shape_constants()
    I = {name: nc.dram_tensor(f"in_{name}", a.shape, F32, kind="ExternalInput").ap() for name, a in arrays.items()}
    out = nc.dram_tensor("out_0_dram", (T, D), F32, kind="ExternalOutput").ap()
    build(nc, I, out)
    r = _run(nc, [{f"in_{name}": a for name, a in arrays.items()}], core_ids=[0])
    return r.results[0]["out_0_dram"].reshape(1, T, D)
```

```python
import math
from contextlib import ExitStack

import numpy as np

import concourse.bass as bass
from concourse import mybir

F32 = mybir.dt.float32
F32R = mybir.dt.float32r
ALU = mybir.AluOpType
ACT = mybir.ActivationFunctionType
AX = mybir.AxisListType

P = 128
T = 256
TT = T // P
D = 1024
KT = D // P
DH = 64
H = 8
FF = 2816
FC = FF // 256
E = 16
FE = 512
EC = FE // 256
W3 = 3 * P
NCMP = 15
NEG = -1e30
EPS = 1e-6
RING = 3
PARTS = 3
LOOP = 6
GAINBUFS = 4
SLOT = 2048
MH = 4
VW = P + 1



def bucket_table(max_distance, distances):
    d = np.maximum(distances, 0)
    scaled = np.log(np.maximum(d, 1).astype(np.float32) / np.float32(16)) / np.float32(math.log(max_distance / 16))
    log_part = 16 + (scaled * np.float32(16)).astype(np.int32)
    return np.where(d < 16, d, np.minimum(log_part, 31))


C_IDENT = 0
C_MSTRICT = C_IDENT + P
C_MINCL = C_MSTRICT + W3
C_CAUSAL = C_MINCL + W3
C_AFTER = C_CAUSAL + W3
C_ONES = C_AFTER + P
C_COS = C_ONES + P
C_SIN = C_COS + TT * 32
C_LOWER = C_SIN + TT * 32
C_EPS = C_LOWER + 16
C_FLIP = C_EPS + 1
NCONST = C_FLIP + P


def shape_constants():
    c = np.zeros((P, NCONST), np.float32)
    p, j = np.arange(P)[:, None], np.arange(T)[None, :]
    c[:, C_IDENT:C_IDENT + P] = np.eye(P)
    for at, mask in ((C_MSTRICT, j > p), (C_MINCL, j >= p)):
        c[:, at:at + T] = mask
        c[:, at + T:at + W3] = mask[:, :P]
    c[:, C_CAUSAL:C_CAUSAL + P] = np.where(j[:, :P] <= p, 0, NEG)
    c[:, C_CAUSAL + P:C_CAUSAL + W3] = np.where(j <= p + P, 0, NEG)
    c[:, C_AFTER:C_AFTER + P] = p > j[:, :P]
    c[:, C_ONES:C_ONES + P] = 1
    inv = np.float32(10000.0) ** (-np.arange(0, 64, 2, dtype=np.float32) / np.float32(64))
    angle = (np.arange(T, dtype=np.float32)[:, None] * inv[None, :]).reshape(TT, P, 32).transpose(1, 0, 2)
    c[:, C_COS:C_COS + TT * 32] = np.cos(angle).reshape(P, TT * 32)
    c[:, C_SIN:C_SIN + TT * 32] = np.sin(angle).reshape(P, TT * 32)
    a = np.arange(4)
    c[:, C_LOWER:C_LOWER + 16] = (a[None, :] < a[:, None]).reshape(1, 16)
    c[:, C_EPS] = EPS
    c[:, C_FLIP:C_FLIP + P] = np.eye(P)[::-1]
    d = 255 - np.arange(W3)
    count = (d <= 128) * 1 + (d % 4 == 0) * 1 + (d % 16 == 0) * 1
    count = np.where(d >= 0, count, 0)
    dil = np.where(count > 0, np.log(np.maximum(count, 1)), NEG)
    rel = np.where(d >= 0, 0, NEG)
    swa = np.where((d >= 0) & (d < 128), 0, NEG)
    rows = np.zeros((32, 5, W3), np.float32)
    rows[:, 0] = bucket_table(2048, d)[None, :] == np.arange(32)[:, None]
    rows[:, 1] = bucket_table(1024, d)[None, :] == np.arange(32)[:, None]
    rows[:, 2], rows[:, 3], rows[:, 4] = dil, rel, swa
    d = 511 - np.arange(512)
    pads = np.zeros((32, 2, 512), np.float32)
    pads[:, 0] = bucket_table(1024, d)[None, :] == np.arange(32)[:, None]
    pads[:, 1] = np.where(d < 128, 0, NEG)
    return c, np.concatenate([rows.reshape(32, 5 * W3), pads.reshape(32, 1024)], axis=1)


def spread(ap, axis, n):
    dims = [list(x) for x in ap.ap]
    return bass.AP(ap.tensor, ap.offset, dims[:axis] + [[0, n]] + dims[axis:])


def build(nc, I, out):
    ctx = ExitStack()
    with ctx:
        def sb(name, shape, dt=F32):
            return ctx.enter_context(nc.sbuf_tensor(name, shape, dt))

        def sem(name):
            return ctx.enter_context(nc.semaphore(name))

        ring = [sb(f"ring{i}", [P, SLOT]) for i in range(RING)]
        x = sb("x", [P, TT, D])
        nrm = sb("nrm", [P, TT, D])
        xh = sb("xh", [P, KT, T], F32R)
        xl = sb("xl", [P, KT, T], F32R)
        const = sb("const", [P, NCONST])
        gain = [sb(f"gain{i}", [P, D]) for i in range(GAINBUFS)]
        ccol = sb("ccol", [P, KT])
        biasT = sb("biasT", [P, H, W3])
        big = sb("big", [P, 8192])
        wide_addr = -(-nc.sbuf_base // 32) * 32
        wide = sb("wide", [P, 2, H, W3])
        hT = [sb(f"hT{i}", [P, 2, T]) for i in range(2)]
        hh = [sb(f"hh{i}", [P, 2, T], F32R) for i in range(2)]
        hl = [sb(f"hl{i}", [P, 2, T], F32R) for i in range(2)]
        PT = [sb(f"PT{i}", [P, W3]) for i in range(2)]
        small = sb("small", [P, 512])
        aux = sb("aux", [P, 1664])
        rw_high = sb("router_high", [P, P], F32R)
        rw_low = sb("router_low", [P, P], F32R)
        stat = sb("stat", [P, 8])
        psum = ctx.enter_context(nc.psum_tensor("psum", [P, 8, 512], F32))

        wh = [sb(f"wh{i}", [P, SLOT], F32R) for i in range(PARTS - 1)]
        wl = [sb(f"wl{i}", [P, SLOT], F32R) for i in range(PARTS - 1)]
        wh.append(nc.alloc_sbuf_tensor_at("wh2", [P, SLOT], F32R, offset=wide_addr))
        wl.append(nc.alloc_sbuf_tensor_at("wl2", [P, SLOT], F32R, offset=wide_addr + 4 * SLOT))

        modpart = nc.dram_tensor("adaln_parts", (2, 6, P, D), F32, kind="Internal").ap()
        rowbuf = nc.dram_tensor("bias_rows", (3, H, P, W3), F32, kind="Internal").ap()

        loaded = [sem(f"slot{i}_loaded") for i in range(RING)]
        piece_used = sem("piece_used")
        freed = sem("slot_freed")
        high = sem("high")
        crossed = sem("stage_crossed")
        act_step = sem("act_step")
        dve_step = sem("dve_step")
        const_in = sem("const_in")
        gain_in = [sem(f"gain{i}_in") for i in range(GAINBUFS)]
        gain_used = sem("gain_used")
        extra_in = sem("extra_in")
        bias_in = sem("bias_in")
        rows_ready = sem("rows_ready")
        rows_out = sem("rows_out")
        ada_in = [sem(f"ada{i}_in") for i in range(2)]
        ada_bias_in = sem("ada_bias_in")
        ada_step = sem("ada_step")
        ada_out = sem("ada_out")
        spread_pe = sem("vectors_spread")
        squared = sem("squared")
        turned = sem("turned")
        turn_high = sem("turn_high")
        gated = sem("gated")
        hidden = sem("hidden")
        proj_read = sem("proj_read")
        score = sem("score")
        biased = sem("biased")
        expd = sem("expd")
        p_turned = sem("p_turned")
        p_read = sem("p_read")
        headout = sem("headout")
        out_done = sem("out_done")

        x_added = sem("x_added")
        scaled = sem("outputs_scaled")
        normed = sem("normed")
        gate_copied = sem("gate_copied")

        def trio(name):
            return sem(name + "_pe"), sem(name + "_act"), sem(name + "_dve")

        setup_pe, setup_act, setup_dve = trio("setup")
        pad_dve, pad_act = sem("padding_dve"), sem("padding_act")
        stick_pe, stick_act, stick_dve = trio("stick")
        gates_pe, gates_act, gates_dve = trio("gates")
        ml_pe, ml_act, ml_dve = trio("mlstm")
        comp_pe, comp_act, comp_dve = trio("compress")
        cmp_pe, cmp_act, cmp_dve = trio("cmp")
        lat_pe, lat_act, lat_dve = trio("latent")
        route_pe, route_act, route_dve = trio("router")

        ident = const[:, C_IDENT:C_IDENT + P]

        def cols(w, c0, n):
            return w[:, c0:c0 + n].rearrange("(k p) n -> p k n", p=P)

        def slot(n, shape):
            k, w = shape
            return ring[n % RING][:, 0:k * w].rearrange("p (k w) -> p k w", k=k)

        def linear_slots(w, widths):
            at, got = 0, []
            for n in widths:
                got.append(("one", cols(w, at, n), (w.shape[0] // P, n)))
                at += n
            return got

        g_w, u_w, d_w = I["ffn_w_gate"], I["ffn_w_up"], I["ffn_w_down"]

        def ffn_chunk(which, layer, part, c):
            if which == "d":
                w = d_w[layer, part].rearrange("(c s p) n -> c p s n", p=P, s=2)
                return w[c]
            w = {"g": g_w, "u": u_w}[which][layer, part].rearrange("(k p) (c n) -> c p k n", p=P, n=256)
            return w[c]

        mg, mu, md = I["moe_w_gate_2"], I["moe_w_up_2"], I["moe_w_down_2"]

        def moe_chunk(which, layer, c, i):
            e = c // EC if i is None else i + c // EC
            if which == "d":
                return md[layer].rearrange("e (h s p) n -> h e p s n", p=P, s=2, h=EC)[c % EC][e]
            w = {"g": mg, "u": mu}[which]
            return w[layer].rearrange("e (k p) (h n) -> h e p k n", p=P, h=EC)[c % EC][e]

        GU, DN = (KT, 256), (2, D)

        ATTN_IN = [256] * 12
        MLSTM_IN = [256] * 16 + [16]
        EVEN_IN = [256, 256, 256, 256, 256, 24] + [256] * 6
        ODD_IN = [256, 192, 256, 256, 256]
        OUT4 = [256] * 4
        WIDTHS = {"attn": ATTN_IN, "mlstm": MLSTM_IN, "even": EVEN_IN, "odd": ODD_IN}

        def parts(n, shape):
            k, w = shape
            return [b[n % PARTS][:, 0:k * w].rearrange("p (k w) -> p k w", k=k) for b in (wh, wl)]

        def slot_count(n):
            return 16 * (n // RING + 1)

        def chunk_piece(n0, which, c, chunks):
            if which == "d":
                return n0 + 2 + 3 * c + 2 if c < chunks - 1 else n0 + 3 * chunks - 1
            return n0 + (0 if c == 0 else 2 + 3 * (c - 1)) + (1 if which == "u" else 0)

        def loop_pairs(chunks):
            return (chunks - 2) // 2

        wide_flat = wide[:, :, :, :].rearrange("p a h w -> p (a h w)")

        def wide_at(at, n):
            return wide_flat[0:8, at:at + n]

        S_RB, S_CONVW = 0, 24
        S_NMX, S_SUM, S_INV = 88, 104, 120
        S_G = 136
        S_COL, S_THR, S_DEN = 184, 200, 216
        S_MG = 136
        S_PAD = 440
        S_RW, S_R = 232, 360

        R_DIL, R_REL, R_PAD, R_PADMASK, R_END = 0, W3, 5 * W3, 5 * W3 + 512, 5 * W3 + 1024

        pad_b = [wide_at(1536 + 512 * i, 512) for i in range(2)]
        pad_m = [wide_at(2560 + 640 * i, 513) for i in range(2)]
        pad_a = [wide_at(3840 + 1024 * i, 512) for i in range(2)]
        pad_e = [wide_at(4352 + 1024 * i, 512) for i in range(2)]

        A_I, A_F, A_L, A_B, A_G = 256, 512, 768, 1024, 1280
        A_QRT, A_KRT = 384, 1408

        QA, KA, VA, QD, KD, VD = (1024 * i for i in range(6))
        M_PRE, M_V = 0, 4096
        (N_Q, N_KC, N_VC, N_KS, N_VS, N_KW, N_VW, N_QB, N_KB, N_VB) = (
            0, 1024, 1280, 1536, 1792, 2048, 2304, 2560, 3584, 4608)
        N_F = 5632
        (N_POS, N_U, N_GT, N_KCMP, N_VCMP) = (6656, 6720, 7232, 7360, 7376)
        (O_Q, O_K, O_V, O_CQ, O_CKV, O_KR, O_QM, O_KVM, O_QNT, O_KNT) = (
            0, 1024, 1280, 1536, 2048, 2304, 2432, 3968, 6016, 7040)

        def big_n(at, w):
            return big[:, at:at + TT * w].rearrange("p (t w) -> p t w", t=TT)

        def big_t(at, m):
            return big[:, at + m * T:at + (m + 1) * T]

        def t2(at, scale=1.0):
            return [("TT", 0, 256, big[:, at:at + 512], scale)]

        def n1(dst, c=0, scale=1.0):
            return ("N", c, dst.shape[2], dst, scale)

        def n256(at, w, j):
            return [n1(big_n(at, w)[:, :, j * 256:(j + 1) * 256])]

        def qgroup(kv, at, scale):
            return [("Q", 0, 256, big[64 * kv:64 * kv + 64, at:at + 1024], scale)]

        vM = big[:, M_V:M_V + TT * H * VW].rearrange("p (t h w) -> p t h w", t=TT, h=H)
        o_flat = biasT[:, :, :].rearrange("p h w -> p (h w)")[:, 0:TT * D]
        oM = o_flat.rearrange("p (t w) -> p t w", t=TT)

        def gview(at):
            return small[:, at:at + 48].rearrange("p (t w) -> p t w", t=TT)

        PROJ = {
            "attn": [t2(QA, 0.125), t2(QA + 512, 0.125), t2(KA), t2(KA + 512), n256(VA, 512, 0), n256(VA, 512, 1),
                     t2(QD, 0.125), t2(QD + 512, 0.125), t2(KD), t2(KD + 512), n256(VD, 512, 0), n256(VD, 512, 1)],
            "mlstm": [t2(M_PRE + 512 * j) for j in range(8)]
                     + [[("V", 0, 256, vM[:, :, 2 * j:2 * j + 2, 0:P], 1.0)] for j in range(4)]
                     + [[n1(oM[:, :, 256 * j:256 * j + 256])] for j in range(4)]
                     + [[n1(small[:, S_MG:S_MG + 32].rearrange("p (t w) -> p t w", t=TT))]],
            "even": [qgroup(0, N_Q, 0.125), qgroup(1, N_Q, 0.125),
                     [("T", 0, P, big_t(N_KC, 0), 1.0), ("T", P, P, big_t(N_VC, 0), 1.0)],
                     [("T", 0, P, big_t(N_KS, 0), 1.0), n1(big_n(N_VS, P), P)],
                     [("T", 0, P, big_t(N_KW, 0), 1.0), n1(big_n(N_VW, P), P)],
                     [n1(gview(S_G))],
                     t2(N_QB, 0.125), t2(N_QB + 512, 0.125), t2(N_KB), t2(N_KB + 512),
                     n256(N_VB, 512, 0), n256(N_VB, 512, 1)],
            "odd": [[n1(big_n(O_CQ, 256))], [n1(big_n(O_CKV, P)), n1(big_n(O_KR, 64), P)],
                    qgroup(0, O_Q, 0.125), qgroup(1, O_Q, 0.125),
                    [("T", 0, P, big_t(O_K, 0), 1.0), n1(big_n(O_V, P), P)]],
        }
        PROJ_AT, at = {}, 0
        for name in PROJ:
            PROJ_AT[name] = at
            at += len(PROJ[name])

        def pair_heads(qat, kat):
            def parts(h):
                p0 = 64 * (h % 2)
                return [(big[p0:p0 + 64, qat + (h // 2) * T:qat + (h // 2 + 1) * T],
                         big[p0:p0 + 64, kat + (h // 2) * T:kat + (h // 2 + 1) * T])]
            return parts

        def group_heads(qat, kat):
            def parts(h):
                p0, g = 64 * (h // 4), h % 4
                return [(big[p0:p0 + 64, qat + g * T:qat + (g + 1) * T], big[p0:p0 + 64, kat:kat + T])]
            return parts

        def mla_heads(h):
            qrT = aux[0:64, A_QRT + h * T:A_QRT + (h + 1) * T]
            return [(big_t(O_QNT, h), big_t(O_KNT, h)), (qrT, aux[0:64, A_KRT:A_KRT + T])]

        vmla = big_n(O_KVM, 1024).rearrange("p t (h w) -> p t h w", h=MH)

        def soft(parts, v, heads, dv, dst, bias=True, scale=1.0, pad=None, gate=None):
            return dict(parts=parts, v=v, heads=heads, dv=dv, dst=dst, bias=bias, scale=scale, pad=pad, gate=gate)

        SOFT = {
            "dilated": soft(pair_heads(QD, KD), lambda h, t: big_n(VD, 512)[:, t, 64 * h:64 * h + 64], H, 64, 512),
            "selected": soft(group_heads(N_Q, N_KS), lambda h, t: big_n(N_VS, P)[:, t, 64 * (h // 4):64 * (h // 4) + 64],
                             H, 64, 0, gate=1),
            "window": soft(group_heads(N_Q, N_KW), lambda h, t: big_n(N_VW, P)[:, t, 64 * (h // 4):64 * (h // 4) + 64],
                           H, 64, 0, gate=2, pad=S_PAD),
            "moba": soft(pair_heads(N_QB, N_KB), lambda h, t: big_n(N_VB, 512)[:, t, 64 * h:64 * h + 64], H, 64, 512),
            "mla": soft(mla_heads, lambda h, t: vmla[:, t, h, P:2 * P], MH, P, 0, bias=False, scale=192.0 ** -0.5),
            "sliding": soft(group_heads(O_Q, O_K), lambda h, t: big_n(O_V, P)[:, t, 64 * (h // 4):64 * (h // 4) + 64],
                            H, 64, 512, pad=S_PAD + 32),
        }
        PADDED = [name for name in SOFT if SOFT[name]["pad"] is not None]
        at, steps = 0, 0
        for spec in SOFT.values():
            spec["head0"], spec["step0"], spec["steps"] = at, steps, 3 if spec["pad"] is None else 5
            at, steps = at + spec["heads"], steps + spec["heads"] * spec["steps"]

        STAGES = []
        stream = []

        def add(name, *args, gains=0, pieces=()):
            STAGES.append((name, args, gains))
            stream.extend(pieces)

        def mixer_end(weights, residual):
            add("turn")
            add("outproj", pieces=linear_slots(weights, OUT4))
            add(*residual, gains=1)

        for layer in range(2):
            add("norm", None, gains=1)
            add("turn")
            if layer == 0:
                add("setup")
            add("ffn", FC, False, pieces=[("ffn", (layer, 0), FC)])
            add("residual", "norm", 0.5, gains=1)
            add("norm", None, gains=1)
            add("turn")
            if layer == 0:
                add("project", "attn", pieces=linear_slots(I["attn_w_in"][0], ATTN_IN))
                add("stick")
                add("soft", "dilated")
                mixer_end(I["attn_w_out"][0], ("residual", "norm", 1.0))
            else:
                add("project", "mlstm", pieces=linear_slots(I["mlstm_w_in"][0], MLSTM_IN))
                add("gates")
                add("mlstm", gains=1)
                mixer_end(I["mlstm_w_out"][0], ("residual", "norm", 1.0))
            add("norm", None, gains=1)
            add("turn")
            add("ffn", FC, False, pieces=[("ffn", (layer, 1), FC)])
            add("residual", "norm", 0.5, gains=1)
        for layer in range(2):
            add("norm", "ada", gains=3)
            add("turn")
            if layer == 0:
                add("project", "even", pieces=linear_slots(I["ev_w_in_2"][0], EVEN_IN))
                add("compress", pieces=[("one", w1[half * 1024:half * 1024 + 1024, :].rearrange("(k p) n -> p k n", p=P), GU)
                                        for w1 in (I["nsa_ck_w1_2"][0], I["nsa_cv_w1_2"][0]) for half in range(2)])
                add("cmp")
                for name in ("selected", "window", "moba"):
                    add("soft", name)
                mixer_end(I["ev_w_out_2"][0], ("residual", "gate", None))
            else:
                add("project", "odd", pieces=linear_slots(I["od_w_in_2"][0], ODD_IN))
                add("latent", pieces=[("one", cols(I["mla_w_q_up_2"][0], 0, 768), (2, 768)),
                                      ("one", cols(I["mla_w_kv_up_2"][0], 0, 1024), (1, 1024))])
                add("soft", "mla")
                add("soft", "sliding")
                mixer_end(I["od_w_out_2"][0], ("residual", "gate", None))
            add("norm", "ada", gains=3)
            add("turn")
            add("router")
            add("ffn", E * EC, True, pieces=[("moe", (layer, 0), E * EC)])
            add("residual", "gate", None, gains=1)
        add("final", gains=1)

        seen, INSTANCE = {}, []
        for name, _, _ in STAGES:
            INSTANCE.append(seen.get(name, 0))
            seen[name] = INSTANCE[-1] + 1

        GAINS = []
        for layer in range(2):
            g = [I["norm_g"][layer, j] for j in range(6)]
            GAINS += g[0:3] + ([I["mlstm_head_g"][0]] if layer == 1 else []) + g[3:6]
        for layer in range(2):
            for name, m in (("norm_mix_2", 0), ("norm_ffn_2", 3)):
                GAINS += [I[name][layer]] + [modpart[layer, v] for v in (m + 1, m, m + 2)]
        GAINS.append(I["final_norm_2"])
        assert len(GAINS) == sum(s[2] for s in STAGES)

        ada_w = [big[:, SLOT * i:SLOT * (i + 1)].rearrange("p (k n) -> p k n", k=KT) for i in range(2)]
        ada_sum = big[:, 2 * SLOT:2 * SLOT + D]
        ada_bias = aux[0:1, 0:D]
        ADA_TURNS = {0: [(0, 0)], 1: [(0, 3), (1, 0)], 3: [(1, 3)]}

        JOINED = [s > 0 and (name, STAGES[s - 1][0]) in (("norm", "residual"), ("final", "residual"),
                                                         ("turn", "norm"), ("soft", "soft"), ("ffn", "router"))
                  for s, (name, _, _) in enumerate(STAGES)] + [False]
        CROSSED = [3 * (s - sum(JOINED[1:s + 1])) for s in range(len(STAGES) + 1)]

        def boundary(eng, s):
            if not JOINED[s]:
                eng.drain().then_inc(crossed, 1)
                eng.wait_ge(crossed, CROSSED[s])

        block = ctx.enter_context(nc.Block())

        @block.sync
        def _(sp):
            def load(n, src, shape, i=None):
                if i is not None:
                    sp.wait_ge(freed, i * LOOP + (n - RING + 1))
                elif n >= RING:
                    sp.wait_ge(freed, n - RING + 1)
                sp.dma_start(slot(n, shape), src).then_inc(loaded[n % RING], 16)

            def chunked(n, source, chunks):
                def piece(which, c, i=None):
                    load(chunk_piece(n, which, c, chunks), source(which, c, i), DN if which == "d" else GU, i)

                for which, c in (("g", 0), ("u", 0), ("g", 1), ("u", 1), ("d", 0)):
                    piece(which, c)
                with sp.Fori(0, loop_pairs(chunks)) as i:
                    for c in (1, 2):
                        piece("g", c + 1, i)
                        piece("u", c + 1, i)
                        piece("d", c, i)
                for c in range(1 + 2 * loop_pairs(chunks), chunks):
                    if c + 1 < chunks:
                        piece("g", c + 1)
                        piece("u", c + 1)
                    piece("d", c)

            n = 0
            sp.dma_start(const[:, :], I["const"]).then_inc(const_in, 16)
            sp.dma_start(x[:, :, :], I["x"][0].rearrange("(t p) d -> p t d", p=P)).then_inc(const_in, 16)
            for kind, what, more in stream:
                if kind == "one":
                    load(n, what, more)
                    n += 1
                elif kind == "ffn":
                    chunked(n, lambda which, c, i: ffn_chunk(which, *what, c if i is None else i * 2 + c), more)
                    n += 3 * more
                else:
                    chunked(n, lambda which, c, i: moe_chunk(which, what[0], c, i), more)
                    n += 3 * more

        @block.gpsimd
        def _(pool):
            def load_gain(k):
                if k >= GAINBUFS:
                    pool.wait_ge(gain_used, k - GAINBUFS + 1)
                src = GAINS[k] if len(GAINS[k].shape) == 2 else GAINS[k].rearrange("(a n) -> a n", a=1)\
                    .broadcast_to([P, D])
                pool.dma_start(gain[k % GAINBUFS][:, :], src).then_inc(gain_in[k % GAINBUFS], 16)

            def load_bias(kind):
                at = rowbuf[kind].offset + 127
                pool.dma_start(biasT[:, :, P:W3],
                               bass.AP(rowbuf.tensor, at, [[W3 - 1, P], [P * W3, H], [1, T]])).then_inc(bias_in, 16)
                pool.dma_start(biasT[:, :, 0:P],
                               bass.AP(rowbuf.tensor, at + P, [[W3 - 1, P], [P * W3, H], [1, P]])).then_inc(bias_in, 16)

            def small_in(dst, src):
                pool.dma_start(dst, src).then_inc(extra_in, 16)

            def row(ap):
                return ap.rearrange("(a n) -> a n", a=1)

            def adaln_turn(layer, turn, i=None):
                w = I["ada_w_2"][layer].rearrange("(k p) (s r n) -> r s p k n", p=P, r=4, n=256)
                place = turn if i is None else i + turn
                q = 6 * layer + turn

                def at(per_turn, v):
                    v += q * per_turn
                    return v if i is None else i * per_turn + v

                def load(r):
                    pool.dma_start(ada_w[r % 2], w[r][place]).then_inc(ada_in[r % 2], 16)

                def step(v, out_, a, b, op):
                    pool.tensor_tensor(out_, a, b, op).then_inc(ada_step, 1)
                    pool.wait_ge(ada_step, at(17, v))

                pool.dma_start(ada_bias, I["ada_b_2"][layer:layer + 1, :].rearrange("a (s n) -> s a n", s=6)[place])\
                    .then_inc(ada_bias_in, 16)
                load(0)
                load(1)
                for r in range(4):
                    pool.wait_ge(ada_in[r % 2], at(32, 16 * (r // 2 + 1)))
                    piece = ada_w[r % 2]
                    step(4 * r + 1, piece, piece, spread(ccol[:, :], 2, 256), ALU.mult)
                    step(4 * r + 2, piece[:, 0:4], piece[:, 0:4], piece[:, 4:8], ALU.add)
                    step(4 * r + 3, piece[:, 0:2], piece[:, 0:2], piece[:, 2:4], ALU.add)
                    step(4 * r + 4, ada_sum[:, 256 * r:256 * r + 256], piece[:, 0], piece[:, 1], ALU.add)
                    if r < 2:
                        load(r + 2)
                pool.wait_ge(ada_bias_in, at(16, 16))
                step(17, ada_sum[0:1, :], ada_sum[0:1, :], ada_bias, ALU.add)
                pool.dma_start(modpart[layer][place], ada_sum).then_inc(ada_out, 16)
                pool.wait_ge(ada_out, at(16, 16))

            small_in(aux[0:32, 0:8], I["rel_bias"])
            small_in(aux[0:32, 8:16], I["rel_table_2"])
            small_in(big[0:32, 0:R_END], I["rows"])
            small_in(aux[0:8, 16:144], I["c_2"][0].rearrange("(k p) -> k p", p=P))
            small_in(small[:, S_RB:S_RB + E], row(I["router_b_2"]).broadcast_to([P, E]))
            small_in(aux[0:8, 144:145], I["swa_sinks_2"].rearrange("a h -> h a"))
            small_in(small[:, S_RW:S_RW + P].rearrange("p (k e) -> p k e", k=KT),
                     I["router_w_2"].rearrange("(k p) e -> p k e", p=P))
            for g in range(GAINBUFS):
                load_gain(g)
            g = GAINBUFS
            for s, (name, args, used) in enumerate(STAGES):
                if name == "setup":
                    pool.wait_ge(rows_out, 48)
                    load_bias(0)
                if name == "project" and args[0] != "attn":
                    pool.wait_ge(crossed, CROSSED[s])
                if name == "project" and args[0] == "mlstm":
                    small_in(aux[0:8, 0:1], I["mlstm_b_gates"][0, 0:8].rearrange("(p a) -> p a", a=1))
                    small_in(aux[0:8, 1:2], I["mlstm_b_gates"][0, 8:16].rearrange("(p a) -> p a", a=1))
                    small_in(aux[0:64, 16:144], I["mlstm_conv_w"][0].rearrange("j (t p) -> (j t) p", p=P))
                if name == "project" and args[0] == "even":
                    load_bias(1)
                    for at in (0, 64):
                        small_in(aux[0:32, at:at + 64], I["nsa_pos_k_2"][0])
                        small_in(aux[0:32, P + at:P + at + 64], I["nsa_pos_v_2"][0])
                    for at, w in ((256, I["nsa_ck_w2_2"]), (384, I["nsa_cv_w2_2"])):
                        small_in(aux[:, at:at + P].rearrange("p (k n) -> p k n", k=2),
                                 w[0].rearrange("(k p) n -> p k n", p=P))
                if name == "project" and args[0] == "odd":
                    load_bias(2)
                    small_in(aux[:, 0:256], I["mla_q_norm_2"].broadcast_to([P, 256]))
                    small_in(aux[:, 256:384], I["mla_kv_norm_2"].broadcast_to([P, P]))
                if name == "ffn" and INSTANCE[s] in ADA_TURNS:
                    pool.wait_ge(crossed, CROSSED[s])
                    for layer, turn in ADA_TURNS[INSTANCE[s]]:
                        with pool.Fori(0, 3) as i:
                            adaln_turn(layer, turn, i)
                for _ in range(used):
                    if g < len(GAINS):
                        load_gain(g)
                        g += 1

        PIECE0, n_piece, extra = [], 0, iter(())
        SLOTS = {"outproj": 4, "compress": 4, "latent": 2}
        SQ0, n_sq = [], 0
        for name, args, _ in STAGES:
            PIECE0.append(n_piece)
            SQ0.append(n_sq)
            n_piece += (3 * args[0] if name == "ffn" else len(PROJ[args[0]]) if name == "project"
                        else SLOTS.get(name, 0))
            n_sq += 2 if name in ("norm", "final") or (name == "residual" and args[0] == "norm") else 0
        SPLIT0 = [PIECE0[s] - sum(SLOTS.get(n, 0) for n, _, _ in STAGES[:s] if n != "outproj")
                  for s in range(len(STAGES))]
        SPREAD0 = [sum(a[0] in ("ada", "gate") for n, a, _ in STAGES[:s] if n in ("norm", "residual"))
                   for s in range(len(STAGES))]

        def early(s):
            if s < len(STAGES) and STAGES[s][0] == "outproj":
                return [GU] * max(0, 2 - PIECE0[s] % PARTS)
            if s >= len(STAGES) or STAGES[s][0] not in ("ffn", "project"):
                return []
            if STAGES[s][0] == "ffn":
                return [GU] * (3 if STAGES[s][1][1] else 2)
            return [(KT, n) for n in WIDTHS[STAGES[s][1][0]][0:2]]

        def early_lows(s):
            return 1 if STAGES[s - 1][0] == "turn" else len(early(s))

        def ran(s, *names):
            return sum(n in names for n, _, _ in STAGES[:s])

        def k_gate(s):
            return sum(n == "residual" and a[0] == "gate" for n, a, _ in STAGES[:s])

        GAIN0 = [sum(u for _, _, u in STAGES[:s]) for s in range(len(STAGES))]
        EXTRA = {"setup": 7 * 16, "mlstm": 10 * 16, "even": 16 * 16, "odd": 18 * 16}

        def ffn_bases(k):
            if k < 4:
                return k * FC, 3 * k * FC
            return 4 * FC + (k - 4) * E * EC, 12 * FC + 4 * (k - 4) * E * EC

        def wait_gain(eng, g):
            eng.wait_ge(gain_in[g % GAINBUFS], 16 * (g // GAINBUFS + 1))

        GB, UB = 4, 6
        route = big[:, 4096:8192]
        routing = big[:, 0:4096].rearrange("p (e t) -> p e t", e=E)
        cv = wide_flat[:, 0:4096].rearrange("p (m t) -> p m t", t=T)
        mE = [wide_flat[:, 4096 + W3 * i:4096 + W3 * (i + 1)] for i in range(2)]
        raw = big[:, 0:TT * H * VW].rearrange("p (t h w) -> p t h w", t=TT, h=H)
        hid = nrm[:, :, :].rearrange("p t (h w) -> p t h w", h=H)
        qm = big[:, O_QM:O_QM + 1536].rearrange("p (t h w) -> p t h w", t=TT, h=MH)
        blocksF = [big[:, N_F + 480 * i:N_F + 480 * (i + 1)].rearrange("p (j v n) -> p j v n", j=16, v=2)
                   for i in range(2)]
        cS = wide_flat[:, 0:256].rearrange("p (h t n) -> p h t n", h=H, t=TT)
        cPT = wide_flat[:, 1024:3072]
        cqT = wide_flat[:, 0:3 * T].rearrange("p (k t) -> p k t", t=T)

        @block.tensor
        def _(pe):
            def mm(out_, lhsT, rhs, start, stop, **kw):
                return pe.matmul(out_, lhsT, rhs, start=start, stop=stop, **kw)

            def piece_in(n, i=None):
                if i is None:
                    pe.wait_ge(loaded[n % RING], slot_count(n))
                else:
                    pe.wait_ge(loaded[n % RING], i * (16 * LOOP // RING) + slot_count(n))

            def used(last, n, i=None):
                last.then_inc(piece_used, 1)
                pe.wait_ge(piece_used, n + 1 if i is None else i * LOOP + (n + 1))
                pe.nop().then_inc(freed, 1)

            def split_in(n, i=None):
                pe.wait_ge(freed, n + 1 if i is None else i * LOOP + (n + 1))

            def three(out_, stationary, moving, first, last):
                (sh, sl), (mh, ml) = stationary, moving
                mm(out_, sh, mh, first, False)
                mm(out_, sh, ml, False, False)
                return mm(out_, sl, mh, False, last)

            def both(ap, *index):
                return [a[index] for a in ap]

            xs = (xh, xl)

            def setup(s, k):
                pe.wait_ge(extra_in, EXTRA["setup"])
                pe.transpose(psum[:, 0, 0:8], aux[0:8, 16:144], ident[0:8, 0:8])
                mm(psum[0:8, 1, 0:W3], aux[0:32, 0:8], big[0:32, 0:W3], True, True)
                mm(psum[0:8, 2, 0:W3], aux[0:32, 8:16], big[0:32, R_REL:R_REL + W3], True, True)
                mm(psum[0:8, 3, :], aux[0:32, 8:16], big[0:32, R_PAD:R_PAD + 512], True, True).then_inc(setup_pe, 1)
                pe.wait_ge(setup_dve, 3)
                for i in range(2):
                    for t in range(TT):
                        lo, at = 383 - P * t, 32 * i + 8 * t
                        pe.transpose(psum[:, 4, at:at + 8], pad_m[i][:, lo + 1:lo + 1 + P], ident[0:8, 0:8])
                        last = pe.transpose(psum[:, 4, at + 16:at + 24], pad_b[i][:, lo:lo + P], ident[0:8, 0:8])
                last.then_inc(setup_pe, 1)
                pe.wait_ge(setup_dve, 4)
                mm(psum[:, 5, 0:64], const[:, C_FLIP:C_FLIP + P], small[:, S_PAD:S_PAD + 64], True, True)\
                    .then_inc(setup_pe, 1)

            def turn(s, k):
                for q in range(4):
                    t, half = q // 2, q % 2
                    if JOINED[s] and half == 0:
                        pe.wait_ge(normed, 2 * ran(s, "norm") - 2 + t + 1)
                    for i in range(4):
                        f = (4 * half + i) * P
                        last = pe.transpose(psum[:, q, i * P:(i + 1) * P], nrm[:, t, f:f + P], ident)
                    last.then_inc(turned, 1)

            def ffn(s, k, chunks, moe):
                n0 = PIECE0[s]
                c0, h0 = ffn_bases(k)
                steps = 4 if moe else 3

                def gate_up_products(c, i=None):
                    if c >= 2:
                        v = h0 + steps * (c - 1)
                        pe.wait_ge(hidden, v if i is None else i * (2 * steps) + v)
                    for which, bank in (("g", GB + c % 2), ("u", UB + c % 2)):
                        n = chunk_piece(n0, which, c, chunks)
                        split_in(n, i)
                        w = parts(n, GU)
                        for f in range(2):
                            for kt in range(KT):
                                last = three(psum[:, bank, f * T:(f + 1) * T],
                                             both(w, slice(0, P), kt, slice(f * P, (f + 1) * P)),
                                             both(xs, slice(0, P), kt, slice(0, T)), kt == 0, kt == KT - 1)
                        last.then_inc(piece_used, 1)

                def down_products(c, i=None):
                    v = h0 + steps * (c + 1)
                    pe.wait_ge(hidden, v if i is None else i * (2 * steps) + v)
                    n = chunk_piece(n0, "d", c, chunks)
                    split_in(n, i)
                    w, h = parts(n, DN), (hh[c % 2], hl[c % 2])
                    for f in range(2):
                        for t in range(TT):
                            for half in range(2):
                                last = three(psum[:, 2 * t + half, :],
                                             both(h, slice(0, P), f, slice(t * P, (t + 1) * P)),
                                             both(w, slice(0, P), f, slice(half * 512, (half + 1) * 512)),
                                             c == 0 and f == 0, c == chunks - 1 and f == 1)
                    last.then_inc(piece_used, 1)

                gate_up_products(0)
                gate_up_products(1)
                if moe:
                    spread_routing(k - 4)
                down_products(0)
                with pe.Fori(0, loop_pairs(chunks)) as i:
                    for c in (1, 2):
                        gate_up_products(c + 1, i)
                        down_products(c, i)
                for c in range(1 + 2 * loop_pairs(chunks), chunks):
                    if c + 1 < chunks:
                        gate_up_products(c + 1)
                    down_products(c)

            def project(s, k, name):
                widths = WIDTHS[name]
                for j, pieces in enumerate(PROJ[name]):
                    n = PIECE0[s] + j
                    if j >= 4:
                        pe.wait_ge(proj_read, PROJ_AT[name] + j - 3)
                    split_in(n)
                    w = parts(n, (KT, widths[j]))
                    at = 0
                    for kind, c, m, _, _ in pieces:
                        for t in range(TT if kind in ("N", "V") else m // P):
                            for kt in range(KT):
                                if kind in ("N", "V"):
                                    width, a, b = m, both(xs, slice(0, P), kt, slice(t * P, (t + 1) * P)), \
                                        both(w, slice(0, P), kt, slice(c, c + m))
                                else:
                                    width, b, a = T, both(xs, slice(0, P), kt, slice(0, T)), \
                                        both(w, slice(0, P), kt, slice(c + t * P, c + (t + 1) * P))
                                last = three(psum[:, j % 4, at:at + width], a, b, kt == 0, kt == KT - 1)
                            at += width
                    last.then_inc(piece_used, 1)

            def outproj(s, k):
                for j in range(4):
                    n = PIECE0[s] + j
                    split_in(n)
                    w = parts(n, GU)
                    for t in range(TT):
                        for kt in range(KT):
                            last = three(psum[:, 2 * t + j // 2, (j % 2) * 256:(j % 2 + 1) * 256],
                                         both(xs, slice(0, P), kt, slice(t * P, (t + 1) * P)),
                                         both(w, slice(0, P), kt, slice(0, 256)), kt == 0, kt == KT - 1)
                    last.then_inc(piece_used, 1)

            def stick(s, k):
                def scores(h):
                    if h >= 2:
                        pe.wait_ge(stick_dve, h - 1)
                    p0, c = 64 * (h % 2), (h // 2) * T
                    q, key = big[p0:p0 + 64, QA + c:QA + c + T], big[p0:p0 + 64, KA + c:KA + c + T]
                    mm(psum[:, h % 2, 0:T], key[:, 0:P], q, True, True)
                    mm(psum[:, h % 2, T:W3], key[:, P:T], q[:, P:T], True, True).then_inc(stick_pe, 1)

                def later(h):
                    pe.wait_ge(stick_dve, H + 3 * (h + 1))
                    if h >= 2:
                        pe.wait_ge(stick_dve, 4 * H + h - 1)
                    sp_h, b = wide[:, 1, h, :], 2 + h % 2
                    mm(psum[:, b, 0:T], const[:, C_AFTER:C_AFTER + P], sp_h[:, 0:T], True, False,
                       skip_group_check=True)
                    mm(psum[:, b, P:T], const[:, C_ONES:C_ONES + P], sp_h[:, T:W3], False, True,
                       skip_group_check=True)
                    mm(psum[:, b, T:W3], const[:, C_AFTER:C_AFTER + P], sp_h[:, T:W3], True, True)\
                        .then_inc(stick_pe, 1)

                def values(h):
                    pe.wait_ge(stick_dve, 5 * H + h + 1)
                    w = wide[:, 0, h, :]
                    v = big_n(VA, 512)[:, :, 64 * h:64 * h + 64]
                    mm(psum[:, 4, 64 * h:64 * h + 64], w[:, 0:P], v[:, 0], True, True)
                    mm(psum[:, 5, 64 * h:64 * h + 64], w[:, P:T], v[:, 0], True, False)
                    return mm(psum[:, 5, 64 * h:64 * h + 64], w[:, T:W3], v[:, 1], False, True)

                for h in range(H):
                    scores(h)
                for h in range(H):
                    later(h)
                for h in range(H):
                    last = values(h)
                last.then_inc(stick_pe, 1)

            def soft_attention(s, k, name):
                a = SOFT[name]
                h0, s0, n, dv = a["head0"], a["step0"], a["steps"], a["dv"]

                def scores(h):
                    if h >= 2:
                        pe.wait_ge(biased, s0 + n * (h - 2) + 1)
                    elif JOINED[s]:
                        pe.wait_ge(biased, s0)
                    parts = a["parts"](h)
                    for lo, hi, t in ((0, P, 0), (P, W3, 1)):
                        for i, (q, key) in enumerate(parts):
                            last = mm(psum[:, h % 2, lo:hi], q[:, t * P:(t + 1) * P], key[:, 0:hi - lo],
                                      i == 0, i == len(parts) - 1)
                    last.then_inc(score, 1)

                def turn_probs(h):
                    pe.wait_ge(expd, 2 * (h0 + h + 1))
                    if h >= 2 or JOINED[s]:
                        pe.wait_ge(p_read, h0 + h - 1)
                    for i in range(3):
                        last = pe.transpose(psum[:, 2 + h % 2, i * P:(i + 1) * P],
                                            wide[:, 0, h, i * P:(i + 1) * P], ident)
                    last.then_inc(p_turned, 1)

                def values(h):
                    pe.wait_ge(p_read, h0 + h + 1)
                    if JOINED[s] and h == 0:
                        pe.wait_ge(scaled, 2 * ran(s, "soft"))
                    p, c = PT[h % 2], slice(h * dv, (h + 1) * dv)
                    mm(psum[:, 4, c], p[:, 0:P], a["v"](h, 0), True, True)
                    mm(psum[:, 5, c], p[:, P:T], a["v"](h, 0), True, False)
                    mm(psum[:, 5, c], p[:, T:W3], a["v"](h, 1), False, True).then_inc(headout, 1)

                scores(0)
                scores(1)
                for h in range(a["heads"]):
                    turn_probs(h)
                    if h + 2 < a["heads"]:
                        scores(h + 2)
                    if h >= 1:
                        values(h - 1)
                values(a["heads"] - 1)

            def gates(s, k):
                pe.wait_ge(extra_in, EXTRA["mlstm"])
                pe.transpose(psum[:, 0, 0:64], aux[0:64, 16:144], ident[0:64, 0:64])
                for t in range(TT):
                    for i in range(2):
                        at = S_MG + 16 * t + 8 * i
                        last = pe.transpose(psum[0:8, 2 + i, t * P:(t + 1) * P], small[:, at:at + 8], ident)
                last.then_inc(gates_pe, 1)
                pe.wait_ge(gates_act, 2)
                for t in range(TT):
                    pe.transpose(psum[:, 1, 8 * t:8 * t + 8], aux[0:8, A_G + t * P:A_G + (t + 1) * P], ident[0:8, 0:8])
                    last = pe.transpose(psum[:, 1, 16 + 8 * t:24 + 8 * t],
                                        aux[0:8, A_F + t * P:A_F + (t + 1) * P], ident[0:8, 0:8])
                last.then_inc(gates_pe, 1)

            def mlstm(s, k):
                def products(h):
                    if h >= 2:
                        pe.wait_ge(ml_dve, 4 * (h - 1))
                    mm(psum[:, h % 2, 0:T], spread(ident[0:8, h], 1, P), aux[0:8, A_L:A_L + T], True, True)\
                        .then_inc(ml_pe, 1)
                    mm(psum[:, 2 + h % 2, 0:T], cv[:, 8 + h, 0:P], cv[:, h, :], True, True)
                    mm(psum[:, 2 + h % 2, T:W3], cv[:, 8 + h, P:T], cv[:, h, P:T], True, True).then_inc(ml_pe, 1)

                def values(h):
                    pe.wait_ge(ml_dve, 4 * (h + 1))
                    if h >= 2:
                        pe.wait_ge(ml_act, 2 * h - 1)
                    p, b = PT[h % 2], 4 + h % 2
                    mm(psum[:, b, 0:VW], p[:, 0:P], vM[:, 0, h, :], True, True)
                    mm(psum[:, b, VW:2 * VW], p[:, P:T], vM[:, 0, h, :], True, False)
                    mm(psum[:, b, VW:2 * VW], p[:, T:W3], vM[:, 1, h, :], False, True).then_inc(ml_pe, 1)

                products(0)
                for h in range(H):
                    if h + 1 < H:
                        products(h + 1)
                    values(h)

            def spread_vector(g, bank):
                wait_gain(pe, g)
                for half in range(2):
                    last = mm(psum[:, bank + half, :], const[:, C_ONES:C_ONES + P],
                              gain[g % GAINBUFS][:, half * 512:(half + 1) * 512], True, True)
                return last

            def norm(s, k, m):
                if m is not None:
                    if k_gate(s):
                        pe.wait_ge(gate_copied, k_gate(s))
                    spread_vector(GAIN0[s] + 1, 4)
                    spread_vector(GAIN0[s] + 2, 6).then_inc(spread_pe, 1)

            def residual(s, k, kind, coef):
                if kind == "gate":
                    spread_vector(GAIN0[s], 4).then_inc(spread_pe, 1)

            def compress(s, k):
                pe.wait_ge(extra_in, EXTRA["even"])
                pe.transpose(psum[:, 0, 0:32], aux[0:32, 0:P], ident[0:32, 0:32])
                pe.transpose(psum[:, 0, 32:64], aux[0:32, P:2 * P], ident[0:32, 0:32]).then_inc(comp_pe, 1)
                pe.wait_ge(comp_dve, 9)
                for i in range(2):
                    for half in range(2):
                        n = PIECE0[s] + 2 * i + half
                        piece_in(n)
                        w = slot(n, GU)
                        for kt in range(KT):
                            j = half * KT + kt
                            last = mm(psum[0:30, 1 + i, 0:256], blocksF[i][:, j, :, :], w[:, kt, :],
                                      j == 0, j == 15)
                        used(last, n)
                pe.wait_ge(comp_act, 1)
                for i in range(2):
                    for half in range(2):
                        at = N_U + 256 * i + P * half
                        last = pe.transpose(psum[:, 3, (2 * i + half) * 30:(2 * i + half + 1) * 30],
                                            big[0:30, at:at + P], ident[0:30, 0:30])
                last.then_inc(comp_pe, 1)
                pe.wait_ge(comp_dve, 10)
                for v in range(2):
                    for half in range(2):
                        g = N_GT + 30 * half + NCMP * v
                        mm(psum[64 * v:64 * v + 64, 4, 0:NCMP], aux[:, 256 + 64 * half:320 + 64 * half],
                           big[:, g:g + NCMP], half == 0, half == 1)
                for v in range(2):
                    for half in range(2):
                        g = N_GT + 60 + 30 * half + NCMP * v
                        last = mm(psum[0:NCMP, 5, 64 * v:64 * v + 64], big[:, g:g + NCMP],
                                  aux[:, 384 + 64 * half:448 + 64 * half], half == 0, half == 1)
                last.then_inc(comp_pe, 1)

            def cmp_attention(s, k):
                for h in range(H):
                    p0, c = 64 * (h // 4), N_Q + (h % 4) * T
                    for t in range(TT):
                        at = (2 * h + t) * 16
                        last = mm(psum[:, (0, 7)[h // 4], at:at + NCMP], big[p0:p0 + 64, c + t * P:c + (t + 1) * P],
                                  big[p0:p0 + 64, N_KCMP:N_KCMP + NCMP], True, True)
                last.then_inc(cmp_pe, 1)
                pe.wait_ge(cmp_act, 2)
                for i in range(2 * H):
                    last = pe.transpose(psum[0:NCMP, 1 + i // 4, (i % 4) * P:(i % 4 + 1) * P],
                                        cS[:, i // 2, i % 2, 0:NCMP], ident)
                last.then_inc(cmp_pe, 1)
                pe.wait_ge(cmp_act, 3)
                for h in range(H):
                    for t in range(TT):
                        i = 2 * h + t
                        v = N_VCMP + 64 * (h // 4)
                        last = mm(psum[:, 5 + t, 64 * h:64 * h + 64], cPT[0:NCMP, i * P:(i + 1) * P],
                                  big[0:NCMP, v:v + 64], True, True)
                last.then_inc(cmp_pe, 1)

            def latent(s, k):
                pe.wait_ge(lat_dve, 1)
                for t in range(TT):
                    for i in range(2):
                        pe.transpose(psum[:, 0, i * T + t * P:i * T + (t + 1) * P],
                                     big_n(O_CQ, 256)[:, t, i * P:(i + 1) * P], ident)
                    last = pe.transpose(psum[:, 1, t * P:(t + 1) * P], big_n(O_CKV, P)[:, t, :], ident)
                last.then_inc(lat_pe, 1)
                pe.wait_ge(lat_dve, 2)
                n = PIECE0[s]
                piece_in(n)
                w = slot(n, (2, 768))
                for t in range(TT):
                    for lo, hi in ((0, 512), (512, 768)):
                        for i in range(2):
                            last = mm(psum[:, 2 + 2 * t + lo // 512, 0:hi - lo], cqT[:, i, t * P:(t + 1) * P],
                                      w[:, i, lo:hi], i == 0, i == 1)
                used(last, n)
                piece_in(n + 1)
                w = slot(n + 1, (1, 1024))
                for t in range(TT):
                    for half in range(2):
                        last = mm(psum[:, (6, 0)[t] + half, :], cqT[:, 2, t * P:(t + 1) * P],
                                  w[:, 0, half * 512:(half + 1) * 512], True, True)
                used(last, n + 1)
                pe.wait_ge(lat_act, 3)
                pe.wait_ge(lat_dve, 3)
                for h in range(MH):
                    for t in range(TT):
                        at = (h % 2) * T + t * P
                        pe.transpose(psum[:, 2 + h // 2, at:at + P], qm[:, t, h, 0:P], ident)
                        pe.transpose(psum[:, 4 + h // 2, at:at + P], vmla[:, t, h, 0:P], ident)
                        last = pe.transpose(psum[0:64, 6 + h // 2, at:at + P], qm[:, t, h, P:P + 64], ident)
                for t in range(TT):
                    last = pe.transpose(psum[0:64, 0, t * P:(t + 1) * P], big_n(O_KR, 64)[:, t, :], ident)
                last.then_inc(lat_pe, 1)

            def router(s, k):
                for t in range(TT):
                    for kt in range(KT):
                        last = three(psum[:, 0, E * t:E * t + E], both(xs, slice(0, P), kt, slice(t * P, (t + 1) * P)),
                                     both((rw_high, rw_low), slice(0, P), slice(E * kt, E * kt + E)),
                                     kt == 0, kt == KT - 1)
                last.then_inc(route_pe, 1)

            def spread_routing(k):
                pe.wait_ge(route_dve, 4 * k + 1)
                for t in range(TT):
                    last = pe.transpose(psum[0:E, 1, t * P:(t + 1) * P], route[:, E * t:E * t + E], ident)
                last.then_inc(route_pe, 1)
                for j in range(2):
                    pe.wait_ge(route_dve, 4 * k + 2 + j)
                    if j:
                        pe.wait_ge(route_act, 3 * k + 2)
                    for e in range(E // 2):
                        last = mm(psum[:, e // 2, (e % 2) * T:(e % 2 + 1) * T],
                                  spread(ident[0:E, e + j * E // 2], 1, P), route[0:E, 1024:1024 + T], True, True)
                    last.then_inc(route_pe, 1)

            fns = {"setup": setup, "turn": turn, "ffn": ffn, "project": project, "outproj": outproj,
                   "stick": stick, "soft": soft_attention, "gates": gates, "mlstm": mlstm, "norm": norm,
                   "residual": residual, "compress": compress, "cmp": cmp_attention, "latent": latent,
                   "router": router}
            pe.wait_ge(const_in, 32)
            for s, (name, args, _) in enumerate(STAGES):
                if name in fns:
                    fns[name](s, INSTANCE[s], *args)
                boundary(pe, s + 1)

        @block.scalar
        def _(act):
            steps = [0]

            def link(ins):
                steps[0] += 1
                ins.then_inc(act_step, 1)
                act.wait_ge(act_step, steps[0])

            def high_part(n, shape, i=None):
                act.wait_ge(loaded[n % RING], slot_count(n) if i is None
                            else i * (16 * LOOP // RING) + slot_count(n))
                if n >= PARTS:
                    v = n - PARTS + 1
                    act.wait_ge(piece_used, v if i is None else i * LOOP + v)
                w = shape[0] * shape[1]
                act.activation(wh[n % PARTS][:, 0:w], ring[n % RING][:, 0:w], ACT.Copy).then_inc(high, 1)

            def root_mean(ss, n):
                return act.activation(ss, ss, ACT.Sqrt, scale=1.0 / n, bias=const[:, C_EPS:C_EPS + 1])

            def setup(s, k):
                for j, shape in enumerate(early(s + 1)):
                    high_part(PIECE0[s] + j, shape)
                act.wait_ge(setup_dve, 1)
                act.activation(small[:, S_R:S_R + 8], small[:, S_R:S_R + 8], ACT.Silu).then_inc(setup_act, 1)
                act.wait_ge(rows_ready, 1)
                for i in range(3):
                    act.dma_start(rowbuf[i], spread(wide[0:8, 0, i, :], 1, P)).then_inc(rows_out, 16)
                act.wait_ge(setup_dve, 2)
                act.activation(wide_at(3840, 2048), wide_at(3840, 2048), ACT.Exp).then_inc(setup_act, 1)
                act.wait_ge(rows_out, 48)

            def norm(s, k, m):
                for t in range(TT):
                    if JOINED[s]:
                        act.wait_ge(x_added, 2 * ran(s, "residual") - 2 + t + 1)
                    link(act.activation(nrm[:, t, :], x[:, t, :], ACT.Square, accum_out=stat[:, t:t + 1]))
                    root_mean(stat[:, t:t + 1], D).then_inc(squared, 1)
                for j, shape in enumerate(early(s + 2)):
                    high_part(PIECE0[s] + j, shape)

            def turn(s, k):
                for q in range(4):
                    f = 4 * (q % 2)
                    act.wait_ge(turned, 4 * k + q + 1)
                    act.activation(xh[:, f:f + 4, (q // 2) * P:(q // 2 + 1) * P],
                                   psum[:, q, :].rearrange("p (a b) -> p a b", a=4), ACT.Copy).then_inc(turn_high, 1)

            def ffn(s, k, chunks, moe):
                n0 = PIECE0[s]
                c0, h0 = ffn_bases(k)
                n = 4 if moe else 3

                def high_of(which, c, i=None):
                    high_part(chunk_piece(n0, which, c, chunks), DN if which == "d" else GU, i)

                def silu_of_gate(c, i=None):
                    v = chunk_piece(n0, "g", c, chunks) + 1
                    act.wait_ge(piece_used, v if i is None else i * LOOP + v)
                    if c >= 2:
                        v = h0 + n * (c - 1)
                        act.wait_ge(hidden, v if i is None else i * (2 * n) + v)
                    act.activation(hT[c % 2][:, :, :], psum[:, GB + c % 2, :].rearrange("p (f t) -> p f t", f=2),
                                   ACT.Silu).then_inc(gated, 1)

                def step(c, i=None):
                    if c + 1 < chunks:
                        if not (moe and c == 0):
                            high_of("g", c + 1, i)
                        high_of("u", c + 1, i)
                    silu_of_gate(c, i)
                    high_of("d", c, i)

                for c in range(4 if moe else 3):
                    step(c)
                    if moe and c == 0:
                        copy_routing(k - 4)
                first = 4 if moe else 3
                pairs = (chunks - 1 - first) // 2
                with act.Fori(0, pairs) as i:
                    step(first, i)
                    step(first + 1, i)
                for c in range(first + 2 * pairs, chunks):
                    step(c)

            def project(s, k, name):
                widths = WIDTHS[name]
                act.wait_ge(ada_out, 16 * {"attn": 3, "mlstm": 9}.get(name, 12))
                for j, pieces in enumerate(PROJ[name]):
                    if j + 2 < len(widths):
                        high_part(PIECE0[s] + j + 2, (KT, widths[j + 2]))
                    act.wait_ge(piece_used, PIECE0[s] + j + 1)
                    b, at = j % 4, 0
                    for kind, c, m, dst, scale in pieces:
                        if kind == "N":
                            src = psum[:, b, at:at + TT * m].rearrange("p (t w) -> p t w", t=TT)
                            at += TT * m
                        elif kind == "V":
                            src = psum[:, b, 0:512].rearrange("p (t h w) -> p t h w", t=TT, h=2)
                        elif kind == "TT":
                            src = psum[:, b, 0:512]
                        elif kind == "T":
                            src = psum[0:m, b, at:at + T]
                            at += T
                        else:
                            dst = dst.rearrange("p (i o t) -> p i o t", i=2, o=2)
                            src = psum[64:P, b, :].rearrange("p (i t) -> p i t", i=2)
                            act.activation(dst[:, :, 1, :], src, ACT.Copy, scale=scale)
                            dst, src = dst[:, :, 0, :], psum[0:64, b, :].rearrange("p (i t) -> p i t", i=2)
                        last = act.activation(dst, src, ACT.Copy, scale=scale)
                    last.then_inc(proj_read, 1)

            def outproj(s, k):
                for j in range(len(early(s)), 4):
                    high_part(PIECE0[s] + j, GU)

            def residual(s, k, kind, coef):
                if kind == "norm":
                    for t in range(TT):
                        link(act.activation(nrm[:, t, :], psum[:, 2 * t:2 * t + 2, :].rearrange("p b w -> p (b w)"),
                                            ACT.Square, accum_out=stat[:, t:t + 1]))
                        root_mean(stat[:, t:t + 1], D).then_inc(squared, 1)
                else:
                    act.wait_ge(spread_pe, SPREAD0[s] + 1)
                    act.activation(gain[GAIN0[s] % GAINBUFS][:, :], psum[:, 4:6, :].rearrange("p b w -> p (b w)"),
                                   ACT.Copy).then_inc(gate_copied, 1)

            def stick(s, k):
                for h in range(H):
                    act.wait_ge(stick_dve, h + 1)
                    link(act.activation(wide[:, 1, h, :], wide[:, 0, h, :], ACT.Abs))
                    link(act.activation(wide[:, 1, h, :], wide[:, 1, h, :], ACT.Exp, scale=-1.0))
                for h in range(H):
                    act.activation(wide[:, 1, h, :], wide[:, 1, h, :], ACT.Ln, bias=ones).then_inc(stick_act, 1)
                for h in range(H):
                    act.wait_ge(stick_dve, 4 * H + h + 1)
                    act.activation(wide[:, 0, h, :], wide[:, 0, h, :], ACT.Exp).then_inc(stick_act, 1)
                act.wait_ge(stick_pe, 2 * H + 1)
                for t in range(TT):
                    act.activation(nrm[:, t, 0:512], psum[:, 4 + t, :], ACT.Copy)

            def soft_attention(s, k, name):
                a = SOFT[name]
                for h in range(a["heads"]):
                    act.wait_ge(biased, a["step0"] + a["steps"] * (h + 1))
                    for t, (lo, hi) in enumerate(((0, P), (P, W3))):
                        i = 2 * h + t
                        act.activation(wide[:, 0, h, lo:hi], wide[:, 0, h, lo:hi], ACT.Exp,
                                       bias=small[:, S_NMX + i:S_NMX + i + 1],
                                       accum_out=small[:, S_SUM + i:S_SUM + i + 1]).then_inc(expd, 1)
                    if h == 3:
                        for j, shape in enumerate(early(s + 2)):
                            high_part(PIECE0[s] + j, shape)
                if a["pad"] is not None:
                    act.wait_ge(pad_dve, PADDED.index(name) + 1)
                    act.activation(small[:, S_R:S_R + 16], small[:, S_R:S_R + 16], ACT.Exp).then_inc(pad_act, 1)

            def gates(s, k):
                act.wait_ge(gates_dve, 2)
                link(act.activation(aux[0:8, A_L:A_L + T], aux[0:8, A_F:A_F + T], ACT.Abs))
                link(act.activation(aux[0:8, A_L:A_L + T], aux[0:8, A_L:A_L + T], ACT.Exp, scale=-1.0))
                act.activation(aux[0:8, A_L:A_L + T], aux[0:8, A_L:A_L + T], ACT.Ln, bias=ones[0:8, :])\
                    .then_inc(gates_act, 1)
                act.wait_ge(gates_dve, 8)
                act.activation(aux[0:8, A_F:A_F + T], aux[0:8, A_F:A_F + T], ACT.Exp, scale=-1.0)\
                    .then_inc(gates_act, 1)
                for j in range(4):
                    act.wait_ge(gates_dve, 8 + 48 + 4 * (j + 1))
                    act.activation(wide_flat[:, 1024 * j:1024 * (j + 1)], wide_flat[:, 1024 * j:1024 * (j + 1)],
                                   ACT.Silu)
                act.activation(o_flat, o_flat, ACT.Sigmoid)

            def mlstm(s, k):
                def outputs(h):
                    act.wait_ge(ml_pe, 3 * h + 5 if h < H - 1 else 3 * H)
                    act.activation(raw[:, :, h, :], psum[:, 4 + h % 2, 0:2 * VW].rearrange("p (t w) -> p t w", t=TT),
                                   ACT.Copy).then_inc(ml_act, 1)

                for h in range(H):
                    act.wait_ge(ml_dve, 4 * h + 2)
                    act.activation(mE[h % 2], mE[h % 2], ACT.Exp, scale=-1.0).then_inc(ml_act, 1)
                    if h >= 1:
                        outputs(h - 1)
                    if h == 3:
                        for j, shape in enumerate(early(s + 2)):
                            high_part(PIECE0[s] + j, shape)
                outputs(H - 1)
                act.wait_ge(ml_dve, 4 * H + 1)
                root_mean(small[:, S_DEN:S_DEN + 16], P).then_inc(ml_act, 1)

            def compress(s, k):
                act.wait_ge(piece_used, PIECE0[s] + 4)
                act.activation(big[0:30, N_U:N_U + 512].rearrange("p (a b) -> p a b", a=2), psum[0:30, 1:3, 0:256],
                               ACT.Gelu_apprx_tanh).then_inc(comp_act, 1)

            def cmp_attention(s, k):
                act.activation(gview(S_G), gview(S_G), ACT.Sigmoid).then_inc(cmp_act, 1)
                act.wait_ge(cmp_dve, 1)
                act.activation(cS, cS, ACT.Exp).then_inc(cmp_act, 1)
                act.wait_ge(cmp_pe, 2)
                act.activation(cPT[0:NCMP, :], psum[0:NCMP, 1:5, :].rearrange("p b w -> p (b w)"), ACT.Copy)\
                    .then_inc(cmp_act, 1)

            def latent(s, k):
                for t in range(TT):
                    act.activation(nrm[:, t, 0:256], big_n(O_CQ, 256)[:, t, :], ACT.Square,
                                   accum_out=stat[:, t:t + 1])
                    last = act.activation(nrm[:, t, 256:384], big_n(O_CKV, P)[:, t, :], ACT.Square,
                                          accum_out=stat[:, 2 + t:3 + t])
                link(last)
                root_mean(stat[:, 0:2], 256)
                root_mean(stat[:, 2:4], P).then_inc(lat_act, 1)
                n = PIECE0[s]
                act.wait_ge(piece_used, n + 1)
                for t in range(TT):
                    last = act.activation(qm[:, t, :, :], psum[:, 2 + 2 * t:4 + 2 * t, :]
                                          .rearrange("p b w -> p (b w)")[:, 0:768].rearrange("p (h w) -> p h w", h=MH),
                                          ACT.Copy)
                last.then_inc(lat_act, 1)
                act.wait_ge(piece_used, n + 2)
                for t in range(TT):
                    b = (6, 0)[t]
                    last = act.activation(big_n(O_KVM, 1024)[:, t, :],
                                          psum[:, b:b + 2, :].rearrange("p b w -> p (b w)"), ACT.Copy)
                last.then_inc(lat_act, 1)
                act.wait_ge(lat_pe, 2)
                act.activation(big[:, O_QNT:O_QNT + 1024], psum[:, 2:4, :].rearrange("p b w -> p (b w)"), ACT.Copy)
                act.activation(big[:, O_KNT:O_KNT + 1024], psum[:, 4:6, :].rearrange("p b w -> p (b w)"), ACT.Copy)

            def router(s, k):
                for j, shape in enumerate(early(s + 1)):
                    high_part(PIECE0[s] + j, shape)
                act.wait_ge(route_pe, 4 * k + 1)
                act.activation(route[:, 0:2 * E], psum[:, 0, 0:2 * E], ACT.Sigmoid).then_inc(route_act, 1)

            def copy_routing(k):
                for j in range(2):
                    act.wait_ge(route_pe, 4 * k + 3 + j)
                    act.activation(big[:, 2048 * j:2048 * j + 1024], psum[:, 0:2, :].rearrange("p b w -> p (b w)"),
                                   ACT.Copy).then_inc(route_act, 1)

            def final(s, k):
                norm(s, k, None)

            ones = const[:, C_ONES:C_ONES + 1]
            fns = {"setup": setup, "norm": norm, "turn": turn, "ffn": ffn, "project": project,
                   "outproj": outproj, "residual": residual, "stick": stick, "soft": soft_attention, "gates": gates,
                   "mlstm": mlstm, "compress": compress, "cmp": cmp_attention, "latent": latent,
                   "router": router, "final": final}
            act.wait_ge(const_in, 32)
            for s, (name, args, _) in enumerate(STAGES):
                if name in fns:
                    fns[name](s, INSTANCE[s], *args)
                if name in ("ffn", "outproj"):
                    act.activation(stat[:, 7:8], const[:, C_EPS:C_EPS + 1], ACT.Sqrt)
                boundary(act, s + 1)
            act.dma_start(out.rearrange("(t p) d -> p t d", p=P), nrm[:, :, :]).then_inc(out_done, 16)
            act.wait_ge(out_done, 16)

        @block.vector
        def _(dve):
            steps = [0]

            def link(ins):
                steps[0] += 1
                ins.then_inc(dve_step, 1)
                dve.wait_ge(dve_step, steps[0])

            def mark(ins, signal, value):
                ins.then_inc(signal, 1)
                dve.wait_ge(signal, value)

            def tt(out_, a, b, op):
                return dve.tensor_tensor(out_, a, b, op)

            def setup(s, k):
                for j, shape in enumerate(early(s + 1)):
                    low_part(s, PIECE0[s] + j, shape)
                dve.wait_ge(setup_pe, 1)
                c = small[:, S_R:S_R + 8]
                dve.tensor_copy(c, psum[:, 0, 0:8]).then_inc(setup_dve, 1)
                link(dve.tensor_copy(rw_high[:, :], small[:, S_RW:S_RW + P]))
                tt(rw_low[:, :], small[:, S_RW:S_RW + P], rw_high[:, :].bitcast(F32), ALU.subtract)
                dil, rel, swa = (big[0:8, (2 + i) * W3:(3 + i) * W3] for i in range(3))
                tt(wide[0:8, 0, 0, :], psum[0:8, 1, 0:W3], dil, ALU.add)
                tt(wide[0:8, 0, 1, :], psum[0:8, 2, 0:W3], rel, ALU.add)
                tt(wide[0:8, 0, 2, :], psum[0:8, 2, 0:W3], swa, ALU.add).then_inc(rows_ready, 1)
                dve.wait_ge(setup_act, 1)
                dve.tensor_copy(ccol[:, :], c)
                link(dve.tensor_copy(pad_b[0], psum[0:8, 3, :]))
                link(tt(pad_b[1], psum[0:8, 3, :], big[0:8, R_PADMASK:R_PADMASK + 512], ALU.add))
                sink = aux[0:8, 144:145]
                dve.memset(pad_m[0][:, 0:1], NEG)
                link(dve.tensor_copy(pad_m[1][:, 0:1], sink))
                for b, m, first in zip(pad_b, pad_m, (NEG, sink)):
                    link(dve.tensor_tensor_scan(m[:, 1:513], b, b, first, ALU.max, ALU.max))
                for i in range(2):
                    tt(pad_a[i], pad_m[i][:, 0:512], pad_m[i][:, 1:513], ALU.subtract)
                    ins = tt(pad_e[i], pad_b[i], pad_m[i][:, 1:513], ALU.subtract)
                ins.then_inc(setup_dve, 1)
                dve.wait_ge(setup_act, 2)
                for i in range(2):
                    ins = dve.tensor_tensor_scan(pad_b[i], pad_a[i], pad_e[i], float(i), ALU.mult, ALU.add)
                ins.then_inc(setup_dve, 1)
                dve.wait_ge(setup_pe, 2)
                mark(dve.tensor_copy(small[:, S_PAD:S_PAD + 64], psum[:, 4, 0:64]), setup_dve, 4)
                dve.wait_ge(setup_pe, 3)
                link(dve.tensor_copy(small[:, S_PAD:S_PAD + 64], psum[:, 5, 0:64]))
                for i in range(2):
                    m = small[:, S_PAD + 32 * i:S_PAD + 32 * i + 16]
                    dve.tensor_scalar(m, m, -1.0, None, ALU.mult)

            def norm(s, k, m):
                g = GAIN0[s]
                wait_gain(dve, g)
                scale, shift = (psum[:, b:b + 2, :].rearrange("p b w -> p (b w)") for b in (4, 6))
                for t in range(TT):
                    dve.wait_ge(squared, SQ0[s] + t + 1)
                    link(dve.reciprocal(stat[:, t:t + 1], stat[:, t:t + 1]))
                    ins = dve.scalar_tensor_tensor(out=nrm[:, t, :], in0=x[:, t, :], scalar=stat[:, t:t + 1],
                                                   in1=gain[g % GAINBUFS][:, :], op0=ALU.mult, op1=ALU.mult)
                    done = 2 * (ran(s, "norm", "final")) + t + 1
                    if m is None:
                        mark(ins, normed, done)
                    else:
                        link(ins)
                        dve.wait_ge(spread_pe, SPREAD0[s] + 1)
                        link(dve.scalar_tensor_tensor(out=nrm[:, t, :], in0=scale, scalar=1.0,
                                                      in1=nrm[:, t, :], op0=ALU.add, op1=ALU.mult))
                        mark(tt(nrm[:, t, :], nrm[:, t, :], shift, ALU.add), normed, done)
                for _ in range(1 if m is None else 3):
                    dve.nop().then_inc(gain_used, 1)

            def turn(s, k):
                if early(s + 1) and JOINED[s]:
                    low_part(s, PIECE0[s], early(s + 1)[0])
                for q in range(4):
                    f = 4 * (q % 2)
                    place = (slice(0, P), slice(f, f + 4), slice((q // 2) * P, (q // 2 + 1) * P))
                    dve.wait_ge(turn_high, 4 * k + q + 1)
                    tt(xl[place], psum[:, q, :].rearrange("p (a b) -> p a b", a=4), xh[place].bitcast(F32),
                       ALU.subtract)

            def low_part(s, n, shape, i=None):
                v = SPLIT0[s] + n - PIECE0[s] + 1
                dve.wait_ge(high, v if i is None else i * LOOP + v)
                w = shape[0] * shape[1]
                tt(wl[n % PARTS][:, 0:w], ring[n % RING][:, 0:w], wh[n % PARTS][:, 0:w].bitcast(F32), ALU.subtract)\
                    .then_inc(freed, 1)

            def outproj(s, k):
                for j in range(len(early(s)), 4):
                    low_part(s, PIECE0[s] + j, GU)

            def project(s, k, name):
                widths = WIDTHS[name]
                for j in range(early_lows(s), len(widths)):
                    low_part(s, PIECE0[s] + j, (KT, widths[j]))

            def ffn(s, k, chunks, moe):
                n0 = PIECE0[s]
                c0, h0 = ffn_bases(k)
                n = 4 if moe else 3
                if early_lows(s) == 1:
                    low_part(s, n0 + 1, GU)

                def hidden_features(c, i=None, e=None):
                    def at(v, per_pair):
                        return v if i is None else i * per_pair + v

                    h, v = hT[c % 2][:, :, :], h0 + n * c
                    up = psum[:, UB + c % 2, :].rearrange("p (f t) -> p f t", f=2)
                    dve.wait_ge(gated, at(c0 + c + 1, 2))
                    dve.wait_ge(piece_used, at(chunk_piece(n0, "u", c, chunks) + 1, LOOP))
                    tt(h, h, up, ALU.mult).then_inc(hidden, 1)
                    if moe:
                        dve.wait_ge(hidden, at(v + 1, 2 * n))
                        tt(h, h, spread(routing[:, e, :], 1, 2), ALU.mult).then_inc(hidden, 1)
                    dve.wait_ge(hidden, at(v + n - 2, 2 * n))
                    if c >= 2:
                        dve.wait_ge(piece_used, at(chunk_piece(n0, "d", c - 2, chunks) + 1, LOOP))
                    dve.tensor_copy(hh[c % 2][:, :, :], h).then_inc(hidden, 1)
                    dve.wait_ge(hidden, at(v + n - 1, 2 * n))
                    tt(hl[c % 2][:, :, :], h, hh[c % 2][:, :, :].bitcast(F32), ALU.subtract).then_inc(hidden, 1)

                def low_of(which, c, i=None):
                    low_part(s, chunk_piece(n0, which, c, chunks), DN if which == "d" else GU, i)

                def step(c, i=None, e=None):
                    if c + 1 < chunks:
                        if not (moe and c == 0):
                            low_of("g", c + 1, i)
                        low_of("u", c + 1, i)
                    if moe and i is None and c == 0:
                        low_of("d", c)
                        copy_routing(k - 4)
                        hidden_features(c, i, e)
                    else:
                        hidden_features(c, i, e)
                        low_of("d", c, i)

                first = 4 if moe else 3
                for c in range(first):
                    step(c, None, c // EC)
                pairs = (chunks - 1 - first) // 2
                with dve.Fori(0, pairs) as i:
                    step(first, i, i + first // EC)
                    step(first + 1, i, i + first // EC)
                for c in range(first + 2 * pairs, chunks):
                    step(c, None, c // EC)

            def residual(s, k, kind, coef):
                dve.wait_ge(piece_used, PIECE0[s])
                g = GAIN0[s]
                factor = gain[g % GAINBUFS][:, :]
                if kind == "norm":
                    wait_gain(dve, g)
                else:
                    dve.wait_ge(gate_copied, k_gate(s) + 1)
                for t in range(TT):
                    y = psum[:, 2 * t:2 * t + 2, :].rearrange("p b w -> p (b w)")
                    if kind == "norm":
                        dve.wait_ge(squared, SQ0[s] + t + 1)
                        link(dve.reciprocal(stat[:, t:t + 1], stat[:, t:t + 1]))
                        ins = dve.scalar_tensor_tensor(out=nrm[:, t, :], in0=y, scalar=stat[:, t:t + 1],
                                                       in1=factor, op0=ALU.mult, op1=ALU.mult)
                    else:
                        ins = tt(nrm[:, t, :], y, factor, ALU.mult)
                    if t == TT - 1:
                        mark(ins, gain_used, g + 1)
                    else:
                        link(ins)
                    if kind == "norm":
                        ins = dve.scalar_tensor_tensor(out=x[:, t, :], in0=nrm[:, t, :], scalar=coef,
                                                       in1=x[:, t, :], op0=ALU.mult, op1=ALU.add)
                    else:
                        ins = tt(x[:, t, :], x[:, t, :], nrm[:, t, :], ALU.add)
                    ins.then_inc(x_added, 1)

            def stick(s, k):
                for h in range(H):
                    dve.wait_ge(stick_pe, h + 1)
                    dve.tensor_copy(wide[:, 0, h, :], psum[:, h % 2, 0:W3]).then_inc(stick_dve, 1)
                for h in range(H):
                    z, sp_h = wide[:, 0, h, :], wide[:, 1, h, :]
                    at = H + 3 * h
                    dve.wait_ge(stick_act, h + 1)
                    mark(dve.scalar_tensor_tensor(out=sp_h, in0=z, scalar=0.0, in1=sp_h, op0=ALU.max, op1=ALU.add),
                         stick_dve, at + 1)
                    mark(tt(z, z, sp_h, ALU.subtract), stick_dve, at + 2)
                    mark(tt(sp_h, sp_h, const[:, C_MSTRICT:C_MSTRICT + W3], ALU.mult), stick_dve, at + 3)
                for h in range(H):
                    dve.wait_ge(stick_pe, H + h + 1)
                    tt(wide[:, 0, h, :], wide[:, 0, h, :], psum[:, 2 + h % 2, 0:W3], ALU.subtract)\
                        .then_inc(stick_dve, 1)
                for h in range(H):
                    dve.wait_ge(stick_act, H + h + 1)
                    tt(wide[:, 0, h, :], wide[:, 0, h, :], const[:, C_MSTRICT:C_MSTRICT + W3], ALU.mult)\
                        .then_inc(stick_dve, 1)

            def biased_scores(name, h):
                a = SOFT[name]
                if a["bias"] and h == 0:
                    dve.wait_ge(bias_in, {"dilated": 32, "sliding": 96}.get(name, 64))
                S, at = wide[:, 0, h, :], a["step0"] + a["steps"] * h
                add = biasT[:, h, :] if a["bias"] else const[:, C_CAUSAL:C_CAUSAL + W3]
                dve.wait_ge(score, a["head0"] + h + 1)
                mark(dve.scalar_tensor_tensor(out=S, in0=psum[:, h % 2, 0:W3], scalar=a["scale"], in1=add,
                                              op0=ALU.mult, op1=ALU.add), biased, at + 1)
                for t, (lo, hi) in enumerate(((0, P), (P, W3))):
                    i = S_NMX + 2 * h + t
                    mark(dve.tensor_reduce(small[:, i:i + 1], S[:, lo:hi], AX.X, ALU.max, negate=True),
                         biased, at + 2 + t)
                if a["pad"] is not None:
                    for t in range(TT):
                        i, m = S_NMX + 2 * h + t, a["pad"] + 8 * t + h
                        mark(tt(small[:, i:i + 1], small[:, i:i + 1], small[:, m:m + 1], ALU.min), biased, at + 4 + t)

            def soft_attention(s, k, name):
                a = SOFT[name]
                h0, heads, dv = a["head0"], a["heads"], a["dv"]
                def probs(h):
                    dve.wait_ge(p_turned, h0 + h + 1)
                    if h >= 2 or JOINED[s]:
                        dve.wait_ge(headout, h0 + h - 1)
                    dve.tensor_copy(PT[h % 2][:, :], psum[:, 2 + h % 2, 0:W3]).then_inc(p_read, 1)

                if not JOINED[s]:
                    biased_scores(name, 0)
                    biased_scores(name, 1)
                for h in range(heads):
                    if h + 2 < heads:
                        biased_scores(name, h + 2)
                    probs(h)
                for j, shape in enumerate(early(s + 2)):
                    low_part(s, PIECE0[s] + j, shape)
                dve.wait_ge(expd, 2 * (h0 + heads))
                cols_ = 2 * heads
                sums = small[:, S_SUM:S_SUM + cols_].rearrange("p (h t) -> p h t", t=TT)
                inv = small[:, S_INV:S_INV + cols_].rearrange("p (h t) -> p h t", t=TT)
                nmx = small[:, S_NMX:S_NMX + cols_].rearrange("p (h t) -> p h t", t=TT)
                tmp = small[:, S_R:S_R + 16].rearrange("p (h t) -> p h t", t=TT)
                if a["pad"] is not None:
                    m, total = (small[:, c:c + 16].rearrange("p (t h) -> p h t", t=TT) for c in (a["pad"], a["pad"] + 16))
                    n_pad = PADDED.index(name) + 1
                    tt(tmp, nmx, m, ALU.subtract).then_inc(pad_dve, 1)
                    dve.wait_ge(pad_act, n_pad)
                    link(tt(tmp, tmp, total, ALU.mult))
                    link(tt(sums, sums, tmp, ALU.add))
                link(dve.reciprocal(inv, sums))
                if a["gate"] is not None:
                    link(tt(inv, inv, gate_of(a["gate"]), ALU.mult))
                if JOINED[s + 1]:
                    biased_scores(STAGES[s + 1][1][0], 0)
                    biased_scores(STAGES[s + 1][1][0], 1)
                dve.wait_ge(headout, h0 + heads)
                for t in range(TT):
                    y = psum[:, 4 + t, :].rearrange("p (h w) -> p h w", h=heads)
                    o = nrm[:, t, a["dst"]:a["dst"] + 512].rearrange("p (h w) -> p h w", h=heads)
                    f = spread(inv[:, :, t], 2, dv)
                    if a["gate"] is None:
                        tt(o, y, f, ALU.mult).then_inc(scaled, 1)
                    else:
                        part = wide_flat[:, 3072 + 512 * t:3584 + 512 * t].rearrange("p (h w) -> p h w", h=heads)
                        link(tt(part, y, f, ALU.mult))
                        if JOINED[s]:
                            dve.wait_ge(scaled, 2 * ran(s, "soft"))
                        tt(o, o, part, ALU.add).then_inc(scaled, 1)

            def gate_of(c):
                return gview(S_G).rearrange("p t (h c) -> p h t c", c=3)[:, :, :, c]

            def gates(s, k):
                I_, F_, L_, B_, G_ = (aux[0:8, at:at + T] for at in (A_I, A_F, A_L, A_B, A_G))
                dve.memset(vM[:, :, :, P:VW], 1.0)
                dve.wait_ge(gates_pe, 1)
                mark(dve.tensor_copy(small[:, S_CONVW:S_CONVW + 64], psum[:, 0, 0:64]), gates_dve, 1)
                dve.tensor_copy(I_, psum[0:8, 2, 0:T])
                mark(dve.tensor_scalar(F_, psum[0:8, 3, 0:T], aux[0:8, 1:2], None, ALU.add), gates_dve, 2)
                dve.wait_ge(gates_act, 1)
                mark(dve.tensor_scalar(F_, F_, 0.0, None, ALU.min), gates_dve, 3)
                mark(tt(F_, F_, L_, ALU.subtract), gates_dve, 4)
                mark(dve.tensor_tensor_scan(B_, const[0:8, C_ONES:C_ONES + 1].to_broadcast([8, T]), F_, 0.0,
                                            ALU.mult, ALU.add), gates_dve, 5)
                mark(dve.scalar_tensor_tensor(out=G_, in0=I_, scalar=aux[0:8, 0:1], in1=B_, op0=ALU.add,
                                              op1=ALU.subtract), gates_dve, 6)
                mark(dve.tensor_tensor_scan(L_, G_, G_, 0.0, ALU.max, ALU.max), gates_dve, 7)
                mark(tt(F_, B_, L_, ALU.add), gates_dve, 8)
                for tap in range(4):
                    for m in range(16):
                        w = small[:, S_CONVW + 16 * (3 - tap) + m:S_CONVW + 16 * (3 - tap) + m + 1]
                        src = big_t(M_PRE, m)
                        if tap:
                            dve.wait_ge(gates_dve, 8 + 16 * (tap - 1) + m + 1)
                            dve.scalar_tensor_tensor(out=cv[:, m, tap:T], in0=src[:, 0:T - tap], scalar=w,
                                                     in1=cv[:, m, tap:T], op0=ALU.mult, op1=ALU.add)\
                                .then_inc(gates_dve, 1)
                        else:
                            dve.tensor_scalar(cv[:, m, :], src, w, None, ALU.mult).then_inc(gates_dve, 1)
                dve.wait_ge(gates_pe, 2)
                dve.tensor_copy(small[:, S_COL:S_COL + 32], psum[:, 1, 0:32])

            def mlstm(s, k):
                scale = 1.0 / math.sqrt(P)
                for h in range(H):
                    e = mE[h % 2]
                    col = [small[:, S_COL + 8 * t + h:S_COL + 8 * t + h + 1] for t in range(TT)]
                    dve.wait_ge(ml_pe, 3 * h if h else 1)
                    dve.tensor_scalar(e[:, 0:T], psum[:, h % 2, 0:T], col[0], 0.0, ALU.subtract, ALU.max)\
                        .then_inc(ml_dve, 1)
                    dve.tensor_scalar(e[:, T:W3], psum[:, h % 2, P:T], col[1], 0.0, ALU.subtract, ALU.max)\
                        .then_inc(ml_dve, 1)
                    dve.wait_ge(ml_act, 2 * h if h else 1)
                    mark(tt(e, e, const[:, C_MINCL:C_MINCL + W3], ALU.mult), ml_dve, 4 * h + 3)
                    dve.wait_ge(ml_pe, 3 * h + 1 if h else 2)
                    if h >= 2:
                        dve.wait_ge(ml_pe, 3 * (h - 2) + 5)
                    dve.scalar_tensor_tensor(out=PT[h % 2][:, :], in0=psum[:, 2 + h % 2, 0:W3], scalar=scale, in1=e,
                                             op0=ALU.mult, op1=ALU.mult).then_inc(ml_dve, 1)
                for j, shape in enumerate(early(s + 2)):
                    low_part(s, PIECE0[s] + j, shape)
                dve.wait_ge(ml_act, 2 * H)
                den = small[:, S_DEN:S_DEN + 16].rearrange("p (t h) -> p t h", t=TT)
                thr = small[:, S_THR:S_THR + 16].rearrange("p (t h) -> p t h", t=TT)
                n_num = raw[:, :, :, P]
                link(dve.scalar_tensor_tensor(out=den, in0=n_num, scalar=-1.0, in1=n_num, op0=ALU.mult, op1=ALU.max))
                link(tt(den, den, thr, ALU.max))
                link(dve.reciprocal(den, den))
                sq = wide_flat[:, 0:2048].rearrange("p (t h w) -> p t h w", t=TT, h=H)
                g = GAIN0[s]
                wait_gain(dve, g)
                for t in range(TT):
                    link(tt(hid[:, t], raw[:, t, :, 0:P], spread(den[:, t, :], 2, P), ALU.mult))
                for t in range(TT):
                    link(tt(sq[:, t], hid[:, t], hid[:, t], ALU.mult))
                dve.tensor_reduce(den[:, 0, :], sq[:, 0], AX.X, ALU.add)
                dve.tensor_reduce(den[:, 1, :], sq[:, 1], AX.X, ALU.add).then_inc(ml_dve, 1)
                dve.wait_ge(ml_act, 2 * H + 1)
                link(dve.reciprocal(den, den))
                for t in range(TT):
                    link(tt(hid[:, t], hid[:, t], spread(den[:, t, :], 2, P), ALU.mult))
                for t in range(TT):
                    ins = tt(nrm[:, t, :], nrm[:, t, :], gain[g % GAINBUFS][:, :], ALU.mult)
                    if t == TT - 1:
                        mark(ins, gain_used, g + 1)
                    else:
                        link(ins)
                tt(nrm[:, :, :], nrm[:, :, :], oM, ALU.mult)

            def compress(s, k):
                pos = big[:, N_POS:N_POS + 64]
                dve.wait_ge(comp_pe, 1)
                mark(dve.tensor_copy(pos, psum[:, 0, 0:64]), comp_dve, 1)
                for i, at in enumerate((N_KC, N_VC)):
                    for v in range(2):
                        for odd in range(2):
                            p0 = 64 * v
                            part = big[p0:p0 + 64, at + odd:at + odd + 1]
                            tokens = bass.AP(part.tensor, part.offset, [list(part.ap[0]), [2, 16], [16, NCMP]])
                            place = pos[p0:p0 + 64, 32 * i + odd:32 * i + 32:2]
                            tt(blocksF[i][64 * odd:64 * odd + 64, :, v, :], tokens, spread(place, 2, NCMP), ALU.add)\
                                .then_inc(comp_dve, 1)
                dve.wait_ge(comp_pe, 2)
                mark(dve.tensor_copy(big[:, N_GT:N_GT + 120], psum[:, 3, 0:120]), comp_dve, 10)
                dve.wait_ge(comp_pe, 3)
                dve.tensor_copy(big[:, N_KCMP:N_KCMP + NCMP], psum[:, 4, 0:NCMP])
                dve.tensor_copy(big[0:NCMP, N_VCMP:N_VCMP + P], psum[0:NCMP, 5, 0:P])

            def cmp_attention(s, k):
                dve.wait_ge(bias_in, 64)
                link(dve.memset(cS, NEG))
                dve.wait_ge(cmp_pe, 1)
                for v in range(2):
                    g = slice(4 * v, 4 * v + 4)
                    ps = psum[:, (0, 7)[v], 0:256].rearrange("p (h t n) -> p h t n", h=H, t=TT)
                    for t, n in ((0, 7), (1, NCMP)):
                        lo = P * t + 31
                        link(tt(cS[:, g, t, 0:n], ps[:, g, t, 0:n], biasT[:, g, lo:lo + 16 * (n - 1) + 1:16],
                                ALU.add))
                mx = small[:, S_NMX:S_NMX + 16].rearrange("p (h t) -> p h t", t=TT)
                sums = small[:, S_SUM:S_SUM + 16].rearrange("p (h t) -> p h t", t=TT)
                inv = small[:, S_INV:S_INV + 16].rearrange("p (h t) -> p h t", t=TT)
                link(dve.tensor_reduce(mx, cS, AX.X, ALU.max))
                link(dve.tensor_scalar(mx, mx, -1e20, None, ALU.max))
                for t in range(TT):
                    ins = tt(cS[:, :, t, :], cS[:, :, t, :], spread(mx[:, :, t], 2, 16), ALU.subtract)
                ins.then_inc(cmp_dve, 1)
                dve.wait_ge(cmp_act, 2)
                link(dve.tensor_reduce(sums, cS, AX.X, ALU.add))
                link(dve.tensor_scalar(sums, sums, 1e-30, None, ALU.max))
                link(dve.reciprocal(inv, sums))
                link(tt(inv, inv, gate_of(0), ALU.mult))
                dve.wait_ge(cmp_pe, 3)
                for t in range(TT):
                    tt(nrm[:, t, 0:512].rearrange("p (h w) -> p h w", h=H),
                       psum[:, 5 + t, :].rearrange("p (h w) -> p h w", h=H), spread(inv[:, :, t], 2, 64), ALU.mult)

            def rope(x_, t, tmp):
                heads = x_.shape[1] if len(x_.shape) == 3 else 0
                cos = const[:, C_COS + 32 * t:C_COS + 32 * t + 32]
                sin = const[:, C_SIN + 32 * t:C_SIN + 32 * t + 32]
                if heads:
                    cos, sin = spread(cos, 1, heads), spread(sin, 1, heads)
                    x1, x2 = x_[:, :, 0:32], x_[:, :, 32:64]
                else:
                    x1, x2 = x_[:, 0:32], x_[:, 32:64]
                tt(tmp[0], x1, cos, ALU.mult)
                tt(tmp[1], x2, sin, ALU.mult)
                tt(tmp[2], x1, sin, ALU.mult)
                link(tt(tmp[3], x2, cos, ALU.mult))
                tt(x1, tmp[0], tmp[1], ALU.subtract)
                return tt(x2, tmp[2], tmp[3], ALU.add)

            def latent(s, k):
                dve.wait_ge(lat_act, 1)
                link(dve.reciprocal(stat[:, 0:4], stat[:, 0:4]))
                dve.wait_ge(extra_in, EXTRA["odd"])
                for t in range(TT):
                    cq, ckv = big_n(O_CQ, 256)[:, t, :], big_n(O_CKV, P)[:, t, :]
                    dve.scalar_tensor_tensor(out=cq, in0=cq, scalar=stat[:, t:t + 1], in1=aux[:, 0:256],
                                             op0=ALU.mult, op1=ALU.mult)
                    ins = dve.scalar_tensor_tensor(out=ckv, in0=ckv, scalar=stat[:, 2 + t:3 + t], in1=aux[:, 256:384],
                                                   op0=ALU.mult, op1=ALU.mult)
                ins.then_inc(lat_dve, 1)
                dve.wait_ge(lat_pe, 1)
                dve.tensor_copy(cqT[:, 0:2, :], psum[:, 0, :].rearrange("p (a b) -> p a b", a=2))
                dve.tensor_copy(cqT[:, 2, :], psum[:, 1, 0:T]).then_inc(lat_dve, 1)
                for t in range(TT):
                    tmp = [hT[i // 2][:, i % 2, 32 * t:32 * t + 32] for i in range(4)]
                    last = rope(big_n(O_KR, 64)[:, t, :], t, tmp)
                link(last)
                dve.wait_ge(lat_act, 2)
                for t in range(TT):
                    tmp = [hT[t][:, i // 2, P * (i % 2):P * (i % 2) + P].rearrange("p (h w) -> p h w", h=MH)
                           for i in range(4)]
                    ins = rope(qm[:, t, :, P:P + 64], t, tmp)
                ins.then_inc(lat_dve, 1)
                dve.wait_ge(lat_pe, 2)
                dve.tensor_copy(aux[0:64, A_QRT:A_QRT + 1024], psum[0:64, 6:8, :].rearrange("p b w -> p (b w)"))
                dve.tensor_copy(aux[0:64, A_KRT:A_KRT + T], psum[0:64, 0, 0:T])

            def router(s, k):
                def at(a, *dims):
                    n = int(np.prod(dims))
                    names = "abc"[:len(dims)]
                    return route[:, a:a + n].rearrange(f"p ({' '.join(names)}) -> p {' '.join(names)}",
                                                       **dict(zip(names, dims)))

                aff, biased_ = at(0, 8, 4), at(64, 8, 4)
                gt, eq = at(128, 8, 4, 4), at(256, 8, 4, 4)
                sel, top, rank = at(384, 8, 4), at(448, 8, 4), at(512, 8, 4)
                group, grank = at(576, 2, 4), at(592, 2, 4)
                ggt, geq = at(608, 2, 4, 4), at(640, 2, 4, 4)
                total = at(672, 2)
                lower = const[:, C_LOWER:C_LOWER + 16].rearrange("p (a b) -> p a b", a=4)
                for j, shape in enumerate(early(s + 1)):
                    low_part(s, PIECE0[s] + j, shape)
                dve.wait_ge(route_act, 3 * k + 1)
                rb = small[:, S_RB:S_RB + E].rearrange("p (g e) -> p g e", g=4)
                for t in range(TT):
                    link(tt(biased_[:, 4 * t:4 * t + 4], aff[:, 4 * t:4 * t + 4], rb, ALU.add))

                def ranks(values, n, g_, e_, out_):
                    for j in range(4):
                        other = spread(values[:, :, j], 2, 4)
                        tt(g_[:, :, j, :], values, other, ALU.is_gt)
                        last = tt(e_[:, :, j, :], values, other, ALU.is_equal)
                    link(last)
                    link(tt(e_, e_, spread(lower, 1, n), ALU.mult))
                    link(tt(g_, g_, e_, ALU.add))
                    link(dve.tensor_reduce(out_, g_, AX.X, ALU.add))

                ranks(biased_, 8, gt, eq, rank)
                link(dve.tensor_scalar(sel, rank, 1.5, None, ALU.is_lt))
                link(tt(top, sel, biased_, ALU.mult))
                link(dve.tensor_reduce(group.rearrange("p a b -> p (a b)"), top, AX.X, ALU.add))
                ranks(group, 2, ggt, geq, grank)
                link(dve.tensor_scalar(grank, grank, 0.5, None, ALU.is_lt))
                link(tt(sel, sel, spread(grank.rearrange("p a b -> p (a b)"), 2, 4), ALU.mult))
                link(tt(aff, aff, sel, ALU.mult))
                link(dve.tensor_reduce(total, route[:, 0:32].rearrange("p (t e) -> p t e", t=TT), AX.X, ALU.add))
                link(dve.reciprocal(total, total))
                w = route[:, 0:32].rearrange("p (t e) -> p t e", t=TT)
                tt(w, w, spread(total, 2, E), ALU.mult).then_inc(route_dve, 1)

            def copy_routing(k):
                dve.wait_ge(route_pe, 4 * k + 2)
                dve.tensor_copy(route[0:E, 1024:1024 + T], psum[0:E, 1, 0:T]).then_inc(route_dve, 1)
                for j in range(2):
                    dve.wait_ge(route_pe, 4 * k + 3 + j)
                    dve.tensor_copy(big[:, 2048 * j + 1024:2048 * j + 2048],
                                    psum[:, 2:4, :].rearrange("p b w -> p (b w)")).then_inc(route_dve, 1)
                dve.wait_ge(route_act, 3 * k + 3)
                dve.wait_ge(route_dve, 4 * k + 4)

            def final(s, k):
                norm(s, k, None)

            fns = {"setup": setup, "norm": norm, "turn": turn, "ffn": ffn, "project": project,
                   "outproj": outproj, "residual": residual, "stick": stick, "soft": soft_attention, "gates": gates,
                   "mlstm": mlstm, "compress": compress, "cmp": cmp_attention,
                   "latent": latent, "router": router, "final": final}
            dve.wait_ge(const_in, 32)
            for s, (name, args, _) in enumerate(STAGES):
                if name in fns:
                    fns[name](s, INSTANCE[s], *args)
                boundary(dve, s + 1)


_INS = ['x', 'norm_g', 'ffn_w_gate', 'ffn_w_up', 'ffn_w_down', 'attn_w_in', 'attn_w_out', 'rel_bias',
        'mlstm_w_in', 'mlstm_b_gates', 'mlstm_conv_w', 'mlstm_head_g', 'mlstm_w_out', 'c_2', 'rel_table_2',
        'router_w_2', 'router_b_2', 'final_norm_2', 'norm_mix_2', 'norm_ffn_2', 'ada_w_2', 'ada_b_2',
        'moe_w_gate_2', 'moe_w_up_2', 'moe_w_down_2', 'ev_w_in_2', 'ev_w_out_2', 'nsa_pos_k_2', 'nsa_pos_v_2',
        'nsa_ck_w1_2', 'nsa_ck_w2_2', 'nsa_cv_w1_2', 'nsa_cv_w2_2', 'od_w_in_2', 'od_w_out_2', 'mla_q_norm_2',
        'mla_kv_norm_2', 'mla_w_q_up_2', 'mla_w_kv_up_2', 'swa_sinks_2']


def kernel(**inputs):
    import concourse.bacc as _bacc
    from concourse.bass_utils import run_bass_kernel_spmd as _run

    nc = _bacc.Bacc("TRN2", target_bir_lowering=False, num_devices=1)
    arrays = {name: np.ascontiguousarray(inputs[name]) for name in _INS}
    arrays["const"], arrays["rows"] = shape_constants()
    I = {name: nc.dram_tensor(f"in_{name}", a.shape, F32, kind="ExternalInput").ap() for name, a in arrays.items()}
    out = nc.dram_tensor("out_0_dram", (T, D), F32, kind="ExternalOutput").ap()
    build(nc, I, out)
    r = _run(nc, [{f"in_{name}": a for name, a in arrays.items()}], core_ids=[0])
    return r.results[0]["out_0_dram"].reshape(1, T, D)
```
